# Optimizing a Trainium2 kernel written in Bass

```python
import jax, jax.numpy as jnp
from jax import lax
import numpy as np

D_MODEL = 1024
BATCH = 1
SEQ = 512
DEPTH = 1
DEC_BATCH = 8
DEC_SEQ = 1
PAST_LEN = 4096
PAGE_SIZE = 128

W_SCONV = D_MODEL
K_SCONV = 3
W_CCONV = D_MODEL
K_CCONV = 31
D_IN_ALL = 3 * W_SCONV + 2 * W_CCONV + 2 * D_MODEL
N_EXPERTS = 64
TOP_K = 8
N_GROUPS = 8
TOPK_GROUPS = 4
D_EXPERT = D_MODEL // 4
D_SHARED = D_EXPERT
ROUTED_SCALE = 2.5
RMS_EPS = 1e-6
LN_EPS = 1e-5

kernel_name = "hybrid_gconv_conformer_moe_step"

def rmsnorm(x, g):
    xf = x.astype(jnp.float32)
    y = xf * lax.rsqrt(jnp.mean(xf * xf, axis=-1, keepdims=True) + RMS_EPS)
    return (y * g.astype(jnp.float32)).astype(x.dtype)

def layernorm(x, g, b):
    xf = x.astype(jnp.float32)
    mu = jnp.mean(xf, axis=-1, keepdims=True)
    var = jnp.mean(jnp.square(xf - mu), axis=-1, keepdims=True)
    y = (xf - mu) * lax.rsqrt(var + LN_EPS) * g.astype(jnp.float32) + b.astype(jnp.float32)
    return y.astype(x.dtype)

def causal_dwconv(u, ctx, w):
    k, ch = w.shape
    full = jnp.concatenate([ctx.astype(u.dtype), u], axis=1)
    y = lax.conv_general_dilated(full, w[:, None, :].astype(u.dtype), window_strides=(1,),
                                 padding='VALID', dimension_numbers=('NWC', 'WIO', 'NWC'),
                                 feature_group_count=ch)
    return y, full[:, full.shape[1] - (k - 1):]

def token_mixer(h, st_a, st_b, p):
    z = h @ p['w_in']
    cut = np.cumsum([W_SCONV, W_SCONV, W_SCONV, W_CCONV, W_CCONV, D_MODEL]).tolist()
    a_in, a_b, a_c, b_val, b_gate, g_a, g_b = jnp.split(z, cut, axis=-1)
    v, new_a = causal_dwconv(a_c * a_in, st_a, p['w_sconv'])
    y_a = (a_b * v) @ p['w_out_a']
    glu = b_val * jax.nn.sigmoid(b_gate)
    cv, new_b = causal_dwconv(glu, st_b, p['w_cconv'])
    cv = cv + p['b_cconv']
    y_b = jax.nn.silu(layernorm(cv, p['ln_g'], p['ln_b'])) @ p['w_out_b'] + p['b_out_b']
    m = jax.nn.sigmoid(g_a) * y_a + jax.nn.sigmoid(g_b) * y_b
    return m @ p['w_o'], new_a, new_b

def moe_tokens(h, p):
    t = h.shape[0]
    scores = jax.nn.sigmoid((h @ p['w_router']).astype(jnp.float32))
    sel = scores + p['e_bias'].astype(jnp.float32)
    gscore = jnp.sum(lax.top_k(sel.reshape(t, N_GROUPS, N_EXPERTS // N_GROUPS), 2)[0], axis=-1)
    _, gidx = lax.top_k(gscore, TOPK_GROUPS)
    gmask = jnp.sum(jax.nn.one_hot(gidx, N_GROUPS, dtype=jnp.float32), axis=1) > 0
    emask = jnp.repeat(gmask, N_EXPERTS // N_GROUPS, axis=1)
    _, eidx = lax.top_k(jnp.where(emask, sel, -jnp.inf), TOP_K)
    w = jnp.take_along_axis(scores, eidx, axis=1)
    w = w / jnp.sum(w, axis=-1, keepdims=True) * ROUTED_SCALE
    gate = jnp.sum(jax.nn.one_hot(eidx, N_EXPERTS, dtype=jnp.float32) * w[..., None], axis=1)
    hg = jnp.einsum('td,edf->tef', h, p['w1'])
    hu = jnp.einsum('td,edf->tef', h, p['w3'])
    act = jax.nn.silu(hg) * hu * gate[:, :, None].astype(h.dtype)
    routed = jnp.einsum('tef,efd->td', act, p['w2'])
    shared = (jax.nn.silu(h @ p['ws1']) * (h @ p['ws3'])) @ p['ws2']
    return routed + shared

def layer(x, c, st_a, st_b, p):
    ada = jax.nn.silu(c) @ p['w_ada'] + p['b_ada']
    sh1, sc1, gt1, sh2, sc2, gt2 = [a[:, None, :] for a in jnp.split(ada, 6, axis=-1)]
    h = rmsnorm(x, p['g_pre1']) * (1 + sc1) + sh1
    t, new_a, new_b = token_mixer(h, st_a, st_b, p)
    x = x + gt1 * rmsnorm(t, p['g_post1'])
    h = rmsnorm(x, p['g_pre2']) * (1 + sc2) + sh2
    f = lax.map(lambda hs: moe_tokens(hs, p), h)
    x = x + gt2 * rmsnorm(f, p['g_post2'])
    return x, new_a, new_b

def setup_inputs(seed: int = 0) -> dict:
    key = jax.random.key(seed)
    ks = list(jax.random.split(key, 40))
    nrm = lambda k, shape, s: jax.random.normal(k, shape, jnp.float32) * s
    L, D, E, F = DEPTH, D_MODEL, N_EXPERTS, D_EXPERT
    return {
        'x_prompt': nrm(ks[0], (BATCH, SEQ, D), 1.0),
        'x_sample': nrm(ks[1], (DEC_BATCH, DEC_SEQ, D), 1.0),
        'state_sconv': nrm(ks[2], (L, DEC_BATCH, K_SCONV - 1, W_SCONV), 1.0),
        'state_cconv': nrm(ks[3], (L, DEC_BATCH, K_CCONV - 1, W_CCONV), 0.5),
        'c_prompt': nrm(ks[4], (BATCH, D), 1.0),
        'c_sample': nrm(ks[5], (DEC_BATCH, D), 1.0),
        'w_ada': nrm(ks[6], (L, D, 6 * D), 0.5 * D ** -0.5),
        'b_ada': nrm(ks[7], (L, 6 * D), 0.02),
        'g_pre1': 1.0 + nrm(ks[8], (L, D), 0.02),
        'g_post1': 1.0 + nrm(ks[9], (L, D), 0.02),
        'g_pre2': 1.0 + nrm(ks[10], (L, D), 0.02),
        'g_post2': 1.0 + nrm(ks[11], (L, D), 0.02),
        'w_in': nrm(ks[12], (L, D, D_IN_ALL), D ** -0.5),
        'w_sconv': nrm(ks[13], (L, K_SCONV, W_SCONV), K_SCONV ** -0.5),
        'w_out_a': nrm(ks[14], (L, W_SCONV, D), W_SCONV ** -0.5),
        'w_cconv': nrm(ks[15], (L, K_CCONV, W_CCONV), K_CCONV ** -0.5),
        'b_cconv': nrm(ks[16], (L, W_CCONV), 0.02),
        'ln_g': 1.0 + nrm(ks[17], (L, W_CCONV), 0.02),
        'ln_b': nrm(ks[18], (L, W_CCONV), 0.02),
        'w_out_b': nrm(ks[19], (L, W_CCONV, D), W_CCONV ** -0.5),
        'b_out_b': nrm(ks[20], (L, D), 0.02),
        'w_o': nrm(ks[21], (L, D, D), D ** -0.5),
        'w_router': nrm(ks[22], (L, D, E), D ** -0.5),
        'e_bias': nrm(ks[23], (L, E), 0.01),
        'w1': nrm(ks[24], (L, E, D, F), D ** -0.5),
        'w3': nrm(ks[25], (L, E, D, F), D ** -0.5),
        'w2': nrm(ks[26], (L, E, F, D), F ** -0.5),
        'ws1': nrm(ks[27], (L, D, D_SHARED), D ** -0.5),
        'ws3': nrm(ks[28], (L, D, D_SHARED), D ** -0.5),
        'ws2': nrm(ks[29], (L, D_SHARED, D), D_SHARED ** -0.5),
    }

def reference(x_prompt, x_sample, state_sconv, state_cconv, c_prompt, c_sample,
              w_ada, b_ada, g_pre1, g_post1, g_pre2, g_post2,
              w_in, w_sconv, w_out_a, w_cconv, b_cconv, ln_g, ln_b, w_out_b, b_out_b, w_o,
              w_router, e_bias, w1, w3, w2, ws1, ws3, ws2):
    yp, ys = x_prompt, x_sample
    sa_p, sa_s, sb_p, sb_s = [], [], [], []
    zero_a = jnp.zeros((x_prompt.shape[0], K_SCONV - 1, W_SCONV), x_prompt.dtype)
    zero_b = jnp.zeros((x_prompt.shape[0], K_CCONV - 1, W_CCONV), x_prompt.dtype)
    for l in range(DEPTH):
        p = {'w_ada': w_ada[l], 'b_ada': b_ada[l], 'g_pre1': g_pre1[l], 'g_post1': g_post1[l],
             'g_pre2': g_pre2[l], 'g_post2': g_post2[l], 'w_in': w_in[l], 'w_sconv': w_sconv[l],
             'w_out_a': w_out_a[l], 'w_cconv': w_cconv[l], 'b_cconv': b_cconv[l], 'ln_g': ln_g[l],
             'ln_b': ln_b[l], 'w_out_b': w_out_b[l], 'b_out_b': b_out_b[l], 'w_o': w_o[l],
             'w_router': w_router[l], 'e_bias': e_bias[l], 'w1': w1[l], 'w3': w3[l], 'w2': w2[l],
             'ws1': ws1[l], 'ws3': ws3[l], 'ws2': ws2[l]}
        yp, na_p, nb_p = layer(yp, c_prompt, zero_a, zero_b, p)
        ys, na_s, nb_s = layer(ys, c_sample, state_sconv[l], state_cconv[l], p)
        sa_p.append(na_p); sa_s.append(na_s); sb_p.append(nb_p); sb_s.append(nb_s)
    new_sconv_prompt = jnp.stack(sa_p, axis=0)
    new_sconv_sample = jnp.stack(sa_s, axis=0)
    new_cconv_prompt = jnp.stack(sb_p, axis=0)
    new_cconv_sample = jnp.stack(sb_s, axis=0)
    return (yp, ys, new_sconv_prompt, new_sconv_sample, new_cconv_prompt, new_cconv_sample)


_drawn_inputs = setup_inputs


def setup_inputs(seed=0):
    import zlib

    import numpy as np

    out = dict(_drawn_inputs(seed))
    spreads = {}
    factors = {'g_post1': 3.122, 'g_post2': 8.0, 'ln_g': 5.758}
    for name, (base, spread) in spreads.items():
        noise = np.random.default_rng([zlib.crc32(name.encode()), seed]).standard_normal(out[name].shape)
        drawn = base * np.exp(spread * noise) if base else spread * noise
        out[name] = __import__('jax').numpy.asarray(drawn.astype(out[name].dtype))
    for name, factor in factors.items():
        out[name] = (out[name] * factor).astype(out[name].dtype)
    return out
```

```python
from contextlib import ExitStack

import concourse.bass as bass
from concourse import mybir

F32 = mybir.dt.float32
F16 = mybir.dt.float16
I32 = mybir.dt.int32
U32 = mybir.dt.uint32
ALU = mybir.AluOpType
ACT = mybir.ActivationFunctionType
AX = mybir.AxisListType
ds = bass.ds

P = 128
RMS_EPS = 1e-6
LN_EPS = 1e-5
ROUTED_SCALE = 2.5
NEG = -1e30


def build_program(
    nc, x_prompt, x_sample, state_sconv, state_cconv, c_prompt, c_sample,
    w_ada, b_ada, g_pre1, g_post1, g_pre2, g_post2, w_in, w_sconv, w_out_a,
    w_cconv, b_cconv, ln_g, ln_b, w_out_b, b_out_b, w_o, w_router, e_bias,
    w1, w3, w2, ws1, ws3, ws2,
    y_prompt, y_sample, new_sconv_p, new_sconv_s, new_cconv_p, new_cconv_s,
):
    D = x_prompt.shape[2]
    NP = x_prompt.shape[1]
    NS = x_sample.shape[0]
    T = NP + NS
    HT = T // 2
    C = D // P
    KS, KC = w_sconv.shape[1], w_cconv.shape[1]
    E, FE = w1.shape[1], w1.shape[3]
    TT = (T + P - 1) // P
    LAST = T - (TT - 1) * P
    TOPK, NG, TOPG = 8, 8, 4
    EG = E // NG
    NSEQ = NS + 1
    EXTRA = (T * TOPK) // (P + 1)
    JOBS = E + EXTRA + 1
    FT = FE // P
    assert T % 2 == 0 and FT == 2 and C == 8 and LAST == NS and E == 64 and NP % P == 0

    h2_rows = nc.dram_tensor("h2_rows", (T, D), F32, kind="Internal").ap()
    y_rows = nc.dram_tensor("y_rows", (T * TOPK, D), F32, kind="Internal").ap()

    ctx = ExitStack()
    with ctx:
        def sb(name, shape, dt=F32):
            return ctx.enter_context(nc.sbuf_tensor(name, shape, dt))

        def sem(name):
            return ctx.enter_context(nc.semaphore(name))

        SLOT = 6144
        RING = 4
        ring = sb("ring", [P, RING, SLOT])
        R = C * T
        act5 = sb("act5", [P, 5 * R])
        def region(n):
            return act5[:, n * R:(n + 1) * R].rearrange("p (c t) -> p c t", c=C)
        xT, hT, cv, va, mT = (region(n) for n in range(5))
        x_tok = cv.rearrange("p c t -> p (c t)")[:, 0:4 * D].rearrange("p (i d) -> p i d", i=4)
        va_flat = act5[:, 3 * R:4 * R]
        x_stok = va_flat[0:NS, 0:D]
        c_tok = va_flat[0:NSEQ, D:2 * D]
        vrow = va_flat[:, 2 * D:2 * D + P]
        wcrow = va_flat[0:124, 2 * D + P:2 * D + 3 * P].rearrange("p (a c) -> p a c", a=2)
        sarow = va_flat[:, 2 * D + 3 * P:2 * D + 4 * P]
        sbrow = act5[0:120, 4 * R:4 * R + 2 * D].rearrange("p (a d) -> p a d", a=2)
        o = 2 * R
        x1tok = act5[:, o:o + TT * D].rearrange("p (i d) -> p i d", i=TT)
        shared = act5[:, o + TT * D:o + 2 * TT * D].rearrange("p (i d) -> p i d", i=TT)
        o += 2 * TT * D
        xg = act5[:, o:o + 2 * D].rearrange("p (b d) -> p b d", b=2)
        assert o + 2 * D <= 5 * R
        hflat = act5[:, R:2 * R]
        xgT = hflat[:, 0:D].rearrange("p (c s) -> p c s", c=C)
        xgTo = hflat[:, D:2 * D].rearrange("p (c s) -> p c s", c=C)
        yb = hflat[:, 2 * D:4 * D].rearrange("p (b d) -> p b d", b=2)
        xflat = act5[:, 0:R]
        RE = TT * E
        def rt(n):
            return xflat[:, n * RE:(n + 1) * RE].rearrange("p (i e) -> p i e", i=TT)
        score, sel, selm, repl, tmpr = (rt(n) for n in range(5))
        rank, row, blk = sel, selm, repl
        o = 5 * RE
        eq, eqm = (xflat[:, o + n * TOPK * E:o + (n + 1) * TOPK * E].rearrange("p (k e) -> p k e", k=TOPK) for n in range(2))
        o += 2 * TOPK * E
        sm = xflat[:, o:o + 13 * TT * 8].rearrange("p (n k) -> p n k", n=13)
        o += 13 * TT * 8
        e64 = xflat[:, o:o + 6 * E].rearrange("p (n e) -> p n e", n=6)
        o += 6 * E
        oneA = xflat[:, o:o + 2 * P].bitcast(F16).rearrange("p (b n) -> p b n", b=4)
        o += 2 * P
        oneB = xflat[:, o:o + 2 * JOBS].bitcast(F16).rearrange("p (b n) -> p b n", b=4)
        assert o + 2 * JOBS <= R
        yk = ring[:, :, :].rearrange("p s n -> p (s n)")[:, 0:16 * D].rearrange("p (b d) -> p b d", b=16)
        accb = ring[:, :, :].rearrange("p s n -> p (s n)")[:, 16 * D:20 * D].rearrange("p (b d) -> p b d", b=4)

        ident = sb("ident", [P, P])
        avg = sb("avg", [P, P])
        upper = sb("upper", [P, P], F16)
        ones16 = sb("ones16", [P, P], F16)
        firstrow = sb("firstrow", [NSEQ, P])
        eps = sb("eps", [P, 2])
        NV = 504
        vecs = sb("vecs", [P, NV])
        scT = sb("scT", [P, C, NSEQ])
        ada = sb("ada", [P, 6, C, NSEQ])
        stB = act5[:, 4 * R + 2 * D:4 * R + 2 * D + C * NS * (KC - 1)].rearrange("p (c n) -> p c n", c=C)
        assert 2 * D + C * NS * (KC - 1) <= R
        wide_n = [KC - 1 + NP, NS * KC, KS - 1 + NP, NS * KS, NS * KC]
        conv = sb("conv", [P, sum(wide_n)])
        def cbuf(n):
            return conv[:, sum(wide_n[:n]):sum(wide_n[:n + 1])]
        glu, up = cbuf(0), cbuf(2)
        glus, us, tmps = (cbuf(n).rearrange("p (s k) -> p s k", s=NS) for n in (1, 3, 4))
        grow = conv[0:NSEQ, 0:D]
        wr = conv[:, D:D + C * E].rearrange("p (k e) -> p k e", k=C)
        sg = sb("sg", [P, T])
        scr = sb("scr", [P, 4, T])
        ain, acs, abs_, vv = (scr[:, n, :] for n in range(4))
        rs = sb("rs", [P, T])
        sflat = scr[:, :, :].rearrange("p n t -> p (n t)")
        xgo, ybo = sflat[:, 0:D], sflat[:, D:2 * D]
        esil = sg[:, 0:512].rearrange("p (b f s) -> p b f s", b=2, f=2)
        eact = rs[:, 0:512].rearrange("p (b f s) -> p b f s", b=2, f=2)
        eacto = conv[:, D:D + 256].rearrange("p (f s) -> p f s", f=2)
        esilo = conv[:, D + 256:D + 512].rearrange("p (f s) -> p f s", f=2)
        tail = sb("tail", [P, C, 48])
        tailrows = ring[0:48, 2, 5120:6144]
        s1 = sb("s1", [P, C, NSEQ])
        smp = sb("smp", [P, C, NS])
        rflat = ring[:, :, :].rearrange("p s n -> p (s n)")
        G2 = rflat[:, 20 * D:21 * D]
        G2s = rflat[0:NS, 21 * D:22 * D]
        grow2 = ring[0:NSEQ, 1, 5120:6144]
        ebias = sb("ebias", [P, E])
        iot = sb("iot", [P, P])
        tokp1 = sb("tokp1", [P, TT])
        valid = sb("valid", [P, TT])
        slotid = sb("slotid", [P, 1])
        beyond = sb("beyond", [P, JOBS], I32)
        firsty = sb("firsty", [P, E], I32)
        blocks = sb("blocks", [P, TT], I32)
        ioti = cbuf(4).bitcast(I32)
        mask16 = sb("mask16", [P, TT, E], F16)
        def s8(n):
            return sm[:, n, :].rearrange("p (i k) -> p i k", k=8)
        gates = sb("gates", [P, TT, TOPK])
        yidx = sb("yidx", [P, TT, TOPK], I32)
        idxT = sb("idxT", [P, JOBS], I32)
        rowT = sb("rowT", [P, E + 1], I32)
        cnt_i = sb("cnt_i", [1, 3, E + 2], I32)
        gidx = sb("gidx", [P, 6], I32)
        sidx = sb("sidx", [P, 6], I32)
        red = sb("red", [P, 4])

        ps = ctx.enter_context(nc.psum_tensor("ps", [P, 8, 512], F32))

        V_ADA, V_PRE1, V_POST1, V_PRE2, V_SC, V_BC, V_LG, V_LB, V_OB = 0, 48, 56, 64, 72, 96, 104, 112, 120
        V_WC, V_SA = 128, 376

        consts = sem("consts")
        crow_in, vrow_in, x_in, st_in, late_in = (sem(n) for n in ("crow_in", "vrow_in", "x_in", "st_in", "late_in"))
        out_done = sem("out_done")
        w_ada1 = [sem(f"w_ada1_{s}") for s in range(RING)]
        w_pha = [sem(f"w_pha_{s}") for s in range(RING)]
        w_m = [sem(f"w_m_{s}") for s in range(RING)]
        w_wo = [sem(f"w_wo_{s}") for s in range(RING)]
        w_sh = sem("w_sh")
        w_ex = [sem(f"w_ex_{s}") for s in range(RING)]
        items_used = sem("items_used")
        dve_step = sem("dve_step")
        pool_step = sem("pool_step")
        names = ("bgate bval ain ac sg_done ain_done acs_done abs_done glu_done ada2_done u_done v_done va_done "
                 "pa_chain pool_chain "
                 "vecs_pe vecs_act cT_pe cT_act xT_pe xT_act xs_pe xs_act xsq_act xstat_pe xrt_act stB_pe stB_act csilu_act "
                 "s1_dve xn_dve h_act h_s_dve tails_pe tailrows_act g2rows_pe growc_act grow_dve g2_pe G2_act "
                 "mean_pe cen_dve lrt_act ln_dve s_act trt_act x1_dve x1rt_act x1n_dve h2_act h2_s_dve logits_pe "
                 "score0_dve score_act score_s_act mask_dve rank_pe table_dve late_chain "
                 "g_mm g_done m_done m_chain t_cp stat_mm sqd idx_ab idx_mm hx_T hx_done "
                 "x1t_T x1t_done sh_mm sh_act sh_o sh_done "
                 "exT exT_done ex13 ex_sil ex_act ex_yd gcopy scopy pool_passed "
                 "ovT ovT_done ov13 ov_sil ov_act ov_y ov_yd ovcopy ovx ov_scat yacc fin_sq fin_rt fin_out").split()
        S = {n: sem(n) for n in names}
        hx_out = [sem(f"hx_out{b}") for b in range(2)]
        fin_dma = [sem(f"fin_dma{b}") for b in range(2)]
        xg_in = [sem(f"xg_in{b}") for b in range(2)]
        y_out = [sem(f"y_out{u}") for u in range(4)]
        yk_in = [sem(f"yk_in{b}") for b in range(16)]

        def flat(ap):
            return ap.rearrange("p c t -> p (c t)")

        half = [(0, HT), (HT, T)]

        block = ctx.enter_context(nc.Block())

        @block.sync
        def _(sp):
            def w_src(t, col, n):
                return t[0, :, col:col + n].rearrange("(k p) n -> p k n", p=P)

            for q in range(4):
                dst = ring[:, q, 0:4096].rearrange("p (k a n) -> p k a n", k=C, a=2)
                for a in range(2):
                    sp.dma_start(dst[:, :, a, :], w_src(w_ada, a * D + q * 256, 256)).then_inc(w_ada1[q], 16)
            with sp.Fori(0, C // 2) as it:
                for jj in range(2):
                    j = it * 2 + jj
                    for part in range(2):
                        slot = 2 * jj + part
                        sp.wait_ge(items_used, it * 4 + slot + 1)
                        if part == 0:
                            dst = ring[:, slot, 0:5120].rearrange("p (k a n) -> p k a n", k=C, a=5)
                            for a in range(5):
                                sp.dma_start(dst[:, :, a, :],
                                             w_in[0, :, ds(j * P + a * D, P)].rearrange("(k p) n -> p k n", p=P)
                                             ).then_inc(w_pha[slot], 16)
                        else:
                            dst = ring[:, slot, 0:4096].rearrange("p (k a n) -> p k a n", k=C, a=4)
                            for a in range(4):
                                sp.dma_start(dst[:, :, a, :],
                                             w_ada[0, :, ds(j * P + (2 + a) * D, P)].rearrange("(k p) n -> p k n", p=P)
                                             ).then_inc(w_pha[slot], 16)
            for br, (gcol, wout) in enumerate(((5, w_out_a), (6, w_out_b))):
                with sp.Fori(0, 2) as it:
                    for jj in range(4):
                        j = it * 4 + jj
                        sp.wait_ge(items_used, it * 4 + (17 + 8 * br + jj))
                        dst = ring[:, jj, 0:2048].rearrange("p (k a n) -> p k a n", k=C, a=2)
                        sp.dma_start(dst[:, :, 0, :],
                                     w_in[0, :, ds(j * P + gcol * D, P)].rearrange("(k p) n -> p k n", p=P)
                                     ).then_inc(w_m[jj], 16)
                        sp.dma_start(dst[:, :, 1, :],
                                     wout[0, :, ds(j * P, P)].rearrange("(k p) n -> p k n", p=P)
                                     ).then_inc(w_m[jj], 16)
            with sp.Fori(0, 2) as it:
                for jj in range(4):
                    j = it * 4 + jj
                    sp.wait_ge(items_used, it * 4 + (33 + jj))
                    sp.dma_start(ring[:, jj, 0:1024].rearrange("p (k n) -> p k n", k=C),
                                 w_o[0, :, ds(j * P, P)].rearrange("(k p) n -> p k n", p=P)).then_inc(w_wo[jj], 16)
            sp.wait_ge(items_used, 41)
            sp.dma_start(ring[:, 0, 0:2048].rearrange("p (k n) -> p k n", k=C), w_src(ws1, 0, FE)).then_inc(w_sh, 16)
            sp.dma_start(ring[:, 0, 2048:4096].rearrange("p (k n) -> p k n", k=C), w_src(ws3, 0, FE)).then_inc(w_sh, 16)
            sp.dma_start(ring[:, 0, 4096:6144].rearrange("p (k n) -> p k n", k=FT), w_src(ws2, 0, D)).then_inc(w_sh, 16)
            sp.wait_ge(out_done, 16 * 6)
            with sp.Fori(0, E // 4) as g:
                for u in range(4):
                    slot = (u + 1) % 4
                    e = g * 4 + u
                    sp.wait_ge(items_used, g * 4 + (42 + u))
                    for m, w in enumerate((w1, w3)):
                        sp.dma_start(ring[:, slot, 2048 * m:2048 * (m + 1)],
                                     w[0, ds(e, 1), :, :].rearrange("a (p k) n -> p (a k n)", p=P)
                                     ).then_inc(w_ex[slot], 16)
                    sp.dma_start(ring[:, slot, 4096:6144].rearrange("p (k n) -> p k n", k=FT),
                                 w2[0, ds(e, 1), :, :].rearrange("a (k p) n -> p (a k) n", p=P)
                                 ).then_inc(w_ex[slot], 16)
            for i in range(TT):
                n = P if i < TT - 1 else LAST
                sp.wait_ge(S["fin_out"], i + 1)
                dst = y_prompt[0, i * P:(i + 1) * P, :] if i < TT - 1 else y_sample.rearrange("n a d -> (n a) d")
                sp.dma_start(dst, accb[0:n, 2 + i % 2, :]).then_inc(fin_dma[i % 2], 16)
            sp.wait_ge(out_done, 16 * 6)
            sp.wait_ge(fin_dma[0], 16 * 3)
            sp.wait_ge(fin_dma[1], 16 * 2)

        @block.gpsimd
        def _(pool):
            n_step = [0]

            def link(ins):
                n_step[0] += 1
                ins.then_inc(pool_step, 1)
                pool.wait_ge(pool_step, n_step[0])

            for n in ("glu_done", "u_done", "va_done", "acs_done", "abs_done", "ain_done", "ada2_done", "v_done",
                      "m_done", "t_cp", "ex_yd", "ov_yd"):
                pool.sem_inc(S[n], 1)
            link(pool.memset(ident[:, :], 0.0))
            pool.affine_select(out=ident[:, :], in_=ident[:, :], compare_op=ALU.not_equal, fill=1.0, base=0,
                               pattern=[[-1, P]], channel_multiplier=1).then_inc(consts, 1)
            pool.memset(avg[:, :], 1.0 / D).then_inc(consts, 1)
            pool.memset(eps[:, 0:1], RMS_EPS).then_inc(consts, 1)
            pool.memset(eps[:, 1:2], LN_EPS).then_inc(consts, 1)
            pool.memset(glu[:, 0:KC - 1], 0.0).then_inc(consts, 1)
            pool.memset(up[:, 0:KS - 1], 0.0).then_inc(consts, 1)
            link(pool.memset(firstrow[:, :], 1.0))
            pool.affine_select(out=firstrow[:, :], in_=firstrow[:, :], compare_op=ALU.is_ge, fill=0.0, base=0,
                               pattern=[[0, P]], channel_multiplier=-1).then_inc(consts, 1)
            pool.memset(ones16[:, :], 1.0).then_inc(consts, 1)
            link(pool.memset(upper[:, :], 1.0))
            pool.affine_select(out=upper[:, :], in_=upper[:, :], compare_op=ALU.is_ge, fill=0.0, base=-1,
                               pattern=[[1, P]], channel_multiplier=-1).then_inc(consts, 1)
            for dst, pattern, base, cm in ((iot[:, :], [[1, P]], 0, 0), (tokp1[:, :], [[P, TT]], 1, 1),
                                           (slotid[:, :], [[0, 1]], 0, 1)):
                n = dst.shape[1]
                link(pool.iota(ioti[:, 0:n], pattern=pattern, base=base, channel_multiplier=cm))
                link(pool.tensor_copy(dst, ioti[:, 0:n]))
            link(pool.iota(blocks[:, :], pattern=[[P, TT]], base=0, channel_multiplier=0))
            pool.tensor_scalar(valid[:, :], tokp1[:, :], T + 0.5, None, ALU.is_lt).then_inc(consts, 1)
            pool.wait_ge(S["vecs_act"], 1)
            with pool.Fori(0, C // 2) as it:
                for jj in range(2):
                    j = it * 2 + jj
                    pool.wait_ge(S["acs_done"], j + 2)
                    pool.wait_ge(S["ain_done"], j + 2)
                    pool.wait_ge(S["v_done"], j + 1)
                    pool.tensor_tensor(up[:, KS - 1:], acs[:, 0:NP], ain[:, 0:NP], ALU.mult).then_inc(S["pool_chain"], 1)
                    pool.tensor_tensor(us[:, :, KS - 1], acs[:, NP:T], ain[:, NP:T], ALU.mult).then_inc(S["pool_chain"], 1)
                    pool.tensor_copy(us[:, :, 0:KS - 1],
                                     vecs[:, V_SA:V_SA + 128].rearrange("p (n k c) -> p n k c", n=NS, c=C)[:, :, :, ds(j, 1)]
                                     .rearrange("p n k c -> p n (k c)")).then_inc(S["pool_chain"], 1)
                    pool.wait_ge(S["pool_chain"], j * 4 + 3)
                    pool.tensor_copy(tail[:, ds(j, 1), 38:40].rearrange("p a n -> p (a n)"), up[:, NP:NP + 2]).then_inc(S["pool_chain"], 1)
                    pool.wait_ge(S["pool_chain"], j * 4 + 4)
                    pool.tensor_copy(tail[:, ds(j, 1), 40:48].rearrange("p a n -> p (a n)"), us[:, :, KS - 1]).then_inc(S["u_done"], 1)
                    pool.wait_ge(S["v_done"], j + 2)
                    pool.wait_ge(S["abs_done"], j + 2)
                    pool.tensor_tensor(va[:, ds(j, 1), :].rearrange("p a t -> p (a t)"), vv, abs_, ALU.mult).then_inc(S["va_done"], 1)
            pool.wait_ge(hx_out[0], 16 * 3)
            pool.wait_ge(hx_out[1], 16 * 2)
            pool.wait_ge(S["table_dve"], 1)
            ov = pool.alloc_register("ov_pool")
            pool.reg_mov(ov, 0)
            last_row, last_y = pool.alloc_register("last_row"), pool.alloc_register("last_y")
            pool.reg_mov(last_row, T - 1)
            pool.reg_mov(last_y, T * TOPK - 1)

            def wait_here():
                pool.sem_inc(S["pool_passed"], 1)

            def gather(e, u, count):
                pool.tensor_copy(gidx[:, u:u + 1], idxT[:, ds(e, 1)]).then_inc(S["gcopy"], 1)
                pool.wait_ge(S["gcopy"], count)
                wait_here()
                wide = pool.value_load(cnt_i[0:1, 0, ds(e, 1)], min_val=0, max_val=1)
                for m, n in ((1, P), (0, P // 2)):
                    with pool.If(wide > 0) if m else pool.If(wide < 1):
                        pool.indirect_dma_start(out=xg[0:n, u % 2, :], out_offset=None, in_=h2_rows,
                                                in_offset=bass.IndirectOffsetOnAxis(ap=gidx[0:n, u:u + 1], axis=0),
                                                bounds_check=last_row, oob_is_err=False).then_inc(xg_in[u % 2], 16)

            def scatter(after, u):
                pool.wait_ge(S["ex_yd"], after + 1)
                pool.tensor_copy(sidx[:, u:u + 1], rowT[:, ds(after, 1)]).then_inc(S["scopy"], 1)
                pool.wait_ge(S["scopy"], after)
                wait_here()
                wide = pool.value_load(cnt_i[0:1, 2, ds(after, 1)], min_val=0, max_val=1)
                for m, n in ((1, P), (0, P // 2)):
                    with pool.If(wide > 0) if m else pool.If(wide < 1):
                        pool.indirect_dma_start(out=y_rows,
                                                out_offset=bass.IndirectOffsetOnAxis(ap=sidx[0:n, u:u + 1], axis=0),
                                                in_=yb[0:n, u % 2, :], in_offset=None,
                                                bounds_check=last_y, oob_is_err=False).then_inc(y_out[u], 16)

            def gather_further(o, count):
                pool.tensor_copy(gidx[:, 4:5], idxT[:, ds(o + E, 1)]).then_inc(S["ovcopy"], 1)
                pool.wait_ge(S["ovcopy"], count)
                wait_here()
                pool.indirect_dma_start(out=xgo, out_offset=None, in_=h2_rows,
                                        in_offset=bass.IndirectOffsetOnAxis(ap=gidx[:, 4:5], axis=0),
                                        bounds_check=last_row, oob_is_err=False).then_inc(S["ovx"], 16)

            gather(0, 0, 1)
            gather(1, 1, 2)
            pool.wait_ge(items_used, 45)
            link(pool.memset(xgo, 0.0))
            gather_further(0, 1)
            with pool.Fori(0, E // 4) as g:
                for u in range(4):
                    e = g * 4 + u

                    def ahead():
                        pool.wait_ge(S["exT"], e + 1)
                        gather(e + 2, (u + 2) % 4, e + 3)

                    if u < 2:
                        ahead()
                    else:
                        with pool.If(g < E // 4 - 1):
                            ahead()
                    if u == 0:
                        with pool.If(g > 0):
                            scatter(e, 3)
                    else:
                        scatter(e, u - 1)
                    more = pool.value_load(cnt_i[0:1, 1, ds(e, 1)], min_val=0, max_val=4)
                    with pool.If(more > 0):
                        with pool.Fori(0, more) as b:
                            o = pool.snap(ov, min_val=0, max_val=EXTRA - 1)
                            pool.wait_ge(S["ovT"], o + 1)
                            gather_further(o + 1, o * 3 + 2)
                            pool.wait_ge(S["ov_yd"], o + 2)
                            pool.tensor_tensor(sidx[:, 4:5], firsty[:, ds(e, 1)], beyond[:, ds(o + E, 1)], ALU.add).then_inc(S["ovcopy"], 1)
                            pool.wait_ge(S["ovcopy"], o * 3 + 3)
                            pool.tensor_tensor(sidx[:, 5:6], sidx[:, 4:5], blocks[:, ds(b + 1, 1)], ALU.add).then_inc(S["ovcopy"], 1)
                            pool.wait_ge(S["ovcopy"], o * 3 + 4)
                            wait_here()
                            pool.indirect_dma_start(out=y_rows, out_offset=bass.IndirectOffsetOnAxis(ap=sidx[:, 5:6], axis=0),
                                                    in_=ybo, in_offset=None,
                                                    bounds_check=last_y, oob_is_err=False).then_inc(S["ov_scat"], 16)
                            pool.reg_add(ov, ov, 1)
            scatter(E, 3)
            for u in range(4):
                pool.wait_ge(y_out[u], 16 * (E // 4))
            pool.wait_ge(items_used, 45 + E)
            pool.wait_ge(S["late_chain"], 10 * TT)
            for i in range(TT):
                n = P if i < TT - 1 else LAST
                if i >= 2:
                    pool.wait_ge(S["yacc"], i - 1)
                for k in range(TOPK):
                    b = (i % 2) * 8 + k
                    pool.indirect_dma_start(out=yk[0:n, b, :], out_offset=None, in_=y_rows,
                                            in_offset=bass.IndirectOffsetOnAxis(ap=yidx[0:n, i, k:k + 1], axis=0),
                                            bounds_check=last_y, oob_is_err=False).then_inc(yk_in[b], 16)

        @block.scalar
        def _(act):
            def mark(ins, name):
                ins.then_inc(S[name], 1)

            act.dma_start(c_tok[0:1, :], c_prompt).then_inc(crow_in, 16)
            act.dma_start(c_tok[1:NSEQ, :], c_sample).then_inc(crow_in, 16)
            for base, n, t in ((V_ADA, 48, b_ada.rearrange("l (r c) -> (l r) c", c=P)),
                               (V_PRE1, C, g_pre1.rearrange("l (r c) -> (l r) c", c=P)),
                               (V_POST1, C, g_post1.rearrange("l (r c) -> (l r) c", c=P)),
                               (V_PRE2, C, g_pre2.rearrange("l (r c) -> (l r) c", c=P)),
                               (V_SC, C * KS, w_sconv.rearrange("l k (r c) -> (l k r) c", c=P)),
                               (V_BC, C, b_cconv.rearrange("l (r c) -> (l r) c", c=P)),
                               (V_LG, C, ln_g.rearrange("l (r c) -> (l r) c", c=P)),
                               (V_LB, C, ln_b.rearrange("l (r c) -> (l r) c", c=P)),
                               (V_OB, C, b_out_b.rearrange("l (r c) -> (l r) c", c=P))):
                act.dma_start(vrow[base:base + n, :], t).then_inc(vrow_in, 16)
            wcr = w_cconv.rearrange("l k (r c) -> (l k r) c", c=P)
            for a in range(2):
                act.dma_start(wcrow[:, a, :], wcr[a * 124:(a + 1) * 124, :]).then_inc(vrow_in, 16)
            act.dma_start(sarow, state_sconv.rearrange("l n k (r c) -> (l n k r) c", c=P)).then_inc(vrow_in, 16)
            act.dma_start(x_tok, x_prompt[0].rearrange("(i p) d -> p i d", p=P)).then_inc(x_in, 16)
            act.dma_start(x_stok, x_sample.rearrange("n a d -> (n a) d")).then_inc(x_in, 16)
            act.dma_start(sbrow, state_cconv.rearrange("l n k d -> (l n k) d").rearrange("(a r) d -> r a d", a=2)).then_inc(st_in, 16)
            act.dma_start(ebias[:, :], e_bias.to_broadcast([P, E])).then_inc(late_in, 16)
            act.dma_start(new_cconv_s[0, :, 0:KC - 2, :], state_cconv[0, :, 1:KC - 1, :]).then_inc(out_done, 16)
            act.dma_start(new_sconv_s[0, :, 0:KS - 2, :], state_sconv[0, :, 1:KS - 1, :]).then_inc(out_done, 16)

            act.wait_ge(crow_in, 32)
            mark(act.activation(c_tok, c_tok, ACT.Silu), "csilu_act")
            act.wait_ge(S["vecs_pe"], 1)
            mark(act.activation(vecs[:, 0:NV], ps[:, 6, 0:NV], ACT.Copy), "vecs_act")
            act.wait_ge(S["cT_pe"], 1)
            mark(act.activation(scT[:, :, :].rearrange("p c s -> p (c s)"), ps[:, 7, 0:C * NSEQ], ACT.Copy), "cT_act")
            for c in range(C):
                act.wait_ge(S["xT_pe"], c + 1)
                mark(act.activation(xT[:, c, 0:NP], ps[:, c % 4, 0:NP], ACT.Copy), "xT_act")
            act.wait_ge(S["xs_pe"], 1)
            mark(act.activation(xT[:, :, NP:T], ps[:, 5, 0:C * NS].rearrange("p (c s) -> p c s", c=C), ACT.Copy), "xs_act")
            act.wait_ge(S["xs_act"], 1)
            for c in range(C):
                mark(act.activation(hT[:, c, :], xT[:, c, :], ACT.Square), "xsq_act")
            W2 = NS * (KC - 1)
            for r in range(2):
                act.wait_ge(S["stB_pe"], (r) + 1)
                for q in range(2):
                    c = 4 * r + 2 * q
                    mark(act.activation(stB[:, c:c + 2, :].rearrange("p c n -> p (c n)"), ps[:, 2 * r + q, 0:2 * W2],
                                        ACT.Copy), "stB_act")
            act.wait_ge(S["xstat_pe"], 1)
            for h, (a, b) in enumerate(half):
                mark(act.activation(rs[:, a:b], ps[:, 6 + h, 0:HT], ACT.Sqrt, bias=eps[:, 0:1]), "xrt_act")
            act.wait_ge(S["s1_dve"], 1)
            for c in range(C):
                act.wait_ge(S["xn_dve"], c + 1)
                mark(act.activation(hT[:, c, 0:NP], hT[:, c, 0:NP], ACT.Identity, bias=ada[:, 0, c, 0:1],
                                    scale=s1[:, c, 0:1]), "h_act")
            with act.Fori(0, C // 2) as it:
                for jj in range(2):
                    j = it * 2 + jj
                    act.wait_ge(S["glu_done"], j + 1)
                    act.wait_ge(S["bgate"], j + 1)
                    for h, (a, b) in enumerate(half):
                        ins = act.activation(sg[:, a:b], ps[:, h, 0:HT], ACT.Sigmoid)
                    ins.then_inc(S["sg_done"], 1)
                    act.wait_ge(S["u_done"], j + 1)
                    act.wait_ge(S["ain"], j + 1)
                    for h, (a, b) in enumerate(half):
                        ins = act.activation(ain[:, a:b], ps[:, 4 + h, 0:HT], ACT.Copy)
                    ins.then_inc(S["ain_done"], 1)
                    act.wait_ge(S["ac"], j + 1)
                    for h, (a, b) in enumerate(half):
                        ins = act.activation(acs[:, a:b], ps[:, h, 0:HT], ACT.Copy)
                    ins.then_inc(S["acs_done"], 1)
                    act.wait_ge(S["va_done"], j + 1)
                    act.wait_ge(items_used, it * 4 + (5 + 2 * jj))
                    for h, (a, b) in enumerate(half):
                        ins = act.activation(abs_[:, a:b], ps[:, 2 + h, 0:HT], ACT.Copy)
                    ins.then_inc(S["abs_done"], 1)
            act.wait_ge(S["va_done"], C + 1)
            act.dma_start(wr, w_router[0].rearrange("(k p) e -> p k e", p=P)).then_inc(late_in, 16)
            act.dma_start(grow2, g_post2.to_broadcast([NSEQ, D])).then_inc(late_in, 16)
            act.wait_ge(S["tails_pe"], 1)
            mark(act.activation(tailrows[:, :], ps[0:48, 6:8, :].rearrange("p b n -> p (b n)"), ACT.Copy), "tailrows_act")
            act.wait_ge(S["tailrows_act"], 1)
            act.dma_start(new_cconv_p[0, 0], tailrows[0:KC - 1, :]).then_inc(out_done, 16)
            act.dma_start(new_cconv_s[0, :, KC - 2, :], tailrows[KC - 1:KC - 1 + NS, :]).then_inc(out_done, 16)
            act.dma_start(new_sconv_p[0, 0], tailrows[38:40, :]).then_inc(out_done, 16)
            act.dma_start(new_sconv_s[0, :, KS - 2, :], tailrows[40:48, :]).then_inc(out_done, 16)
            act.wait_ge(S["g2rows_pe"], 1)
            mark(act.activation(grow, ps[0:NSEQ, 4:6, :].rearrange("p b n -> p (b n)"), ACT.Copy), "growc_act")

            def gate_sig(it, jj, q0):
                q = it * 4 + (q0 + jj)
                act.wait_ge(S["m_done"], q + 1)
                act.wait_ge(S["g_mm"], q + 1)
                for h, (a, b) in enumerate(half):
                    ins = act.activation(sg[:, a:b], ps[:, h, 0:HT], ACT.Sigmoid)
                ins.then_inc(S["g_done"], 1)

            for jj in range(4):
                gate_sig(0, jj, 0)
            for h in range(2):
                act.wait_ge(S["cen_dve"], h + 1)
            for c in range(C):
                if c >= 4:
                    act.wait_ge(S["stat_mm"], c - 3)
                act.activation(scr[:, c % 4, :], cv[:, c, :], ACT.Square).then_inc(S["sqd"], 1)
            act.wait_ge(S["stat_mm"], 8)
            for h, (a, b) in enumerate(half):
                mark(act.activation(rs[:, a:b], ps[:, 6 + h, 0:HT], ACT.Sqrt, bias=eps[:, 1:2]), "lrt_act")
            for jj in range(4):
                gate_sig(1, jj, 0)
            for c in range(C):
                act.wait_ge(S["ln_dve"], c + 1)
                mark(act.activation(cv[:, c, :], cv[:, c, :], ACT.Silu, bias=vecs[:, V_LB + c:V_LB + c + 1],
                                    scale=vecs[:, V_LG + c:V_LG + c + 1]), "s_act")
            with act.Fori(0, 2) as it:
                for jj in range(4):
                    gate_sig(it, jj, 8)
            for j in range(C):
                q = 2 * (j % 2)
                act.wait_ge(items_used, 37 + j)
                for h, (a, b) in enumerate(half):
                    ins = act.activation(hT[:, j, a:b], ps[:, q + h, 0:HT], ACT.Copy)
                ins.then_inc(S["t_cp"], 1)
                act.wait_ge(S["stat_mm"], 8 + j - 3)
                act.wait_ge(S["t_cp"], j + 2)
                act.activation(scr[:, j % 4, :], hT[:, j, :], ACT.Square).then_inc(S["sqd"], 1)
            act.wait_ge(S["stat_mm"], 16)
            for h, (a, b) in enumerate(half):
                mark(act.activation(rs[:, a:b], ps[:, 6 + h, 0:HT], ACT.Sqrt, bias=eps[:, 0:1]), "trt_act")
            for j in range(C):
                act.wait_ge(S["x1_dve"], j + 1)
                act.wait_ge(S["stat_mm"], 16 + j - 3)
                act.activation(scr[:, j % 4, :], xT[:, j, :], ACT.Square).then_inc(S["sqd"], 1)
            act.wait_ge(S["stat_mm"], 24)
            for h, (a, b) in enumerate(half):
                mark(act.activation(rs[:, a:b], ps[:, 4 + h, 0:HT], ACT.Sqrt, bias=eps[:, 0:1]), "x1rt_act")
            for c in range(C):
                act.wait_ge(S["x1n_dve"], c + 1)
                mark(act.activation(hT[:, c, 0:NP], hT[:, c, 0:NP], ACT.Identity, bias=ada[:, 3, c, 0:1],
                                    scale=s1[:, c, 0:1]), "h2_act")
            for i in range(TT):
                n = P if i < TT - 1 else LAST
                act.wait_ge(S["x1t_T"], i + 1)
                act.activation(x1tok[0:n, i, :], ps[0:n, 0:2, :].rearrange("p b n -> p (b n)"), ACT.Copy).then_inc(S["x1t_done"], 1)
            act.wait_ge(S["logits_pe"], 1)
            act.wait_ge(S["score0_dve"], 1)
            mark(act.activation(score[:, 0:TT - 1, :], ps[:, 4, 0:(TT - 1) * E].rearrange("p (i e) -> p i e", e=E), ACT.Sigmoid), "score_act")
            mark(act.activation(score[0:LAST, TT - 1, :], ps[0:LAST, 4, (TT - 1) * E:TT * E], ACT.Sigmoid), "score_s_act")
            for i in range(TT):
                n = P if i < TT - 1 else LAST
                act.wait_ge(S["hx_T"], i + 1)
                if i >= 2:
                    act.wait_ge(hx_out[i % 2], 16 * (i // 2))
                act.activation(xg[0:n, i % 2, :], ps[0:n, 2:4, :].rearrange("p b n -> p (b n)"), ACT.Copy).then_inc(S["hx_done"], 1)
                act.wait_ge(S["hx_done"], i + 1)
                act.dma_start(h2_rows[i * P:i * P + n, :], xg[0:n, i % 2, :]).then_inc(hx_out[i % 2], 16)
            for f in range(FT):
                act.wait_ge(S["sh_mm"], f + 1)
                if f == 1:
                    act.wait_ge(S["sh_act"], 1)
                for h, (a, b) in enumerate(half):
                    ins = act.activation(sg[:, a:b], ps[:, h, 0:HT], ACT.Silu)
                ins.then_inc(S["g_done"], 1)
            for i in range(TT):
                n = P if i < TT - 1 else LAST
                if i < TT - 1:
                    act.wait_ge(S["sh_o"], i + 1)
                else:
                    act.wait_ge(items_used, 45)
                act.activation(shared[0:n, i, :], ps[0:n, 2 * (i % 2):2 * (i % 2) + 2, :].rearrange("p b n -> p (b n)"),
                               ACT.Copy).then_inc(S["sh_done"], 1)
            act.wait_ge(S["exT"], 1)
            act.activation(flat(xgT), ps[:, 0:2, :].rearrange("p b n -> p (b n)"), ACT.Copy).then_inc(S["exT_done"], 1)
            ov = act.alloc_register("ov_act")
            act.reg_mov(ov, 0)
            with act.Fori(0, E // 4) as g:
                for u in range(4):
                    e = g * 4 + u
                    act.wait_ge(S["ex13"], e + 1)
                    act.activation(esil[:, u % 2].rearrange("p f s -> p (f s)"), ps[:, 2 + u % 2, 0:256], ACT.Silu).then_inc(S["ex_sil"], 1)

                    def next_rows():
                        act.wait_ge(S["exT"], e + 2)
                        act.activation(flat(xgT), ps[:, 0:2, :].rearrange("p b n -> p (b n)"), ACT.Copy).then_inc(S["exT_done"], 1)

                    if u < 3:
                        next_rows()
                    else:
                        with act.If(g < E // 4 - 1):
                            next_rows()
                    more = act.value_load(cnt_i[0:1, 1, ds(e, 1)], min_val=0, max_val=4)
                    with act.If(more > 0):
                        with act.Fori(0, more) as b:
                            o = act.snap(ov, min_val=0, max_val=EXTRA - 1)
                            act.wait_ge(S["ovT"], o + 1)
                            act.activation(flat(xgTo), ps[:, 6:8, :].rearrange("p b n -> p (b n)"), ACT.Copy).then_inc(S["ovT_done"], 1)
                            act.wait_ge(S["ov13"], o + 1)
                            act.activation(flat(esilo), ps[:, 3 - u % 2, 0:256], ACT.Silu).then_inc(S["ov_sil"], 1)
                            act.reg_add(ov, ov, 1)
            act.wait_ge(S["g2_pe"], 1)
            mark(act.activation(G2, ps[:, 0:2, :].rearrange("p b n -> p (b n)"), ACT.Copy), "G2_act")
            mark(act.activation(G2s, ps[0:NS, 2:4, :].rearrange("p b n -> p (b n)"), ACT.Copy), "G2_act")
            for i in range(TT):
                n = P if i < TT - 1 else LAST
                act.wait_ge(S["yacc"], i + 1)
                act.activation(accb[0:n, 2 + i % 2, :], accb[0:n, i % 2, :], ACT.Square,
                               accum_out=red[0:n, 1:2]).then_inc(S["fin_sq"], 1)
                act.wait_ge(S["fin_sq"], i + 1)
                act.activation(red[0:n, 2:3], red[0:n, 1:2], ACT.Sqrt, bias=eps[0:n, 0:1], scale=1.0 / D).then_inc(S["fin_rt"], 1)

        @block.vector
        def _(dve):
            counts = {}

            def link(ins, name=None, wait=True):
                key = name or "dve_step"
                counts[key] = counts.get(key, 0) + 1
                ins.then_inc(S[name] if name else dve_step, 1)
                if wait:
                    dve.wait_ge(S[name] if name else dve_step, counts[key])

            tt, ts, stt = dve.tensor_tensor, dve.tensor_scalar, dve.scalar_tensor_tensor

            def bc(ap, n):
                return ap.unsqueeze(len(ap.shape)).to_broadcast(list(ap.shape) + [n])

            dve.wait_ge(S["vecs_act"], 1)
            dve.wait_ge(items_used, 4)
            link(tt(ada[:, 0:2, :, :].rearrange("p a c s -> p (a c) s"),
                    ps[:, 4, 0:2 * C * NSEQ].rearrange("p (a s) -> p a s", s=NSEQ), bc(vecs[:, V_ADA:V_ADA + 2 * C], NSEQ), ALU.add))
            link(stt(out=s1[:, :, :], in0=ada[:, 1], scalar=1.0, in1=bc(vecs[:, V_PRE1:V_PRE1 + C], NSEQ),
                     op0=ALU.add, op1=ALU.mult), "s1_dve")
            dve.wait_ge(S["xrt_act"], 2)
            link(dve.reciprocal(rs[:, :], rs[:, :]))
            for c in range(C):
                link(tt(hT[:, c, :], xT[:, c, :], rs[:, :], ALU.mult), "xn_dve", wait=False)
            dve.wait_ge(S["xn_dve"], C)
            link(tt(smp[:, :, :], hT[:, :, NP:T], s1[:, :, 1:NSEQ], ALU.mult))
            link(tt(hT[:, :, NP:T], smp[:, :, :], ada[:, 0, :, 1:NSEQ], ALU.add), "h_s_dve")
            dve.wait_ge(S["stB_act"], 4)
            dve.wait_ge(consts, 10)
            KA = 43
            with dve.Fori(0, C // 2) as it:
                for jj in range(2):
                    j = it * 2 + jj
                    n = [0]

                    def chain(ins, wait=True):
                        n[0] += 1
                        ins.then_inc(S["pa_chain"], 1)
                        if wait:
                            dve.wait_ge(S["pa_chain"], j * KA + n[0])

                    def at(ap3):
                        return ap3.rearrange("p a n -> p (a n)")

                    dve.wait_ge(S["bval"], j + 1)
                    dve.wait_ge(S["sg_done"], j + 1)
                    chain(tt(glu[:, KC - 1:KC - 1 + HT], ps[:, 2, 0:HT], sg[:, 0:HT], ALU.mult), wait=False)
                    chain(tt(glu[:, KC - 1 + HT:KC - 1 + NP], ps[:, 3, 0:NP - HT], sg[:, HT:NP], ALU.mult), wait=False)
                    chain(dve.tensor_copy(glus[:, :, 0:KC - 1],
                                          at(stB[:, ds(j, 1), :]).rearrange("p (n k) -> p n k", n=NS)), wait=False)
                    chain(tt(glus[:, :, KC - 1], ps[:, 3, NP - HT:HT], sg[:, NP:T], ALU.mult))
                    chain(dve.tensor_copy(at(tail[:, ds(j, 1), 0:KC - 1]), glu[:, NP:NP + KC - 1]), wait=False)
                    dve.tensor_copy(at(tail[:, ds(j, 1), KC - 1:KC - 1 + NS]), glus[:, :, KC - 1]).then_inc(S["glu_done"], 1)
                    dve.wait_ge(S["glu_done"], j + 2)
                    acc = at(cv[:, ds(j, 1), 0:NP])
                    chain(ts(acc, glu[:, 0:NP], vecs[:, ds(j + V_WC, 1)], vecs[:, ds(j + V_BC, 1)], ALU.mult, ALU.add))
                    for k in range(1, KC):
                        chain(stt(out=acc, in0=glu[:, k:k + NP], scalar=vecs[:, ds(j + (V_WC + 8 * k), 1)], in1=acc,
                                  op0=ALU.mult, op1=ALU.add))
                    wk = vecs[:, V_WC:V_WC + 8 * KC].rearrange("p (k c) -> p c k", c=C)[:, ds(j, 1), :]
                    chain(tt(tmps[:, :, :], glus[:, :, :], wk.to_broadcast([P, NS, KC]), ALU.mult))
                    chain(dve.tensor_reduce(smp[:, 0, :], tmps[:, :, :], AX.X, ALU.add))
                    chain(ts(at(cv[:, ds(j, 1), NP:T]), smp[:, 0, :], vecs[:, ds(j + V_BC, 1)], None, ALU.add), wait=False)
                    dve.wait_ge(S["u_done"], j + 2)
                    dve.wait_ge(S["va_done"], j + 1)
                    for k in range(KS):
                        w = vecs[:, ds(j + (V_SC + 8 * k), 1)]
                        if k == 0:
                            chain(ts(vv[:, 0:NP], up[:, 0:NP], w, None, ALU.mult))
                        else:
                            chain(stt(out=vv[:, 0:NP], in0=up[:, k:k + NP], scalar=w, in1=vv[:, 0:NP], op0=ALU.mult, op1=ALU.add))
                    ws = vecs[:, V_SC:V_SC + 8 * KS].rearrange("p (k c) -> p c k", c=C)[:, ds(j, 1), :]
                    chain(tt(tmps[:, :, 0:KS], us[:, :, :], ws.to_broadcast([P, NS, KS]), ALU.mult))
                    dve.tensor_reduce(vv[:, NP:T], tmps[:, :, 0:KS], AX.X, ALU.add).then_inc(S["v_done"], 1)
                    dve.wait_ge(items_used, it * 4 + (6 + 2 * jj))
                    bias = vecs[:, V_ADA + 2 * C:V_ADA + 6 * C].rearrange("p (a c) -> p c a", c=C)[:, ds(j, 1), :]
                    tt(ada[:, 2:6, ds(j, 1), :].rearrange("p a c s -> p (a c) s"),
                       ps[:, 6, 0:4 * NSEQ].rearrange("p (a s) -> p a s", s=NSEQ),
                       bc(bias.rearrange("p c a -> p (c a)"), NSEQ), ALU.add).then_inc(S["ada2_done"], 1)
                    assert n[0] == KA, n[0]
            dve.wait_ge(late_in, 48)
            dve.wait_ge(S["growc_act"], 1)
            link(tt(grow, grow, grow2, ALU.mult), "grow_dve")
            dve.wait_ge(S["mean_pe"], 1)
            for h, (a, b) in enumerate(half):
                link(tt(cv[:, :, a:b], cv[:, :, a:b], ps[:, 4 + h, 0:HT].unsqueeze(1).to_broadcast([P, C, HT]), ALU.subtract), "cen_dve")

            def merge_a(j):
                dve.wait_ge(items_used, 21 + j)
                dve.wait_ge(S["g_done"], j + 1)
                for h, (a, b) in enumerate(half):
                    ins = tt(mT[:, j, a:b], sg[:, a:b], ps[:, 2 + h, 0:HT], ALU.mult)
                ins.then_inc(S["m_done"], 1)

            for j in range(4):
                merge_a(j)
            dve.wait_ge(S["lrt_act"], 2)
            link(dve.reciprocal(rs[:, :], rs[:, :]))
            for j in range(4, C):
                for c in range(2 * (j - 4), 2 * (j - 4) + 2):
                    link(tt(cv[:, c, :], cv[:, c, :], rs[:, :], ALU.mult), "ln_dve", wait=False)
                merge_a(j)
            with dve.Fori(0, 2) as it:
                for jj in range(4):
                    j = it * 4 + jj
                    dve.wait_ge(items_used, j + 29)
                    dve.wait_ge(S["g_done"], j + 9)
                    for h, (a, b) in enumerate(half):
                        stt(out=sg[:, a:b], in0=ps[:, 2 + h, 0:HT], scalar=vecs[:, ds(j + V_OB, 1)], in1=sg[:, a:b],
                            op0=ALU.add, op1=ALU.mult).then_inc(S["m_chain"], 1)
                    dve.wait_ge(S["m_chain"], j * 2 + 2)
                    mj = mT[:, ds(j, 1), :].rearrange("p a t -> p (a t)")
                    tt(mj, mj, sg[:, :], ALU.add).then_inc(S["m_done"], 1)
            link(tt(ada[:, 2], ada[:, 2], bc(vecs[:, V_POST1:V_POST1 + C], NSEQ), ALU.mult))
            link(stt(out=s1[:, :, :], in0=ada[:, 4], scalar=1.0, in1=bc(vecs[:, V_PRE2:V_PRE2 + C], NSEQ),
                     op0=ALU.add, op1=ALU.mult))
            dve.wait_ge(S["trt_act"], 2)
            link(dve.reciprocal(rs[:, :], rs[:, :]))
            for c in range(C):
                link(tt(hT[:, c, :], hT[:, c, :], rs[:, :], ALU.mult))
                link(tt(smp[:, c, :], hT[:, c, NP:T], ada[:, 2, c, 1:NSEQ], ALU.mult), wait=False)
                link(stt(out=xT[:, c, 0:NP], in0=hT[:, c, 0:NP], scalar=ada[:, 2, c, 0:1], in1=xT[:, c, 0:NP],
                         op0=ALU.mult, op1=ALU.add))
                link(tt(xT[:, c, NP:T], xT[:, c, NP:T], smp[:, c, :], ALU.add), "x1_dve", wait=False)
            dve.wait_ge(S["x1rt_act"], 2)
            link(dve.reciprocal(rs[:, :], rs[:, :]))
            for c in range(C):
                link(tt(hT[:, c, :], xT[:, c, :], rs[:, :], ALU.mult), "x1n_dve", wait=False)
            dve.wait_ge(S["x1n_dve"], C)
            link(tt(smp[:, :, :], hT[:, :, NP:T], s1[:, :, 1:NSEQ], ALU.mult))
            link(tt(hT[:, :, NP:T], smp[:, :, :], ada[:, 3, :, 1:NSEQ], ALU.add), "h2_s_dve")
            dve.wait_ge(S["x1t_T"], TT)
            link(dve.memset(score[:, TT - 1, :], 0.5), "score0_dve")
            dve.wait_ge(S["score_s_act"], 1)
            dve.wait_ge(late_in, 48)
            link(tt(sel, score, ebias[:, :].unsqueeze(1).to_broadcast([P, TT, E]), ALU.add))
            gs, g8, gi, gm, gneg, t8, wk8, wsum, eif, rowk = (s8(n) for n in range(10))
            gi_u = s8(10).bitcast(U32)
            row_i = s8(11).bitcast(I32)
            top = eq
            for i in range(TT):
                for q in range(NG):
                    link(dve.max(out=top[:, q, 0:8], in_=sel[:, i, q * EG:(q + 1) * EG]), wait=(q == NG - 1))
                link(tt(gs[:, i, :], top[:, :, 0], top[:, :, 1], ALU.add))
            for i in range(TT):
                link(dve.max(out=g8[:, i, :], in_=gs[:, i, :]))
                link(dve.max_index(out=gi_u[:, i, :], in_max=g8[:, i, :], in_values=gs[:, i, :]))
            link(dve.tensor_copy(gi, gi_u))
            for i in range(TT):
                em = eq[:, 0:TOPG, 0:NG]
                link(tt(em, iot[:, 0:NG].unsqueeze(1).to_broadcast([P, TOPG, NG]), bc(gi[:, i, 0:TOPG], NG), ALU.is_equal))
                link(dve.tensor_reduce(gm[:, i, :], em.rearrange("p j g -> p g j"), AX.X, ALU.add))
            link(ts(gneg, gm, -NEG, NEG, ALU.mult, ALU.add))
            for i in range(TT):
                sv, mv = (t[:, i, :].rearrange("p (g q) -> p g q", g=NG) for t in (sel, selm))
                link(tt(mv, sv, bc(gm[:, i, :], EG), ALU.mult))
                link(tt(mv, mv, bc(gneg[:, i, :], EG), ALU.add))
            for i in range(TT):
                link(dve.max(out=t8[:, i, :], in_=selm[:, i, :]))
                link(dve.max_index(out=gi_u[:, i, :], in_max=t8[:, i, :], in_values=selm[:, i, :]), wait=False)
                link(dve.match_replace(out=repl[:, i, :], in_to_replace=t8[:, i, :], in_values=selm[:, i, :], imm_value=2 * NEG))
            link(dve.tensor_copy(eif, gi_u), wait=False)
            link(ts(repl, repl, 1.5 * NEG, None, ALU.is_le))
            link(tt(mask16[:, :, :], repl, bc(valid[:, :], E), ALU.mult), "mask_dve")
            def shared_act(f):
                dve.wait_ge(S["g_done"], 17 + f)
                for h, (a, b) in enumerate(half):
                    ins = tt(scr[:, 2 + f, a:b], sg[:, a:b], ps[:, 2 + h, 0:HT], ALU.mult)
                ins.then_inc(S["sh_act"], 1)

            shared_act(0)
            dve.wait_ge(S["rank_pe"], 1)
            link(dve.tensor_copy(rank, ps[:, 5, 0:RE].rearrange("p (i e) -> p i e", i=TT)))
            cnt, nov, ovb, wide, one64, ybase = (e64[:, n, :] for n in range(6))
            link(dve.tensor_copy(cnt, ps[:, 6, 0:E]))
            link(ts(nov, cnt, P + 0.5, None, ALU.is_gt))
            for m in range(2, TT):
                link(stt(out=nov, in0=cnt, scalar=m * P + 0.5, in1=nov, op0=ALU.is_gt, op1=ALU.add))
            link(ts(wide, cnt, P // 2 + 0.5, None, ALU.is_gt))
            link(dve.memset(one64, 1.0))
            link(dve.tensor_tensor_scan(out=ovb, data0=one64, data1=nov, initial=0.0, op0=ALU.mult, op1=ALU.add))
            link(tt(ovb, ovb, nov, ALU.subtract))
            link(dve.tensor_tensor_scan(out=ybase, data0=one64, data1=cnt, initial=0.0, op0=ALU.mult, op1=ALU.add))
            link(tt(ybase, ybase, cnt, ALU.subtract))
            link(dve.tensor_copy(cnt_i[0:1, 0, 0:E], wide[0:1, :]), wait=False)
            link(dve.tensor_copy(cnt_i[0:1, 2, 1:E + 1], wide[0:1, :]), wait=False)
            link(dve.tensor_copy(cnt_i[0:1, 1, 0:E], nov[0:1, :]))
            link(stt(out=ovb, in0=ovb, scalar=float(E - 1), in1=iot[:, 0:E], op0=ALU.add, op1=ALU.subtract))
            link(ts(blk, rank, P - 0.5, None, ALU.is_gt))
            for m in range(2, TT):
                link(stt(out=blk, in0=rank, scalar=m * P - 0.5, in1=blk, op0=ALU.is_gt, op1=ALU.add))
            link(tt(tmpr, blk, ovb.unsqueeze(1).to_broadcast([P, TT, E]), ALU.add))
            link(stt(out=tmpr, in0=blk, scalar=0.5, in1=tmpr, op0=ALU.is_gt, op1=ALU.mult))
            link(tt(tmpr, tmpr, iot[:, 0:E].unsqueeze(1).to_broadcast([P, TT, E]), ALU.add))
            link(stt(out=row, in0=blk, scalar=-float(P), in1=rank, op0=ALU.mult, op1=ALU.add))
            link(stt(out=row, in0=tmpr, scalar=float(P), in1=row, op0=ALU.mult, op1=ALU.add))
            shared_act(1)
            for i in range(TT):
                link(tt(eq, iot[:, 0:E].unsqueeze(1).to_broadcast([P, TOPK, E]), bc(eif[:, i, :], E), ALU.is_equal))
                link(tt(eqm, eq, row[:, i, :].unsqueeze(1).to_broadcast([P, TOPK, E]), ALU.mult))
                link(dve.tensor_reduce(rowk[:, i, :], eqm, AX.X, ALU.add))
            link(ts(gs[:, :, 0], valid[:, :], -float(P * P), float(P * P), ALU.mult, ALU.add))
            link(tt(rowk, rowk, bc(valid[:, :], TOPK), ALU.mult))
            link(tt(rowk, rowk, bc(gs[:, :, 0], TOPK), ALU.add))
            place = s8(12).bitcast(I32)
            link(dve.tensor_copy(place, rowk))
            link(ts(row_i, place, P - 1, None, ALU.bitwise_and))
            link(dve.tensor_copy(g8, row_i))
            link(ts(row_i, place, 7, None, ALU.logical_shift_right))
            link(dve.tensor_copy(gi, row_i))
            for i in range(TT):
                for k in range(TOPK):
                    n = i * TOPK + k
                    if n >= 4:
                        dve.wait_ge(S["idx_mm"], n - 3)
                    ts(oneA[:, n % 4, :], iot[:, :], g8[:, i, k:k + 1], None, ALU.is_equal).then_inc(S["idx_ab"], 1)
                    ts(oneB[:, n % 4, :], iot[:, 0:JOBS], gi[:, i, k:k + 1], tokp1[:, i:i + 1], ALU.is_equal, ALU.mult).then_inc(S["idx_ab"], 1)
            dve.wait_ge(S["idx_mm"], TT * TOPK)
            tab, tb2 = eq.rearrange("p k e -> p (k e)")[:, 0:JOBS], eq.rearrange("p k e -> p (k e)")[:, 128:128 + JOBS]
            link(ts(tab, ps[:, 7, 0:JOBS], -1.0, None, ALU.add))
            link(dve.tensor_copy(idxT[:, :], tab))
            link(ts(tab, tab, -0.5, 1e6, ALU.is_lt, ALU.mult))
            link(dve.tensor_copy(beyond[:, :], tab))
            link(ts(tb2[:, 0:E], ybase, slotid[:, 0:1], None, ALU.add))
            link(dve.tensor_copy(firsty[:, :], tb2[:, 0:E]))
            link(tt(tb2[:, 0:E], tab[:, 0:E], tb2[:, 0:E], ALU.add))
            link(dve.tensor_copy(rowT[:, 1:], tb2[:, 0:E]), "table_dve")
            link(tt(tmpr, rank, ybase.unsqueeze(1).to_broadcast([P, TT, E]), ALU.add))
            dve.wait_ge(S["sh_done"], TT)
            dve.memset(ps[:, 2:4, :], 0.0).then_inc(S["sh_act"], 1)
            LA = 10
            ov, tile_no = dve.alloc_register("ov_dve"), dve.alloc_register("tile_no")
            dve.reg_mov(ov, 0)
            dve.reg_mov(tile_no, 0)

            def token_tile(i, u):
                n = [(0, 3, 7, 9)[u]]
                eight = wsum[:, 1, :]

                def chain(ins, wait=True):
                    n[0] += 1
                    ins.then_inc(S["late_chain"], 1)
                    if wait:
                        dve.wait_ge(S["late_chain"], i * LA + n[0])

                def at(ap):
                    return ap[:, ds(i, 1), :].rearrange("p a n -> p (a n)")

                def of_all(ap):
                    return at(ap).unsqueeze(1).to_broadcast([P, TOPK, E])

                if u > 0:
                    dve.wait_ge(S["late_chain"], i * LA + n[0])
                if u == 0:
                    chain(tt(eq, iot[:, 0:E].unsqueeze(1).to_broadcast([P, TOPK, E]), bc(at(eif), E), ALU.is_equal))
                    chain(tt(eqm, eq, of_all(score), ALU.mult))
                    chain(dve.tensor_reduce(eight, eqm, AX.X, ALU.add), wait=False)
                elif u == 1:
                    chain(dve.tensor_reduce(wsum[:, 0, 0:1], eight, AX.X, ALU.add))
                    chain(dve.reciprocal(wsum[:, 0, 1:2], wsum[:, 0, 0:1]))
                    chain(tt(eight, eight, wsum[:, 0, 1:2].to_broadcast([P, TOPK]), ALU.mult))
                    chain(ts(at(gates), eight, ROUTED_SCALE, None, ALU.mult), wait=False)
                elif u == 2:
                    chain(tt(eqm, eq, of_all(tmpr), ALU.mult))
                    chain(dve.tensor_reduce(eight, eqm, AX.X, ALU.add), wait=False)
                else:
                    chain(dve.tensor_copy(at(yidx), eight), wait=False)

            def y_out_of(e, b):
                dve.wait_ge(items_used, e + 46)
                dve.tensor_copy(yb[:, b, :], ps[:, 4:6, :].rearrange("p b n -> p (b n)")).then_inc(S["ex_yd"], 1)

            with dve.Fori(0, E // 4) as g:
                for u in range(4):
                    e = g * 4 + u
                    with dve.If(g < TT):
                        token_tile(dve.snap(tile_no, min_val=0, max_val=TT - 1), u)
                        if u == 3:
                            dve.reg_add(tile_no, tile_no, 1)
                    dve.wait_ge(S["ex_sil"], e + 1)
                    tt(eact[:, u % 2].rearrange("p f s -> p (f s)"), esil[:, u % 2].rearrange("p f s -> p (f s)"),
                       ps[:, 2 + u % 2, 256:512], ALU.mult).then_inc(S["ex_act"], 1)
                    if u == 0:
                        with dve.If(g > 0):
                            dve.wait_ge(y_out[1], g * 16)
                            y_out_of(e - 1, 1)
                    else:
                        if u < 3:
                            with dve.If(g > 0):
                                dve.wait_ge(y_out[u + 1], g * 16)
                                y_out_of(e - 1, u - 1)
                            with dve.If(g < 1):
                                y_out_of(e - 1, u - 1)
                        else:
                            dve.wait_ge(y_out[0], g * 16 + 16)
                            y_out_of(e - 1, 0)
                    more = dve.value_load(cnt_i[0:1, 1, ds(e, 1)], min_val=0, max_val=4)
                    with dve.If(more > 0):
                        with dve.Fori(0, more) as b:
                            o = dve.snap(ov, min_val=0, max_val=EXTRA - 1)
                            dve.wait_ge(S["ov_sil"], o + 1)
                            tt(flat(eacto), flat(esilo), ps[:, 3 - u % 2, 256:512], ALU.mult).then_inc(S["ov_act"], 1)
                            yo = ps[:, 6:8, :].rearrange("p b n -> p (b n)")
                            with dve.If(o > 0):
                                dve.wait_ge(S["ov_y"], o + 1)
                                dve.wait_ge(S["ov_scat"], dve.snap(ov, min_val=1, max_val=EXTRA - 1) * 16)
                                dve.tensor_copy(ybo, yo).then_inc(S["ov_yd"], 1)
                            with dve.If(o < 1):
                                dve.wait_ge(S["ov_y"], o + 1)
                                dve.tensor_copy(ybo, yo).then_inc(S["ov_yd"], 1)
                            dve.reg_add(ov, ov, 1)
            dve.wait_ge(y_out[1], 16 * (E // 4))
            y_out_of(E - 1, 1)
            for i in range(TT):
                n = P if i < TT - 1 else LAST
                acc = accb[0:n, i % 2, :]
                if i >= 2:
                    dve.wait_ge(fin_dma[i % 2], 16 * (i // 2))
                for k in range(TOPK):
                    b = (i % 2) * 8 + k
                    dve.wait_ge(yk_in[b], 16 * (i // 2 + 1))
                    ins = stt(out=acc, in0=yk[0:n, b, :], scalar=gates[0:n, i, k:k + 1],
                              in1=shared[0:n, i, :] if k == 0 else acc, op0=ALU.mult, op1=ALU.add)
                    if k < TOPK - 1:
                        link(ins)
                    else:
                        ins.then_inc(S["yacc"], 1)
                if i == 0:
                    dve.wait_ge(S["G2_act"], 2)
                dve.wait_ge(S["fin_rt"], i + 1)
                link(dve.reciprocal(red[0:n, 2:3], red[0:n, 2:3]))
                link(stt(out=acc, in0=acc, scalar=red[0:n, 2:3], in1=(G2 if i < TT - 1 else G2s)[0:n, :], op0=ALU.mult, op1=ALU.mult))
                tt(accb[0:n, 2 + i % 2, :], acc, x1tok[0:n, i, :], ALU.add).then_inc(S["fin_out"], 1)

        @block.tensor
        def _(pe):
            def mark(ins, name):
                ins.then_inc(S[name], 1)

            mm, tr = pe.matmul, pe.transpose
            pe.wait_ge(consts, 10)
            pe.wait_ge(vrow_in, 16 * 12)
            tr(ps[:, 6, 0:128], vrow, ident[:, :])
            for a in range(2):
                tr(ps[:, 6, 128 + 124 * a:128 + 124 * (a + 1)], wcrow[:, a, :], ident[0:124, 0:124])
            mark(tr(ps[:, 6, 376:504], sarow, ident[:, :]), "vecs_pe")
            pe.wait_ge(S["csilu_act"], 1)
            for c in range(C):
                ins = tr(ps[:, 7, c * NSEQ:(c + 1) * NSEQ], c_tok[:, c * P:(c + 1) * P], ident[0:NSEQ, 0:NSEQ])
            mark(ins, "cT_pe")
            pe.wait_ge(x_in, 32)
            for c in range(C):
                if c >= 4:
                    pe.wait_ge(S["xT_act"], c - 4 + 1)
                for i in range(TT - 1):
                    ins = tr(ps[:, c % 4, i * P:(i + 1) * P], x_tok[:, i, c * P:(c + 1) * P], ident[:, :])
                mark(ins, "xT_pe")
            for c in range(C):
                ins = tr(ps[:, 5, c * NS:(c + 1) * NS], x_stok[:, c * P:(c + 1) * P], ident[0:NS, 0:NS])
            mark(ins, "xs_pe")
            pe.wait_ge(st_in, 16)
            W2 = NS * (KC - 1)
            for r in range(2):
                pe.wait_ge(S["xT_act"], 4 + 2 * r + 1 + 1)
                for q in range(4):
                    c = 4 * r + q
                    for a in range(2):
                        at = (q % 2) * W2 + a * 120
                        ins = tr(ps[:, 2 * r + q // 2, at:at + 120], sbrow[:, a, c * P:(c + 1) * P], ident[0:120, 0:120])
                mark(ins, "stB_pe")
            pe.wait_ge(S["cT_act"], 1)

            for q in range(4):
                pe.wait_ge(w_ada1[q], 32)
                w = ring[:, q, 0:4096].rearrange("p (k a n) -> p k a n", k=C, a=2)
                for a in range(2):
                    for jj in range(2):
                        at = (a * C + 2 * q + jj) * NSEQ
                        for k in range(C):
                            ins = mm(ps[:, 4, at:at + NSEQ], w[:, k, a, jj * P:(jj + 1) * P], scT[:, k, :],
                                     start=(k == 0), stop=(k == C - 1))
                ins.then_inc(items_used, 1)

            def stat(bank, src, c):
                for h, (a, b) in enumerate(half):
                    ins = mm(ps[:, bank + h, 0:HT], avg[:, :], src[:, a:b], start=(c == 0), stop=(c == C - 1))
                return ins

            for c in range(C):
                pe.wait_ge(S["xsq_act"], c + 1)
                ins = stat(6, hT[:, c, :], c)
            mark(ins, "xstat_pe")
            pe.wait_ge(S["h_act"], 8)
            pe.wait_ge(S["h_s_dve"], 1)

            def product(bank, w, src):
                for h, (a, b) in enumerate(half):
                    for k in range(C):
                        ins = mm(ps[:, bank + h, 0:HT], w[:, k, :], src[:, k, a:b], start=(k == 0), stop=(k == C - 1))
                return ins

            with pe.Fori(0, C // 2) as it:
                for jj in range(2):
                    j = it * 2 + jj
                    slot = 2 * jj
                    w = ring[:, slot, 0:5120].rearrange("p (k a n) -> p k a n", k=C, a=5)
                    pe.wait_ge(w_pha[slot], it * 80 + 80)
                    pe.wait_ge(S["acs_done"], j + 1)
                    product(0, w[:, :, 4, :], hT).then_inc(S["bgate"], 1)
                    pe.wait_ge(S["abs_done"], j + 1)
                    product(2, w[:, :, 3, :], hT).then_inc(S["bval"], 1)
                    pe.wait_ge(S["ain_done"], j + 1)
                    product(4, w[:, :, 0, :], hT).then_inc(S["ain"], 1)
                    pe.wait_ge(S["sg_done"], j + 1)
                    product(0, w[:, :, 2, :], hT).then_inc(S["ac"], 1)
                    pe.wait_ge(S["glu_done"], j + 2)
                    product(2, w[:, :, 1, :], hT).then_inc(items_used, 1)
                    slot += 1
                    w = ring[:, slot, 0:4096].rearrange("p (k a n) -> p k a n", k=C, a=4)
                    pe.wait_ge(w_pha[slot], it * 64 + 64)
                    pe.wait_ge(S["ada2_done"], j + 1)
                    for a in range(4):
                        for k in range(C):
                            ins = mm(ps[:, 6, a * NSEQ:(a + 1) * NSEQ], w[:, k, a, :], scT[:, k, :], start=(k == 0), stop=(k == C - 1))
                    ins.then_inc(items_used, 1)
            pe.wait_ge(S["va_done"], C + 1)
            pe.wait_ge(S["ada2_done"], C + 1)
            for c in range(C):
                ins = tr(ps[0:48, 6 + c // 4, (c % 4) * P:(c % 4 + 1) * P], tail[:, c, :], ident[:, :])
            mark(ins, "tails_pe")
            for c in range(C):
                ins = tr(ps[0:NSEQ, 4 + c // 4, (c % 4) * P:(c % 4 + 1) * P], ada[:, 5, c, :], ident[:, :])
            mark(ins, "g2rows_pe")
            pe.wait_ge(S["growc_act"], 1)
            for c in range(C):
                ins = stat(4, cv[:, c, :], c)
            mark(ins, "mean_pe")

            def merge(it, jj, br, src):
                w = ring[:, jj, 0:2048].rearrange("p (k a n) -> p k a n", k=C, a=2)
                q = it * 4 + (jj + 8 * br)
                pe.wait_ge(w_m[jj], it * 32 + (32 + 64 * br))
                if not (isinstance(it, int) and it + jj + br == 0):
                    pe.wait_ge(S["g_done"], q)
                product(0, w[:, :, 0, :], hT).then_inc(S["g_mm"], 1)
                pe.wait_ge(S["m_done"], q + 1)
                product(2, w[:, :, 1, :], src).then_inc(items_used, 1)

            for it in range(2):
                for jj in range(4):
                    if it == 0 and jj == 0:
                        pe.wait_ge(S["cen_dve"], 2)
                    merge(it, jj, 0, va)
                if it == 0:
                    for c in range(C):
                        pe.wait_ge(S["sqd"], c + 1)
                        stat(6, scr[:, c % 4, :], c).then_inc(S["stat_mm"], 1)
            pe.wait_ge(S["s_act"], 8)
            with pe.Fori(0, 2) as it:
                for jj in range(4):
                    merge(it, jj, 1, cv)
            pe.wait_ge(S["m_done"], 17)
            for j in range(C + 1):
                if j < C:
                    pe.wait_ge(w_wo[j % 4], 16 * (j // 4 + 1))
                    if j >= 2:
                        pe.wait_ge(S["t_cp"], j)
                    product(2 * (j % 2), ring[:, j % 4, 0:1024].rearrange("p (k n) -> p k n", k=C), mT).then_inc(items_used, 1)
                if j > 0:
                    pe.wait_ge(S["sqd"], 8 + j)
                    stat(6, scr[:, (j - 1) % 4, :], j - 1).then_inc(S["stat_mm"], 1)
            for j in range(C):
                pe.wait_ge(S["sqd"], 17 + j)
                stat(4, scr[:, j % 4, :], j).then_inc(S["stat_mm"], 1)
            for i in range(TT):
                n = P if i < TT - 1 else LAST
                if i >= 1:
                    pe.wait_ge(S["x1t_done"], i)
                for c in range(C):
                    ins = tr(ps[0:n, c // 4, (c % 4) * P:(c % 4 + 1) * P], xT[:, c, i * P:i * P + n], ident[:, :])
                ins.then_inc(S["x1t_T"], 1)
            pe.wait_ge(S["h2_act"], 8)
            pe.wait_ge(S["h2_s_dve"], 1)
            pe.wait_ge(late_in, 48)
            for i in range(TT):
                n = P if i < TT - 1 else LAST
                for k in range(C):
                    ins = mm(ps[0:n, 4, i * E:(i + 1) * E], hT[:, k, i * P:i * P + n], wr[:, k, :], start=(k == 0), stop=(k == C - 1))
            mark(ins, "logits_pe")
            for i in range(TT):
                n = P if i < TT - 1 else LAST
                if i >= 1:
                    pe.wait_ge(S["hx_done"], i)
                for c in range(C):
                    ins = tr(ps[0:n, 2 + c // 4, (c % 4) * P:(c % 4 + 1) * P], hT[:, c, i * P:i * P + n], ident[:, :])
                ins.then_inc(S["hx_T"], 1)
            def shared_up(f):
                for m in range(2):
                    w = ring[:, 0, 2048 * m:2048 * (m + 1)].rearrange("p (k n) -> p k n", k=C)[:, :, f * P:(f + 1) * P]
                    ins = product(2 * m, w, hT)
                ins.then_inc(S["sh_mm"], 1)

            pe.wait_ge(w_sh, 48)
            pe.wait_ge(S["hx_done"], TT)
            pe.wait_ge(S["x1t_done"], TT)
            shared_up(0)
            pe.wait_ge(S["mask_dve"], 1)
            for i in range(TT):
                for q in range(i):
                    mm(ps[:, 5, i * E:(i + 1) * E], ones16[:, :], mask16[:, q, :], start=(q == 0), stop=False)
                mm(ps[:, 5, i * E:(i + 1) * E], upper[:, :], mask16[:, i, :], start=(i == 0), stop=True)
            for i in range(TT):
                ins = mm(ps[:, 6, 0:E], ones16[:, :], mask16[:, i, :], start=(i == 0), stop=(i == TT - 1))
            mark(ins, "rank_pe")
            pe.wait_ge(S["sh_act"], 1)
            shared_up(1)
            pe.wait_ge(S["sh_act"], 2)
            w2s = ring[:, 0, 4096:6144].rearrange("p (k n) -> p k n", k=FT)
            for i in range(TT):
                n = P if i < TT - 1 else LAST
                if i >= 2:
                    pe.wait_ge(S["sh_done"], i - 1)
                for h in range(2):
                    for k in range(FT):
                        ins = mm(ps[0:n, 2 * (i % 2) + h, :], scr[:, 2 + k, i * P:i * P + n], w2s[:, k, h * 512:(h + 1) * 512],
                                 start=(k == 0), stop=(k == FT - 1))
                ins.then_inc(S["sh_o"] if i < TT - 1 else items_used, 1)
            for n in range(TT * TOPK):
                pe.wait_ge(S["idx_ab"], 2 * n + 2)
                mm(ps[:, 7, 0:JOBS], oneA[:, n % 4, :], oneB[:, n % 4, :], start=(n == 0), stop=(n == TT * TOPK - 1)).then_inc(S["idx_mm"], 1)

            def rows_T(src, bank=0):
                v = src.rearrange("s (m c) -> s c m", c=C)
                for c in range(C):
                    ins = tr(ps[:, bank + c // 4, (c % 4) * P:(c % 4 + 1) * P], v[:, c, :], ident[:, :])
                return ins

            def up_products(slot, bank, src, n):
                for m in range(2):
                    w = ring[:, slot, 2048 * m:2048 * (m + 1)].rearrange("p (k n) -> p k n", k=C)
                    for f in range(FT):
                        q = 2 * m + f
                        for k in range(C):
                            ins = mm(ps[:, bank, q * P:q * P + n], w[:, k, f * P:(f + 1) * P], src[:, k, 0:n],
                                     start=(k == 0), stop=(k == C - 1))
                return ins

            def down_products(slot, src, bank=4):
                w = ring[:, slot, 4096:6144].rearrange("p (k n) -> p k n", k=FT)
                for h in range(2):
                    for k in range(FT):
                        ins = mm(ps[:, bank + h, :], src[:, k, :], w[:, k, h * 512:(h + 1) * 512], start=(k == 0), stop=(k == FT - 1))
                return ins

            pe.wait_ge(S["sh_act"], 3)
            pe.wait_ge(S["sh_done"], TT)
            pe.wait_ge(S["table_dve"], 1)
            pe.wait_ge(xg_in[0], 16)
            rows_T(xg[:, 0, :]).then_inc(S["exT"], 1)
            ov = pe.alloc_register("ov_pe")
            pe.reg_mov(ov, 0)
            with pe.Fori(0, E // 4) as g:
                for u in range(4):
                    e = g * 4 + u
                    slot = (u + 1) % 4
                    pe.wait_ge(w_ex[slot], g * 48 + 48)
                    pe.wait_ge(S["exT_done"], e + 1)
                    wide = pe.value_load(cnt_i[0:1, 0, ds(e, 1)], min_val=0, max_val=1)
                    with pe.If(wide > 0):
                        up_products(slot, 2 + u % 2, xgT, P).then_inc(S["ex13"], 1)
                    with pe.If(wide < 1):
                        up_products(slot, 2 + u % 2, xgT, P // 2).then_inc(S["ex13"], 1)

                    def next_rows():
                        pe.wait_ge(xg_in[(u + 1) % 2], g * 32 + 16 * ((u + 1) // 2 + 1))
                        rows_T(xg[:, (u + 1) % 2, :]).then_inc(S["exT"], 1)

                    def last_down():
                        pe.wait_ge(S["ex_act"], e)
                        pe.wait_ge(S["ex_yd"], e)
                        down_products((slot + 3) % 4, eact[:, (u + 3) % 2]).then_inc(items_used, 1)

                    if u < 3:
                        next_rows()
                    else:
                        with pe.If(g < E // 4 - 1):
                            next_rows()
                    if u > 0:
                        last_down()
                    else:
                        with pe.If(g > 0):
                            last_down()
                    more = pe.value_load(cnt_i[0:1, 1, ds(e, 1)], min_val=0, max_val=4)
                    with pe.If(more > 0):
                        with pe.Fori(0, more) as b:
                            o = pe.snap(ov, min_val=0, max_val=EXTRA - 1)
                            pe.wait_ge(S["ovx"], o * 16 + 16)
                            pe.wait_ge(S["ov_yd"], o + 1)
                            rows_T(xgo, 6).then_inc(S["ovT"], 1)
                            pe.wait_ge(S["ovT_done"], o + 1)
                            up_products(slot, 3 - u % 2, xgTo, P).then_inc(S["ov13"], 1)
                            pe.wait_ge(S["ov_act"], o + 1)
                            down_products(slot, eacto, 6).then_inc(S["ov_y"], 1)
                            pe.reg_add(ov, ov, 1)
            pe.wait_ge(S["ex_act"], E)
            pe.wait_ge(S["ex_yd"], E)
            down_products(0, eact[:, 1]).then_inc(items_used, 1)
            for h in range(2):
                mm(ps[:, h, :], firstrow[:, :], grow[:, h * 512:(h + 1) * 512], start=True, stop=True)
            for h in range(2):
                ins = mm(ps[0:NS, 2 + h, :], ident[0:NSEQ, 1:NSEQ], grow[:, h * 512:(h + 1) * 512], start=True, stop=True)
            mark(ins, "g2_pe")


_INS = ['x_prompt', 'x_sample', 'state_sconv', 'state_cconv', 'c_prompt', 'c_sample', 'w_ada', 'b_ada',
        'g_pre1', 'g_post1', 'g_pre2', 'g_post2', 'w_in', 'w_sconv', 'w_out_a', 'w_cconv', 'b_cconv', 'ln_g', 'ln_b',
        'w_out_b', 'b_out_b', 'w_o', 'w_router', 'e_bias', 'w1', 'w3', 'w2', 'ws1', 'ws3', 'ws2']


def kernel(**inputs):
    import numpy as _np
    import concourse.bacc as _bacc
    from concourse import mybir as _mybir
    from concourse.bass_utils import run_bass_kernel_spmd as _run

    nc = _bacc.Bacc("TRN2", target_bir_lowering=False, num_devices=1)
    arrays, args = {}, []
    for name in _INS:
        a = _np.ascontiguousarray(inputs[name])
        arrays[f"in_{name}_dram"] = a
        args.append(nc.dram_tensor(f"in_{name}_dram", a.shape, _mybir.dt.from_np(a.dtype), kind="ExternalInput").ap())
    x_p, x_s, st_a, st_b = (inputs[n].shape for n in ("x_prompt", "x_sample", "state_sconv", "state_cconv"))
    shapes = [x_p, x_s, (st_a[0], x_p[0], st_a[2], st_a[3]), st_a, (st_b[0], x_p[0], st_b[2], st_b[3]), st_b]
    for i, shape in enumerate(shapes):
        args.append(nc.dram_tensor(f"out_{i}_dram", shape, _mybir.dt.float32, kind="ExternalOutput").ap())
    build_program(nc, *args)
    r = _run(nc, [arrays], core_ids=[0])
    return tuple(r.results[0][f"out_{i}_dram"] for i in range(len(shapes)))
```

```python
from contextlib import ExitStack

import concourse.bass as bass
from concourse import mybir

F32 = mybir.dt.float32
F32R = mybir.dt.float32r
F16 = mybir.dt.float16
I32 = mybir.dt.int32
U32 = mybir.dt.uint32
ALU = mybir.AluOpType
ACT = mybir.ActivationFunctionType
AX = mybir.AxisListType
ds = bass.ds

P = 128
RMS_EPS = 1e-6
LN_EPS = 1e-5
ROUTED_SCALE = 2.5
NEG = -1e30


def build_program(
    nc, x_prompt, x_sample, state_sconv, state_cconv, c_prompt, c_sample,
    w_ada, b_ada, g_pre1, g_post1, g_pre2, g_post2, w_in, w_sconv, w_out_a,
    w_cconv, b_cconv, ln_g, ln_b, w_out_b, b_out_b, w_o, w_router, e_bias,
    w1, w3, w2, ws1, ws3, ws2,
    y_prompt, y_sample, new_sconv_p, new_sconv_s, new_cconv_p, new_cconv_s,
):
    D = x_prompt.shape[2]
    NP = x_prompt.shape[1]
    NS = x_sample.shape[0]
    T = NP + NS
    HT = T // 2
    C = D // P
    KS, KC = w_sconv.shape[1], w_cconv.shape[1]
    E, FE = w1.shape[1], w1.shape[3]
    TT = (T + P - 1) // P
    LAST = T - (TT - 1) * P
    TOPK, NG, TOPG = 8, 8, 4
    EG = E // NG
    NSEQ = NS + 1
    EXTRA = (T * TOPK) // (P + 1)
    JOBS = E + EXTRA + 1
    FT = FE // P
    assert T % 2 == 0 and FT == 2 and C == 8 and LAST == NS and E == 64 and NP % P == 0

    h2_rows = nc.dram_tensor("h2_rows", (T, D), F32, kind="Internal").ap()
    y_rows = nc.dram_tensor("y_rows", (T * TOPK, D), F32, kind="Internal").ap()

    ctx = ExitStack()
    with ctx:
        def sb(name, shape, dt=F32):
            return ctx.enter_context(nc.sbuf_tensor(name, shape, dt))

        def sem(name):
            return ctx.enter_context(nc.semaphore(name))

        SLOT = 6144
        RING = 4
        R = C * T
        UNIT = C * P
        RAW0, SPLIT0, ROWS0 = 3 * R, 3 * R + 5 * UNIT, 3 * R + 9 * UNIT

        def parts(*sizes):
            with ExitStack() as inner:
                return [inner.enter_context(nc.sbuf_tensor(f"{n}", [P, size], dt)) for n, size, dt in sizes]

        s_areas = parts(("h_hi", R, F32R), ("h_lo", R, F32R), ("s_hi", R, F32R), ("rawpad", 5 * UNIT, F32),
                        ("wsplit", 4 * UNIT, F32R))
        ring = sb("ring", [P, RING, SLOT])
        x_areas = parts(("xpad", R, F32), ("vm_hi", R, F32R), ("cv_lo", R, F32R), ("va_lo", R, F32R), ("m_lo", R, F32R))
        act5 = sb("act5", [P, 5 * R])

        def tiles(t):
            return t[:, :].rearrange("p (c t) -> p c t", c=C)
        h_hi, h_lo, s_hi = (tiles(t) for t in s_areas[0:3])
        vm_hi, cv_lo, va_lo, m_lo = (tiles(t) for t in x_areas[1:5])
        wsplit = s_areas[4][:, :].rearrange("p (b a k n) -> p b a k n", b=2, a=2, k=C)
        rflat = ring[:, :, :].rearrange("p s n -> p (s n)")
        raw = rflat[:, RAW0:RAW0 + 5 * UNIT].rearrange("p (s k n) -> p s k n", s=5, k=C)
        tT = rflat[:, 2 * R:3 * R].rearrange("p (c t) -> p c t", c=C)
        ada_w = [rflat[:, a:a + 4 * UNIT].rearrange("p (k n) -> p k n", k=C) for a in (0, R, 2 * R, SPLIT0)]
        arow = rflat[0:1 + NS, ROWS0:ROWS0 + 2048]
        assert ROWS0 + 2048 <= RING * SLOT
        def region(n):
            return act5[:, n * R:(n + 1) * R].rearrange("p (c t) -> p c t", c=C)
        xT, hT, cv, va, mT = (region(n) for n in range(5))
        va_before = act5[:, 3 * R - T:4 * R - T].rearrange("p (c t) -> p c t", c=C)
        x_tok = cv.rearrange("p c t -> p (c t)")[:, 0:4 * D].rearrange("p (i d) -> p i d", i=4)
        va_flat = act5[:, 3 * R:4 * R]
        x_stok = va_flat[0:NS, 0:D]
        c_tok = va_flat[0:NSEQ, D:2 * D]
        vrow = va_flat[:, 2 * D:2 * D + P]
        wcrow = va_flat[0:124, 2 * D + P:2 * D + 3 * P].rearrange("p (a c) -> p a c", a=2)
        sarow = va_flat[:, 2 * D + 3 * P:2 * D + 4 * P]
        p2row = va_flat[0:C, 2 * D + 4 * P:2 * D + 5 * P]
        assert 2 * D + 5 * P <= R
        sbrow = act5[0:120, 4 * R:4 * R + 2 * D].rearrange("p (a d) -> p a d", a=2)
        o = 2 * R
        x1tok = act5[:, o:o + TT * D].rearrange("p (i d) -> p i d", i=TT)
        shared = act5[:, o + TT * D:o + 2 * TT * D].rearrange("p (i d) -> p i d", i=TT)
        o += 2 * TT * D
        xg = act5[:, o:o + 2 * D].rearrange("p (b d) -> p b d", b=2)
        assert o + 2 * D <= 5 * R
        hflat = act5[:, R:2 * R]
        xgT = hflat[:, 0:D].rearrange("p (c s) -> p c s", c=C)
        xgTo = hflat[:, D:2 * D].rearrange("p (c s) -> p c s", c=C)
        yb = hflat[:, 2 * D:4 * D].rearrange("p (b d) -> p b d", b=2)
        xflat = act5[:, 0:R]
        RE = TT * E
        def rt(n):
            return xflat[:, n * RE:(n + 1) * RE].rearrange("p (i e) -> p i e", i=TT)
        score, sel, selm, repl, tmpr = (rt(n) for n in range(5))
        rank, row, blk = sel, selm, repl
        o = 5 * RE
        eq, eqm = (xflat[:, o + n * TOPK * E:o + (n + 1) * TOPK * E].rearrange("p (k e) -> p k e", k=TOPK) for n in range(2))
        o += 2 * TOPK * E
        sm = xflat[:, o:o + 13 * TT * 8].rearrange("p (n k) -> p n k", n=13)
        o += 13 * TT * 8
        e64 = xflat[:, o:o + 6 * E].rearrange("p (n e) -> p n e", n=6)
        o += 6 * E
        oneA = xflat[:, o:o + 2 * P].bitcast(F16).rearrange("p (b n) -> p b n", b=4)
        o += 2 * P
        oneB = xflat[:, o:o + 2 * JOBS].bitcast(F16).rearrange("p (b n) -> p b n", b=4)
        assert o + 2 * JOBS <= R
        yk = ring[:, :, :].rearrange("p s n -> p (s n)")[:, 0:16 * D].rearrange("p (b d) -> p b d", b=16)
        accb = ring[:, :, :].rearrange("p s n -> p (s n)")[:, 16 * D:20 * D].rearrange("p (b d) -> p b d", b=4)

        ident = sb("ident", [P, P])
        avg = sb("avg", [P, P])
        upper = sb("upper", [P, P], F16)
        ones16 = sb("ones16", [P, P], F16)
        firstrow = sb("firstrow", [NSEQ, P])
        eps = sb("eps", [P, 2])
        NV = 512
        vecs = sb("vecs", [P, NV])
        scT = sb("scT", [P, C, NSEQ])
        ada = sb("ada", [P, 6, C, NSEQ])
        ada4 = ada[:, :, :, :].rearrange("p a c s -> p (a c s)")[:, 2 * C * NSEQ:].rearrange("p (j n) -> p j n", j=C)
        stB = act5[:, 4 * R + 2 * D:4 * R + 2 * D + C * NS * (KC - 1)].rearrange("p (c n) -> p c n", c=C)
        assert 2 * D + C * NS * (KC - 1) <= R
        wide_n = [KC - 1 + NP, NS * KC, KS - 1 + NP, NS * KS, NS * KC]
        conv = sb("conv", [P, sum(wide_n)])
        def cbuf(n):
            return conv[:, sum(wide_n[:n]):sum(wide_n[:n + 1])]
        glu, up = cbuf(0), cbuf(2)
        glus, us, tmps = (cbuf(n).rearrange("p (s k) -> p s k", s=NS) for n in (1, 3, 4))
        grow = conv[0:NSEQ, 0:D]
        wr = conv[:, D:D + C * E].rearrange("p (k e) -> p k e", k=C)
        sg = sb("sg", [P, T])
        scr = sb("scr", [P, 4, T])
        ain, acs, abs_, vv = (scr[:, n, :] for n in range(4))
        rs = sb("rs", [P, T])
        sflat = scr[:, :, :].rearrange("p n t -> p (n t)")
        xgo, ybo = sflat[:, 0:D], sflat[:, D:2 * D]
        esil = sg[:, 0:512].rearrange("p (b f s) -> p b f s", b=2, f=2)
        eact = rs[:, 0:512].rearrange("p (b f s) -> p b f s", b=2, f=2)
        eacto = conv[:, D:D + 256].rearrange("p (f s) -> p f s", f=2)
        esilo = conv[:, D + 256:D + 512].rearrange("p (f s) -> p f s", f=2)
        tail = sb("tail", [P, C, 48])
        tailrows = rflat[0:48, ROWS0:ROWS0 + D]
        s1 = sb("s1", [P, C, NSEQ])
        smp = sb("smp", [P, C, NS])
        G2 = rflat[:, 20 * D:21 * D]
        G2s = rflat[0:NS, 21 * D:22 * D]
        ebias = sb("ebias", [P, E])
        iot = sb("iot", [P, P])
        tokp1 = sb("tokp1", [P, TT])
        valid = sb("valid", [P, TT])
        slotid = sb("slotid", [P, 1])
        beyond = sb("beyond", [P, JOBS], I32)
        firsty = sb("firsty", [P, E], I32)
        blocks = sb("blocks", [P, TT], I32)
        ioti = cbuf(4).bitcast(I32)
        mask16 = sb("mask16", [P, TT, E], F16)
        def s8(n):
            return sm[:, n, :].rearrange("p (i k) -> p i k", k=8)
        gates = sb("gates", [P, TT, TOPK])
        yidx = sb("yidx", [P, TT, TOPK], I32)
        idxT = sb("idxT", [P, JOBS], I32)
        rowT = sb("rowT", [P, E + 1], I32)
        cnt_i = sb("cnt_i", [1, 3, E + 2], I32)
        gidx = sb("gidx", [P, 6], I32)
        sidx = sb("sidx", [P, 6], I32)
        red = sb("red", [P, 4])

        ps = ctx.enter_context(nc.psum_tensor("ps", [P, 8, 512], F32))

        V_ADA, V_PRE1, V_POST1, V_PRE2, V_SC, V_BC, V_LG, V_LB, V_OB = 0, 48, 56, 64, 72, 96, 104, 112, 120
        V_WC, V_SA, V_POST2 = 128, 376, 504

        consts = sem("consts")
        crow_in, vrow_in, x_in, st_in, late_in = (sem(n) for n in ("crow_in", "vrow_in", "x_in", "st_in", "late_in"))
        out_done = sem("out_done")
        w_ada1 = [sem(f"w_ada1_{s}") for s in range(RING)]
        w_ada2 = sem("w_ada2")
        w_raw = [sem(f"w_raw_{s}") for s in range(5)]
        w_sh = sem("w_sh")
        w_ex = [sem(f"w_ex_{s}") for s in range(RING)]
        items_used = sem("items_used")
        dve_step = sem("dve_step")
        pool_step = sem("pool_step")
        names = ("w_hi w_lo ada_row arow_done ada_T sp_passed va_hi_act va_lo_pool h_lo_dve cv_lo_dve m_split m_lo_dve sg_done ain_done acs_done abs_done glu_done ada2_done u_done v_done va_done "
                 "pa_chain pool_chain "
                 "vecs_pe vecs_act cT_pe cT_act xT_pe xT_act xs_pe xs_act xsq_act xstat_pe xrt_act stB_pe stB_act csilu_act "
                 "s1_dve xn_dve h_act h_s_dve tails_pe tailrows_act g2rows_pe growc_act p2_dve g2_pe G2_act "
                 "mean_pe cen_dve lrt_act ln_dve s_act trt_act x1_dve x1rt_act x1n_dve h2_act h2_s_dve logits_pe "
                 "score0_dve score_act score_s_act mask_dve rank_pe table_dve late_chain "
                 "g_done m_done m_chain t_cp stat_mm sqd idx_ab idx_mm hx_T hx_done "
                 "x1t_T x1t_done sh_mm sh_act sh_o sh_done "
                 "exT exT_done ex13 ex_sil ex_act ex_yd gcopy scopy pool_passed "
                 "ovT ovT_done ov13 ov_sil ov_act ov_y ov_yd ovcopy ovx ov_scat yacc fin_sq fin_rt fin_out").split()
        S = {n: sem(n) for n in names}
        hx_out = [sem(f"hx_out{b}") for b in range(2)]
        fin_dma = [sem(f"fin_dma{b}") for b in range(2)]
        xg_in = [sem(f"xg_in{b}") for b in range(2)]
        y_out = [sem(f"y_out{u}") for u in range(4)]
        yk_in = [sem(f"yk_in{b}") for b in range(16)]

        def flat(ap):
            return ap.rearrange("p c t -> p (c t)")

        half = [(0, HT), (HT, T)]

        block = ctx.enter_context(nc.Block())

        @block.sync
        def _(sp):
            def w_src(t, col, n):
                return t[0, :, col:col + n].rearrange("(k p) n -> p k n", p=P)

            sp.dma_start(x_tok, x_prompt[0].rearrange("(i p) d -> p i d", p=P)).then_inc(x_in, 16)
            for q in range(4):
                sp.dma_start(ada_w[q], w_src(w_ada, q * 512, 512)).then_inc(w_ada1[q], 16)
            def passed():
                sp.sem_inc(S["sp_passed"], 1)

            with sp.Fori(0, C // 2) as it:
                for jj in range(2):
                    j = it * 2 + jj
                    chunk = sp.snap(it * 1024 + (jj * 512 + 2 * D), min_val=2 * D, max_val=6 * D - 512)
                    for i, a in enumerate((4, 3, 0, 2, 1)):
                        sp.wait_ge(S["w_lo"], it * 10 + (5 * jj + i + 1))
                        passed()
                        sp.dma_start(raw[:, i], w_in[0, :, ds(j * P + a * D, P)].rearrange("(k p) n -> p k n", p=P)
                                     ).then_inc(w_raw[i], 16)
                    sp.wait_ge(S["ada_row"], it * 2 + (jj + 4))
                    passed()
                    sp.dma_start(ada_w[2], w_ada[0, :, ds(chunk, 512)].rearrange("(k p) n -> p k n", p=P)
                                 ).then_inc(w_ada2, 16)
            for br, (gcol, wout) in enumerate(((5, w_out_a), (6, w_out_b))):
                with sp.Fori(0, 2) as it:
                    for jj in range(4):
                        j = it * 4 + jj
                        for i in range(2):
                            slot = (2 * jj + i) % 4
                            sp.wait_ge(S["w_lo"], it * 8 + (40 + 16 * br + 2 * jj + i + 2))
                            passed()
                            src = w_in[0, :, ds(j * P + gcol * D, P)] if i == 0 else wout[0, :, ds(j * P, P)]
                            sp.dma_start(raw[:, slot], src.rearrange("(k p) n -> p k n", p=P)).then_inc(w_raw[slot], 16)
            with sp.Fori(0, 2) as it:
                for jj in range(4):
                    j = it * 4 + jj
                    sp.wait_ge(S["w_lo"], it * 4 + (72 + jj + 2))
                    passed()
                    sp.dma_start(raw[:, jj], w_o[0, :, ds(j * P, P)].rearrange("(k p) n -> p k n", p=P)).then_inc(w_raw[jj], 16)
            sp.wait_ge(items_used, 72)
            sp.wait_ge(items_used, 41)
            sp.dma_start(ring[:, 0, 0:2048].rearrange("p (k n) -> p k n", k=C), w_src(ws1, 0, FE)).then_inc(w_sh, 16)
            sp.dma_start(ring[:, 0, 2048:4096].rearrange("p (k n) -> p k n", k=C), w_src(ws3, 0, FE)).then_inc(w_sh, 16)
            sp.dma_start(ring[:, 0, 4096:6144].rearrange("p (k n) -> p k n", k=FT), w_src(ws2, 0, D)).then_inc(w_sh, 16)
            sp.wait_ge(out_done, 16 * 6)
            sp.wait_ge(items_used, 80)
            sp.wait_ge(S["x1_dve"], C)
            with sp.Fori(0, E // 4) as g:
                for u in range(4):
                    slot = (u + 1) % 4
                    e = g * 4 + u
                    sp.wait_ge(items_used, g * 4 + (78 + u))
                    for m, w in enumerate((w1, w3)):
                        sp.dma_start(ring[:, slot, 2048 * m:2048 * (m + 1)],
                                     w[0, ds(e, 1), :, :].rearrange("a (p k) n -> p (a k n)", p=P)
                                     ).then_inc(w_ex[slot], 16)
                    sp.dma_start(ring[:, slot, 4096:6144].rearrange("p (k n) -> p k n", k=FT),
                                 w2[0, ds(e, 1), :, :].rearrange("a (k p) n -> p (a k) n", p=P)
                                 ).then_inc(w_ex[slot], 16)
            for i in range(TT):
                n = P if i < TT - 1 else LAST
                sp.wait_ge(S["fin_out"], i + 1)
                dst = y_prompt[0, i * P:(i + 1) * P, :] if i < TT - 1 else y_sample.rearrange("n a d -> (n a) d")
                sp.dma_start(dst, accb[0:n, 2 + i % 2, :]).then_inc(fin_dma[i % 2], 16)
            sp.wait_ge(out_done, 16 * 6)
            sp.wait_ge(fin_dma[0], 16 * 3)
            sp.wait_ge(fin_dma[1], 16 * 2)

        @block.gpsimd
        def _(pool):
            n_step = [0]

            def link(ins):
                n_step[0] += 1
                ins.then_inc(pool_step, 1)
                pool.wait_ge(pool_step, n_step[0])

            for n in ("glu_done", "u_done", "va_done", "acs_done", "abs_done", "ain_done", "ada2_done", "v_done",
                      "m_done", "t_cp", "ex_yd", "ov_yd"):
                pool.sem_inc(S[n], 1)
            pool.sem_inc(S["w_lo"], 5)
            link(pool.memset(ident[:, :], 0.0))
            pool.affine_select(out=ident[:, :], in_=ident[:, :], compare_op=ALU.not_equal, fill=1.0, base=0,
                               pattern=[[-1, P]], channel_multiplier=1).then_inc(consts, 1)
            pool.memset(avg[:, :], 1.0 / D).then_inc(consts, 1)
            pool.memset(eps[:, 0:1], RMS_EPS).then_inc(consts, 1)
            pool.memset(eps[:, 1:2], LN_EPS).then_inc(consts, 1)
            pool.memset(glu[:, 0:KC - 1], 0.0).then_inc(consts, 1)
            pool.memset(up[:, 0:KS - 1], 0.0).then_inc(consts, 1)
            link(pool.memset(firstrow[:, :], 1.0))
            pool.affine_select(out=firstrow[:, :], in_=firstrow[:, :], compare_op=ALU.is_ge, fill=0.0, base=0,
                               pattern=[[0, P]], channel_multiplier=-1).then_inc(consts, 1)
            pool.memset(ones16[:, :], 1.0).then_inc(consts, 1)
            link(pool.memset(upper[:, :], 1.0))
            pool.affine_select(out=upper[:, :], in_=upper[:, :], compare_op=ALU.is_ge, fill=0.0, base=-1,
                               pattern=[[1, P]], channel_multiplier=-1).then_inc(consts, 1)
            for dst, pattern, base, cm in ((iot[:, :], [[1, P]], 0, 0), (tokp1[:, :], [[P, TT]], 1, 1),
                                           (slotid[:, :], [[0, 1]], 0, 1)):
                n = dst.shape[1]
                link(pool.iota(ioti[:, 0:n], pattern=pattern, base=base, channel_multiplier=cm))
                link(pool.tensor_copy(dst, ioti[:, 0:n]))
            link(pool.iota(blocks[:, :], pattern=[[P, TT]], base=0, channel_multiplier=0))
            pool.tensor_scalar(valid[:, :], tokp1[:, :], T + 0.5, None, ALU.is_lt).then_inc(consts, 1)
            pool.wait_ge(S["vecs_act"], 1)

            def split_lo(n, raw_slot, b):
                pool.wait_ge(S["w_hi"], n + 1)
                pool.tensor_tensor(wsplit[:, b, 1], raw[:, raw_slot], wsplit[:, b, 0], ALU.subtract).then_inc(S["w_lo"], 1)

            def gated(j):
                pool.wait_ge(S["v_done"], j + 2)
                pool.wait_ge(S["abs_done"], j + 2)
                pool.tensor_tensor(va[:, ds(j, 1), :].rearrange("p a t -> p (a t)"), vv, abs_, ALU.mult).then_inc(S["va_done"], 1)

            split_lo(0, 0, 0)
            split_lo(1, 1, 1)
            with pool.Fori(0, C // 2) as it:
                for jj in range(2):
                    j = it * 2 + jj
                    for i in range(5):
                        f = 5 * jj + i
                        split_lo(it * 10 + (f + 2), (f + 2) % 5, f % 2)
                        if i == 2:
                            if jj == 1:
                                gated(j - 1)
                            else:
                                with pool.If(it > 0):
                                    pool.wait_ge(S["v_done"], j + 1)
                                    pool.wait_ge(S["abs_done"], j + 1)
                                    pool.tensor_tensor(va_before[:, ds(j, 1), :].rearrange("p a t -> p (a t)"), vv, abs_,
                                                       ALU.mult).then_inc(S["va_done"], 1)
                        if i == 3:
                            pool.wait_ge(S["acs_done"], j + 2)
                            pool.wait_ge(S["ain_done"], j + 2)
                            pool.wait_ge(S["v_done"], j + 1)
                            pool.tensor_tensor(up[:, KS - 1:], acs[:, 0:NP], ain[:, 0:NP], ALU.mult).then_inc(S["pool_chain"], 1)
                            pool.tensor_tensor(us[:, :, KS - 1], acs[:, NP:T], ain[:, NP:T], ALU.mult).then_inc(S["pool_chain"], 1)
                            pool.tensor_copy(us[:, :, 0:KS - 1],
                                             vecs[:, V_SA:V_SA + 128].rearrange("p (n k c) -> p n k c", n=NS, c=C)[:, :, :, ds(j, 1)]
                                             .rearrange("p n k c -> p n (k c)")).then_inc(S["pool_chain"], 1)
                            pool.wait_ge(S["pool_chain"], j * 4 + 3)
                            pool.tensor_copy(tail[:, ds(j, 1), 38:40].rearrange("p a n -> p (a n)"), up[:, NP:NP + 2]).then_inc(S["pool_chain"], 1)
                            pool.wait_ge(S["pool_chain"], j * 4 + 4)
                            pool.tensor_copy(tail[:, ds(j, 1), 40:48].rearrange("p a n -> p (a n)"), us[:, :, KS - 1]).then_inc(S["u_done"], 1)
            gated(C - 1)
            for c in range(C):
                pool.wait_ge(S["va_hi_act"], c + 1)
                pool.tensor_tensor(va_lo[:, c, :], va[:, c, :], vm_hi[:, c, :], ALU.subtract).then_inc(S["va_lo_pool"], 1)
            for n in range(42, 80):
                split_lo(n, n % 4, n % 2)
            pool.wait_ge(hx_out[0], 16 * 3)
            pool.wait_ge(hx_out[1], 16 * 2)
            pool.wait_ge(S["table_dve"], 1)
            ov = pool.alloc_register("ov_pool")
            pool.reg_mov(ov, 0)
            last_row, last_y = pool.alloc_register("last_row"), pool.alloc_register("last_y")
            pool.reg_mov(last_row, T - 1)
            pool.reg_mov(last_y, T * TOPK - 1)

            def wait_here():
                pool.sem_inc(S["pool_passed"], 1)

            def gather(e, u, count):
                pool.tensor_copy(gidx[:, u:u + 1], idxT[:, ds(e, 1)]).then_inc(S["gcopy"], 1)
                pool.wait_ge(S["gcopy"], count)
                wait_here()
                wide = pool.value_load(cnt_i[0:1, 0, ds(e, 1)], min_val=0, max_val=1)
                for m, n in ((1, P), (0, P // 2)):
                    with pool.If(wide > 0) if m else pool.If(wide < 1):
                        pool.indirect_dma_start(out=xg[0:n, u % 2, :], out_offset=None, in_=h2_rows,
                                                in_offset=bass.IndirectOffsetOnAxis(ap=gidx[0:n, u:u + 1], axis=0),
                                                bounds_check=last_row, oob_is_err=False).then_inc(xg_in[u % 2], 16)

            def scatter(after, u):
                pool.wait_ge(S["ex_yd"], after + 1)
                pool.tensor_copy(sidx[:, u:u + 1], rowT[:, ds(after, 1)]).then_inc(S["scopy"], 1)
                pool.wait_ge(S["scopy"], after)
                wait_here()
                wide = pool.value_load(cnt_i[0:1, 2, ds(after, 1)], min_val=0, max_val=1)
                for m, n in ((1, P), (0, P // 2)):
                    with pool.If(wide > 0) if m else pool.If(wide < 1):
                        pool.indirect_dma_start(out=y_rows,
                                                out_offset=bass.IndirectOffsetOnAxis(ap=sidx[0:n, u:u + 1], axis=0),
                                                in_=yb[0:n, u % 2, :], in_offset=None,
                                                bounds_check=last_y, oob_is_err=False).then_inc(y_out[u], 16)

            def gather_further(o, count):
                pool.tensor_copy(gidx[:, 4:5], idxT[:, ds(o + E, 1)]).then_inc(S["ovcopy"], 1)
                pool.wait_ge(S["ovcopy"], count)
                wait_here()
                pool.indirect_dma_start(out=xgo, out_offset=None, in_=h2_rows,
                                        in_offset=bass.IndirectOffsetOnAxis(ap=gidx[:, 4:5], axis=0),
                                        bounds_check=last_row, oob_is_err=False).then_inc(S["ovx"], 16)

            gather(0, 0, 1)
            gather(1, 1, 2)
            pool.wait_ge(items_used, 81)
            link(pool.memset(xgo, 0.0))
            gather_further(0, 1)
            with pool.Fori(0, E // 4) as g:
                for u in range(4):
                    e = g * 4 + u

                    def ahead():
                        pool.wait_ge(S["exT"], e + 1)
                        gather(e + 2, (u + 2) % 4, e + 3)

                    if u < 2:
                        ahead()
                    else:
                        with pool.If(g < E // 4 - 1):
                            ahead()
                    if u == 0:
                        with pool.If(g > 0):
                            scatter(e, 3)
                    else:
                        scatter(e, u - 1)
                    more = pool.value_load(cnt_i[0:1, 1, ds(e, 1)], min_val=0, max_val=4)
                    with pool.If(more > 0):
                        with pool.Fori(0, more) as b:
                            o = pool.snap(ov, min_val=0, max_val=EXTRA - 1)
                            pool.wait_ge(S["ovT"], o + 1)
                            gather_further(o + 1, o * 3 + 2)
                            pool.wait_ge(S["ov_yd"], o + 2)
                            pool.tensor_tensor(sidx[:, 4:5], firsty[:, ds(e, 1)], beyond[:, ds(o + E, 1)], ALU.add).then_inc(S["ovcopy"], 1)
                            pool.wait_ge(S["ovcopy"], o * 3 + 3)
                            pool.tensor_tensor(sidx[:, 5:6], sidx[:, 4:5], blocks[:, ds(b + 1, 1)], ALU.add).then_inc(S["ovcopy"], 1)
                            pool.wait_ge(S["ovcopy"], o * 3 + 4)
                            wait_here()
                            pool.indirect_dma_start(out=y_rows, out_offset=bass.IndirectOffsetOnAxis(ap=sidx[:, 5:6], axis=0),
                                                    in_=ybo, in_offset=None,
                                                    bounds_check=last_y, oob_is_err=False).then_inc(S["ov_scat"], 16)
                            pool.reg_add(ov, ov, 1)
            scatter(E, 3)
            for u in range(4):
                pool.wait_ge(y_out[u], 16 * (E // 4))
            pool.wait_ge(items_used, 81 + E)
            pool.wait_ge(S["late_chain"], 10 * TT)
            for i in range(TT):
                n = P if i < TT - 1 else LAST
                if i >= 2:
                    pool.wait_ge(S["yacc"], i - 1)
                for k in range(TOPK):
                    b = (i % 2) * 8 + k
                    pool.indirect_dma_start(out=yk[0:n, b, :], out_offset=None, in_=y_rows,
                                            in_offset=bass.IndirectOffsetOnAxis(ap=yidx[0:n, i, k:k + 1], axis=0),
                                            bounds_check=last_y, oob_is_err=False).then_inc(yk_in[b], 16)

        @block.scalar
        def _(act):
            def mark(ins, name):
                ins.then_inc(S[name], 1)

            act.dma_start(c_tok[0:1, :], c_prompt).then_inc(crow_in, 16)
            act.dma_start(c_tok[1:NSEQ, :], c_sample).then_inc(crow_in, 16)
            for base, n, t in ((V_ADA, 48, b_ada.rearrange("l (r c) -> (l r) c", c=P)),
                               (V_PRE1, C, g_pre1.rearrange("l (r c) -> (l r) c", c=P)),
                               (V_POST1, C, g_post1.rearrange("l (r c) -> (l r) c", c=P)),
                               (V_PRE2, C, g_pre2.rearrange("l (r c) -> (l r) c", c=P)),
                               (V_SC, C * KS, w_sconv.rearrange("l k (r c) -> (l k r) c", c=P)),
                               (V_BC, C, b_cconv.rearrange("l (r c) -> (l r) c", c=P)),
                               (V_LG, C, ln_g.rearrange("l (r c) -> (l r) c", c=P)),
                               (V_LB, C, ln_b.rearrange("l (r c) -> (l r) c", c=P)),
                               (V_OB, C, b_out_b.rearrange("l (r c) -> (l r) c", c=P))):
                act.dma_start(vrow[base:base + n, :], t).then_inc(vrow_in, 16)
            act.dma_start(p2row, g_post2.rearrange("l (r c) -> (l r) c", c=P)).then_inc(vrow_in, 16)
            wcr = w_cconv.rearrange("l k (r c) -> (l k r) c", c=P)
            for a in range(2):
                act.dma_start(wcrow[:, a, :], wcr[a * 124:(a + 1) * 124, :]).then_inc(vrow_in, 16)
            act.dma_start(sarow, state_sconv.rearrange("l n k (r c) -> (l n k r) c", c=P)).then_inc(vrow_in, 16)
            act.dma_start(x_stok, x_sample.rearrange("n a d -> (n a) d")).then_inc(x_in, 16)
            act.dma_start(sbrow, state_cconv.rearrange("l n k d -> (l n k) d").rearrange("(a r) d -> r a d", a=2)).then_inc(st_in, 16)
            act.dma_start(ebias[:, :], e_bias.to_broadcast([P, E])).then_inc(late_in, 16)
            act.wait_ge(crow_in, 32)
            mark(act.activation(c_tok, c_tok, ACT.Silu), "csilu_act")
            act.wait_ge(S["vecs_pe"], 1)
            mark(act.activation(vecs[:, 0:NV], ps[:, 6, 0:NV], ACT.Copy), "vecs_act")
            act.wait_ge(S["cT_pe"], 1)
            mark(act.activation(scT[:, :, :].rearrange("p c s -> p (c s)"), ps[:, 7, 0:C * NSEQ], ACT.Copy), "cT_act")
            for c in range(C):
                act.wait_ge(S["xT_pe"], c + 1)
                mark(act.activation(xT[:, c, 0:NP], ps[:, c % 4, 0:NP], ACT.Copy), "xT_act")
            act.wait_ge(S["xs_pe"], 1)
            mark(act.activation(xT[:, :, NP:T], ps[:, 5, 0:C * NS].rearrange("p (c s) -> p c s", c=C), ACT.Copy), "xs_act")
            act.wait_ge(S["xs_act"], 1)
            for c in range(C):
                mark(act.activation(hT[:, c, :], xT[:, c, :], ACT.Square), "xsq_act")
            act.wait_ge(S["xstat_pe"], 1)
            for h, (a, b) in enumerate(half):
                mark(act.activation(rs[:, a:b], ps[:, 6 + h, 0:HT], ACT.Sqrt, bias=eps[:, 0:1]), "xrt_act")
            for q in range(4):
                act.wait_ge(S["ada_row"], q + 1)
                mark(act.activation(arow[:, q * 512:(q + 1) * 512], ps[0:NSEQ, q, :], ACT.Copy), "arow_done")

            def split_hi(raw_slot, b, loads):
                act.wait_ge(w_raw[raw_slot], loads)
                act.activation(wsplit[:, b, 0], raw[:, raw_slot], ACT.Copy).then_inc(S["w_hi"], 1)

            split_hi(0, 0, 16)
            split_hi(1, 1, 16)
            act.wait_ge(S["s1_dve"], 1)
            for c in range(C):
                act.wait_ge(S["xn_dve"], c + 1)
                for dst in (h_hi, hT):
                    ins = act.activation(dst[:, c, 0:NP], hT[:, c, 0:NP], ACT.Identity, bias=ada[:, 0, c, 0:1],
                                         scale=s1[:, c, 0:1])
                mark(ins, "h_act")
            W2 = NS * (KC - 1)
            for q in range(4):
                act.wait_ge(S["stB_pe"], q + 1)
                mark(act.activation(stB[:, 2 * q:2 * q + 2, :].rearrange("p c n -> p (c n)"), ps[:, 4 + q, 0:2 * W2],
                                    ACT.Copy), "stB_act")
            act.dma_start(new_cconv_s[0, :, 0:KC - 2, :], state_cconv[0, :, 1:KC - 1, :]).then_inc(out_done, 16)
            act.dma_start(new_sconv_s[0, :, 0:KS - 2, :], state_sconv[0, :, 1:KS - 1, :]).then_inc(out_done, 16)
            with act.Fori(0, C // 2) as it:
                for jj in range(2):
                    j = it * 2 + jj
                    for i in range(5):
                        f = 5 * jj + i
                        act.wait_ge(items_used, it * 10 + (f + 1))
                        split_hi((f + 2) % 5, f % 2, it * 32 + (16 * ((f + 2) // 5) + 16))
                        if i == 0:
                            act.wait_ge(S["glu_done"], j + 1)
                            for h, (a, b) in enumerate(half):
                                ins = act.activation(sg[:, a:b], ps[:, h, 0:HT], ACT.Sigmoid)
                            ins.then_inc(S["sg_done"], 1)
                        elif i == 2:
                            act.wait_ge(S["u_done"], j + 1)
                            for h, (a, b) in enumerate(half):
                                ins = act.activation(ain[:, a:b], ps[:, 4 + h, 0:HT], ACT.Copy)
                            ins.then_inc(S["ain_done"], 1)
                        elif i == 3:
                            for h, (a, b) in enumerate(half):
                                ins = act.activation(acs[:, a:b], ps[:, h, 0:HT], ACT.Copy)
                            ins.then_inc(S["acs_done"], 1)
                            act.wait_ge(S["ada_row"], j + 5)
                            act.wait_ge(S["ada_T"], j + 1)
                            act.activation(arow[:, 0:512], ps[0:NSEQ, 6, :], ACT.Copy).then_inc(S["arow_done"], 1)
                        elif i == 4:
                            act.wait_ge(S["va_done"], j + 1)
                            for h, (a, b) in enumerate(half):
                                ins = act.activation(abs_[:, a:b], ps[:, 2 + h, 0:HT], ACT.Copy)
                            ins.then_inc(S["abs_done"], 1)
            act.wait_ge(S["va_done"], C + 1)
            act.dma_start(wr, w_router[0].rearrange("(k p) e -> p k e", p=P)).then_inc(late_in, 16)
            for c in range(C):
                mark(act.activation(vm_hi[:, c, :], va[:, c, :], ACT.Copy), "va_hi_act")
            act.wait_ge(S["tails_pe"], 1)
            mark(act.activation(tailrows[:, :], ps[0:48, 6:8, :].rearrange("p b n -> p (b n)"), ACT.Copy), "tailrows_act")
            act.wait_ge(S["tailrows_act"], 1)
            act.dma_start(new_cconv_p[0, 0], tailrows[0:KC - 1, :]).then_inc(out_done, 16)
            act.dma_start(new_cconv_s[0, :, KC - 2, :], tailrows[KC - 1:KC - 1 + NS, :]).then_inc(out_done, 16)
            act.dma_start(new_sconv_p[0, 0], tailrows[38:40, :]).then_inc(out_done, 16)
            act.dma_start(new_sconv_s[0, :, KS - 2, :], tailrows[40:48, :]).then_inc(out_done, 16)
            act.wait_ge(S["g2rows_pe"], 1)
            mark(act.activation(grow, ps[0:NSEQ, 4:6, :].rearrange("p b n -> p (b n)"), ACT.Copy), "growc_act")

            def next_unit(n, raw_slot, b, loads):
                act.wait_ge(items_used, n + 1)
                split_hi(raw_slot, b, loads)

            def gate_sig(it, jj, br):
                n = it * 8 + (40 + 16 * br + 2 * jj)
                next_unit(n, (2 * jj + 2) % 4, 0, it * 32 + (16 * (8 + 4 * br) + 16 * ((2 * jj + 2) // 4) + 16))
                act.wait_ge(S["m_done"], it * 4 + (8 * br + jj + 1))
                for h, (a, b) in enumerate(half):
                    ins = act.activation(sg[:, a:b], ps[:, h, 0:HT], ACT.Sigmoid)
                ins.then_inc(S["g_done"], 1)
                next_unit(n + 1, (2 * jj + 3) % 4, 1, it * 32 + (16 * (8 + 4 * br) + 16 * ((2 * jj + 3) // 4) + 16))

            for jj in range(4):
                gate_sig(0, jj, 0)
            for h in range(2):
                act.wait_ge(S["cen_dve"], h + 1)
            for c in range(C):
                if c >= 4:
                    act.wait_ge(S["stat_mm"], c - 3)
                act.activation(scr[:, c % 4, :], cv[:, c, :], ACT.Square).then_inc(S["sqd"], 1)
            act.wait_ge(S["stat_mm"], 8)
            for h, (a, b) in enumerate(half):
                mark(act.activation(rs[:, a:b], ps[:, 6 + h, 0:HT], ACT.Sqrt, bias=eps[:, 1:2]), "lrt_act")
            for jj in range(4):
                gate_sig(1, jj, 0)
                for c in range(2 * jj, 2 * jj + 2):
                    act.wait_ge(S["ln_dve"], c + 1)
                    for dst in (s_hi, cv):
                        ins = act.activation(dst[:, c, :], cv[:, c, :], ACT.Silu, bias=vecs[:, V_LB + c:V_LB + c + 1],
                                             scale=vecs[:, V_LG + c:V_LG + c + 1])
                    mark(ins, "s_act")
            with act.Fori(0, 2) as it:
                for jj in range(4):
                    gate_sig(it, jj, 1)
            for j in range(C):
                q = 2 * (j % 2)
                act.wait_ge(items_used, 73 + j)
                if j < C - 2:
                    split_hi((j + 2) % 4, j % 2, 16 * (16 + (j + 2) // 4 + 1))
                for h, (a, b) in enumerate(half):
                    ins = act.activation(tT[:, j, a:b], ps[:, q + h, 0:HT], ACT.Copy)
                ins.then_inc(S["t_cp"], 1)
                act.wait_ge(S["stat_mm"], 8 + j - 3)
                act.wait_ge(S["t_cp"], j + 2)
                act.activation(scr[:, j % 4, :], tT[:, j, :], ACT.Square).then_inc(S["sqd"], 1)
            act.wait_ge(S["stat_mm"], 16)
            for h, (a, b) in enumerate(half):
                mark(act.activation(rs[:, a:b], ps[:, 6 + h, 0:HT], ACT.Sqrt, bias=eps[:, 0:1]), "trt_act")
            for j in range(C):
                act.wait_ge(S["x1_dve"], j + 1)
                act.wait_ge(S["stat_mm"], 16 + j - 3)
                act.activation(scr[:, j % 4, :], xT[:, j, :], ACT.Square).then_inc(S["sqd"], 1)
            act.wait_ge(S["stat_mm"], 24)
            for h, (a, b) in enumerate(half):
                mark(act.activation(rs[:, a:b], ps[:, 4 + h, 0:HT], ACT.Sqrt, bias=eps[:, 0:1]), "x1rt_act")
            for c in range(C):
                act.wait_ge(S["x1n_dve"], c + 1)
                mark(act.activation(hT[:, c, 0:NP], hT[:, c, 0:NP], ACT.Identity, bias=ada[:, 3, c, 0:1],
                                    scale=s1[:, c, 0:1]), "h2_act")
            for i in range(TT):
                n = P if i < TT - 1 else LAST
                act.wait_ge(S["x1t_T"], i + 1)
                act.activation(x1tok[0:n, i, :], ps[0:n, 0:2, :].rearrange("p b n -> p (b n)"), ACT.Copy).then_inc(S["x1t_done"], 1)
            act.wait_ge(S["logits_pe"], 1)
            act.wait_ge(S["score0_dve"], 1)
            mark(act.activation(score[:, 0:TT - 1, :], ps[:, 4, 0:(TT - 1) * E].rearrange("p (i e) -> p i e", e=E), ACT.Sigmoid), "score_act")
            mark(act.activation(score[0:LAST, TT - 1, :], ps[0:LAST, 4, (TT - 1) * E:TT * E], ACT.Sigmoid), "score_s_act")
            for i in range(TT):
                n = P if i < TT - 1 else LAST
                act.wait_ge(S["hx_T"], i + 1)
                if i >= 2:
                    act.wait_ge(hx_out[i % 2], 16 * (i // 2))
                act.activation(xg[0:n, i % 2, :], ps[0:n, 2:4, :].rearrange("p b n -> p (b n)"), ACT.Copy).then_inc(S["hx_done"], 1)
                act.wait_ge(S["hx_done"], i + 1)
                act.dma_start(h2_rows[i * P:i * P + n, :], xg[0:n, i % 2, :]).then_inc(hx_out[i % 2], 16)
            for f in range(FT):
                act.wait_ge(S["sh_mm"], f + 1)
                if f == 1:
                    act.wait_ge(S["sh_act"], 1)
                for h, (a, b) in enumerate(half):
                    ins = act.activation(sg[:, a:b], ps[:, h, 0:HT], ACT.Silu)
                ins.then_inc(S["g_done"], 1)
            for i in range(TT):
                n = P if i < TT - 1 else LAST
                if i < TT - 1:
                    act.wait_ge(S["sh_o"], i + 1)
                else:
                    act.wait_ge(items_used, 81)
                act.activation(shared[0:n, i, :], ps[0:n, 2 * (i % 2):2 * (i % 2) + 2, :].rearrange("p b n -> p (b n)"),
                               ACT.Copy).then_inc(S["sh_done"], 1)
            act.wait_ge(S["exT"], 1)
            act.activation(flat(xgT), ps[:, 0:2, :].rearrange("p b n -> p (b n)"), ACT.Copy).then_inc(S["exT_done"], 1)
            ov = act.alloc_register("ov_act")
            act.reg_mov(ov, 0)
            with act.Fori(0, E // 4) as g:
                for u in range(4):
                    e = g * 4 + u
                    act.wait_ge(S["ex13"], e + 1)
                    act.activation(esil[:, u % 2].rearrange("p f s -> p (f s)"), ps[:, 2 + u % 2, 0:256], ACT.Silu).then_inc(S["ex_sil"], 1)

                    def next_rows():
                        act.wait_ge(S["exT"], e + 2)
                        act.activation(flat(xgT), ps[:, 0:2, :].rearrange("p b n -> p (b n)"), ACT.Copy).then_inc(S["exT_done"], 1)

                    if u < 3:
                        next_rows()
                    else:
                        with act.If(g < E // 4 - 1):
                            next_rows()
                    more = act.value_load(cnt_i[0:1, 1, ds(e, 1)], min_val=0, max_val=4)
                    with act.If(more > 0):
                        with act.Fori(0, more) as b:
                            o = act.snap(ov, min_val=0, max_val=EXTRA - 1)
                            act.wait_ge(S["ovT"], o + 1)
                            act.activation(flat(xgTo), ps[:, 6:8, :].rearrange("p b n -> p (b n)"), ACT.Copy).then_inc(S["ovT_done"], 1)
                            act.wait_ge(S["ov13"], o + 1)
                            act.activation(flat(esilo), ps[:, 3 - u % 2, 0:256], ACT.Silu).then_inc(S["ov_sil"], 1)
                            act.reg_add(ov, ov, 1)
            act.wait_ge(S["g2_pe"], 1)
            mark(act.activation(G2, ps[:, 0:2, :].rearrange("p b n -> p (b n)"), ACT.Copy), "G2_act")
            mark(act.activation(G2s, ps[0:NS, 2:4, :].rearrange("p b n -> p (b n)"), ACT.Copy), "G2_act")
            for i in range(TT):
                n = P if i < TT - 1 else LAST
                act.wait_ge(S["yacc"], i + 1)
                act.activation(accb[0:n, 2 + i % 2, :], accb[0:n, i % 2, :], ACT.Square,
                               accum_out=red[0:n, 1:2]).then_inc(S["fin_sq"], 1)
                act.wait_ge(S["fin_sq"], i + 1)
                act.activation(red[0:n, 2:3], red[0:n, 1:2], ACT.Sqrt, bias=eps[0:n, 0:1], scale=1.0 / D).then_inc(S["fin_rt"], 1)

        @block.vector
        def _(dve):
            counts = {}

            def link(ins, name=None, wait=True):
                key = name or "dve_step"
                counts[key] = counts.get(key, 0) + 1
                ins.then_inc(S[name] if name else dve_step, 1)
                if wait:
                    dve.wait_ge(S[name] if name else dve_step, counts[key])

            tt, ts, stt = dve.tensor_tensor, dve.tensor_scalar, dve.scalar_tensor_tensor

            def bc(ap, n):
                return ap.unsqueeze(len(ap.shape)).to_broadcast(list(ap.shape) + [n])

            dve.wait_ge(S["vecs_act"], 1)
            dve.wait_ge(S["ada_T"], 1)
            link(tt(ada[:, 0:2, :, :].rearrange("p a c s -> p (a c) s"),
                    ps[:, 4, 0:2 * C * NSEQ].rearrange("p (a s) -> p a s", s=NSEQ), bc(vecs[:, V_ADA:V_ADA + 2 * C], NSEQ), ALU.add))
            link(stt(out=s1[:, :, :], in0=ada[:, 1], scalar=1.0, in1=bc(vecs[:, V_PRE1:V_PRE1 + C], NSEQ),
                     op0=ALU.add, op1=ALU.mult), "s1_dve")
            dve.wait_ge(S["xrt_act"], 2)
            link(dve.reciprocal(rs[:, :], rs[:, :]))
            for c in range(C):
                link(tt(hT[:, c, :], xT[:, c, :], rs[:, :], ALU.mult), "xn_dve", wait=False)
            dve.wait_ge(S["xn_dve"], C)
            link(tt(smp[:, :, :], hT[:, :, NP:T], s1[:, :, 1:NSEQ], ALU.mult))
            tt(h_hi[:, :, NP:T], smp[:, :, :], ada[:, 0, :, 1:NSEQ], ALU.add).then_inc(S["h_s_dve"], 1)
            tt(hT[:, :, NP:T], smp[:, :, :], ada[:, 0, :, 1:NSEQ], ALU.add).then_inc(S["h_s_dve"], 1)
            dve.wait_ge(S["h_s_dve"], 2)
            for c in range(C):
                dve.wait_ge(S["h_act"], c + 1)
                tt(h_lo[:, c, :], hT[:, c, :], h_hi[:, c, :], ALU.subtract).then_inc(S["h_lo_dve"], 1)
            dve.wait_ge(S["stB_act"], 4)
            dve.wait_ge(consts, 10)
            KA = 43
            with dve.Fori(0, C // 2) as it:
                for jj in range(2):
                    j = it * 2 + jj
                    n = [0]

                    def chain(ins, wait=True):
                        n[0] += 1
                        ins.then_inc(S["pa_chain"], 1)
                        if wait:
                            dve.wait_ge(S["pa_chain"], j * KA + n[0])

                    def at(ap3):
                        return ap3.rearrange("p a n -> p (a n)")

                    dve.wait_ge(items_used, it * 10 + (5 * jj + 2))
                    dve.wait_ge(S["sg_done"], j + 1)
                    chain(tt(glu[:, KC - 1:KC - 1 + HT], ps[:, 2, 0:HT], sg[:, 0:HT], ALU.mult), wait=False)
                    chain(tt(glu[:, KC - 1 + HT:KC - 1 + NP], ps[:, 3, 0:NP - HT], sg[:, HT:NP], ALU.mult), wait=False)
                    chain(dve.tensor_copy(glus[:, :, 0:KC - 1],
                                          at(stB[:, ds(j, 1), :]).rearrange("p (n k) -> p n k", n=NS)), wait=False)
                    chain(tt(glus[:, :, KC - 1], ps[:, 3, NP - HT:HT], sg[:, NP:T], ALU.mult))
                    chain(dve.tensor_copy(at(tail[:, ds(j, 1), 0:KC - 1]), glu[:, NP:NP + KC - 1]), wait=False)
                    dve.tensor_copy(at(tail[:, ds(j, 1), KC - 1:KC - 1 + NS]), glus[:, :, KC - 1]).then_inc(S["glu_done"], 1)
                    dve.wait_ge(S["glu_done"], j + 2)
                    acc = at(cv[:, ds(j, 1), 0:NP])
                    chain(ts(acc, glu[:, 0:NP], vecs[:, ds(j + V_WC, 1)], vecs[:, ds(j + V_BC, 1)], ALU.mult, ALU.add))
                    for k in range(1, KC):
                        chain(stt(out=acc, in0=glu[:, k:k + NP], scalar=vecs[:, ds(j + (V_WC + 8 * k), 1)], in1=acc,
                                  op0=ALU.mult, op1=ALU.add))
                    wk = vecs[:, V_WC:V_WC + 8 * KC].rearrange("p (k c) -> p c k", c=C)[:, ds(j, 1), :]
                    chain(tt(tmps[:, :, :], glus[:, :, :], wk.to_broadcast([P, NS, KC]), ALU.mult))
                    chain(dve.tensor_reduce(smp[:, 0, :], tmps[:, :, :], AX.X, ALU.add))
                    chain(ts(at(cv[:, ds(j, 1), NP:T]), smp[:, 0, :], vecs[:, ds(j + V_BC, 1)], None, ALU.add), wait=False)
                    dve.wait_ge(S["u_done"], j + 2)
                    dve.wait_ge(S["va_done"], j + 1)
                    for k in range(KS):
                        w = vecs[:, ds(j + (V_SC + 8 * k), 1)]
                        if k == 0:
                            chain(ts(vv[:, 0:NP], up[:, 0:NP], w, None, ALU.mult))
                        else:
                            chain(stt(out=vv[:, 0:NP], in0=up[:, k:k + NP], scalar=w, in1=vv[:, 0:NP], op0=ALU.mult, op1=ALU.add))
                    ws = vecs[:, V_SC:V_SC + 8 * KS].rearrange("p (k c) -> p c k", c=C)[:, ds(j, 1), :]
                    chain(tt(tmps[:, :, 0:KS], us[:, :, :], ws.to_broadcast([P, NS, KS]), ALU.mult))
                    dve.tensor_reduce(vv[:, NP:T], tmps[:, :, 0:KS], AX.X, ALU.add).then_inc(S["v_done"], 1)
                    dve.wait_ge(S["ada_T"], j + 2)
                    tt(ada4[:, ds(j, 1), :].rearrange("p a (r s) -> p (a r) s", s=NSEQ),
                       ps[:, 7, 0:4 * NSEQ].rearrange("p (r s) -> p r s", s=NSEQ),
                       bc(vecs[:, V_ADA + 2 * C:V_ADA + 6 * C].rearrange("p (j r) -> p j r", r=4)[:, ds(j, 1), :]
                          .rearrange("p j r -> p (j r)"), NSEQ), ALU.add).then_inc(S["ada2_done"], 1)
                    assert n[0] == KA, n[0]
            dve.wait_ge(S["ada2_done"], C + 1)
            tt(ada[:, 5], ada[:, 5], bc(vecs[:, V_POST2:V_POST2 + C], NSEQ), ALU.mult).then_inc(S["p2_dve"], 1)
            dve.wait_ge(S["mean_pe"], 1)
            for h, (a, b) in enumerate(half):
                link(tt(cv[:, :, a:b], cv[:, :, a:b], ps[:, 4 + h, 0:HT].unsqueeze(1).to_broadcast([P, C, HT]), ALU.subtract), "cen_dve")

            def merge_a(j):
                dve.wait_ge(items_used, 42 + 2 * j)
                dve.wait_ge(S["g_done"], j + 1)
                for h, (a, b) in enumerate(half):
                    ins = tt(mT[:, j, a:b], sg[:, a:b], ps[:, 2 + h, 0:HT], ALU.mult)
                ins.then_inc(S["m_done"], 1)

            for j in range(4):
                merge_a(j)
            dve.wait_ge(S["lrt_act"], 2)
            link(dve.reciprocal(rs[:, :], rs[:, :]))
            for j in range(4, C):
                for c in range(2 * (j - 4), 2 * (j - 4) + 2):
                    link(tt(cv[:, c, :], cv[:, c, :], rs[:, :], ALU.mult), "ln_dve", wait=False)
                merge_a(j)
                for c in range(2 * (j - 4), 2 * (j - 4) + 2):
                    dve.wait_ge(S["s_act"], c + 1)
                    tt(cv_lo[:, c, :], cv[:, c, :], s_hi[:, c, :], ALU.subtract).then_inc(S["cv_lo_dve"], 1)
            with dve.Fori(0, 2) as it:
                for jj in range(4):
                    j = it * 4 + jj
                    dve.wait_ge(items_used, it * 8 + (58 + 2 * jj))
                    dve.wait_ge(S["g_done"], j + 9)
                    for h, (a, b) in enumerate(half):
                        stt(out=sg[:, a:b], in0=ps[:, 2 + h, 0:HT], scalar=vecs[:, ds(j + V_OB, 1)], in1=sg[:, a:b],
                            op0=ALU.add, op1=ALU.mult).then_inc(S["m_chain"], 1)
                    dve.wait_ge(S["m_chain"], j * 2 + 2)
                    mj = mT[:, ds(j, 1), :].rearrange("p a t -> p (a t)")
                    m_hi = vm_hi[:, ds(j, 1), :].rearrange("p a t -> p (a t)")
                    tt(m_hi, mj, sg[:, :], ALU.add).then_inc(S["m_split"], 1)
                    tt(mj, mj, sg[:, :], ALU.add).then_inc(S["m_done"], 1)
                    dve.wait_ge(S["m_done"], j + 10)
                    tt(m_lo[:, ds(j, 1), :].rearrange("p a t -> p (a t)"), mj, m_hi, ALU.subtract).then_inc(S["m_lo_dve"], 1)
            link(tt(ada[:, 2], ada[:, 2], bc(vecs[:, V_POST1:V_POST1 + C], NSEQ), ALU.mult))
            link(stt(out=s1[:, :, :], in0=ada[:, 4], scalar=1.0, in1=bc(vecs[:, V_PRE2:V_PRE2 + C], NSEQ),
                     op0=ALU.add, op1=ALU.mult))
            dve.wait_ge(S["trt_act"], 2)
            link(dve.reciprocal(rs[:, :], rs[:, :]))
            for c in range(C):
                link(tt(tT[:, c, :], tT[:, c, :], rs[:, :], ALU.mult))
                link(tt(smp[:, c, :], tT[:, c, NP:T], ada[:, 2, c, 1:NSEQ], ALU.mult), wait=False)
                link(stt(out=xT[:, c, 0:NP], in0=tT[:, c, 0:NP], scalar=ada[:, 2, c, 0:1], in1=xT[:, c, 0:NP],
                         op0=ALU.mult, op1=ALU.add))
                link(tt(xT[:, c, NP:T], xT[:, c, NP:T], smp[:, c, :], ALU.add), "x1_dve", wait=False)
            dve.wait_ge(S["x1rt_act"], 2)
            link(dve.reciprocal(rs[:, :], rs[:, :]))
            for c in range(C):
                link(tt(hT[:, c, :], xT[:, c, :], rs[:, :], ALU.mult), "x1n_dve", wait=False)
            dve.wait_ge(S["x1n_dve"], C)
            link(tt(smp[:, :, :], hT[:, :, NP:T], s1[:, :, 1:NSEQ], ALU.mult))
            link(tt(hT[:, :, NP:T], smp[:, :, :], ada[:, 3, :, 1:NSEQ], ALU.add), "h2_s_dve")
            dve.wait_ge(S["x1t_T"], TT)
            link(dve.memset(score[:, TT - 1, :], 0.5), "score0_dve")
            dve.wait_ge(S["score_s_act"], 1)
            dve.wait_ge(late_in, 32)
            link(tt(sel, score, ebias[:, :].unsqueeze(1).to_broadcast([P, TT, E]), ALU.add))
            gs, g8, gi, gm, gneg, t8, wk8, wsum, eif, rowk = (s8(n) for n in range(10))
            gi_u = s8(10).bitcast(U32)
            row_i = s8(11).bitcast(I32)
            top = eq
            for i in range(TT):
                for q in range(NG):
                    link(dve.max(out=top[:, q, 0:8], in_=sel[:, i, q * EG:(q + 1) * EG]), wait=(q == NG - 1))
                link(tt(gs[:, i, :], top[:, :, 0], top[:, :, 1], ALU.add))
            for i in range(TT):
                link(dve.max(out=g8[:, i, :], in_=gs[:, i, :]))
                link(dve.max_index(out=gi_u[:, i, :], in_max=g8[:, i, :], in_values=gs[:, i, :]))
            link(dve.tensor_copy(gi, gi_u))
            for i in range(TT):
                em = eq[:, 0:TOPG, 0:NG]
                link(tt(em, iot[:, 0:NG].unsqueeze(1).to_broadcast([P, TOPG, NG]), bc(gi[:, i, 0:TOPG], NG), ALU.is_equal))
                link(dve.tensor_reduce(gm[:, i, :], em.rearrange("p j g -> p g j"), AX.X, ALU.add))
            link(ts(gneg, gm, -NEG, NEG, ALU.mult, ALU.add))
            for i in range(TT):
                sv, mv = (t[:, i, :].rearrange("p (g q) -> p g q", g=NG) for t in (sel, selm))
                link(tt(mv, sv, bc(gm[:, i, :], EG), ALU.mult))
                link(tt(mv, mv, bc(gneg[:, i, :], EG), ALU.add))
            for i in range(TT):
                link(dve.max(out=t8[:, i, :], in_=selm[:, i, :]))
                link(dve.max_index(out=gi_u[:, i, :], in_max=t8[:, i, :], in_values=selm[:, i, :]), wait=False)
                link(dve.match_replace(out=repl[:, i, :], in_to_replace=t8[:, i, :], in_values=selm[:, i, :], imm_value=2 * NEG))
            link(dve.tensor_copy(eif, gi_u), wait=False)
            link(ts(repl, repl, 1.5 * NEG, None, ALU.is_le))
            link(tt(mask16[:, :, :], repl, bc(valid[:, :], E), ALU.mult), "mask_dve")
            def shared_act(f):
                dve.wait_ge(S["g_done"], 17 + f)
                for h, (a, b) in enumerate(half):
                    ins = tt(scr[:, 2 + f, a:b], sg[:, a:b], ps[:, 2 + h, 0:HT], ALU.mult)
                ins.then_inc(S["sh_act"], 1)

            shared_act(0)
            dve.wait_ge(S["rank_pe"], 1)
            link(dve.tensor_copy(rank, ps[:, 5, 0:RE].rearrange("p (i e) -> p i e", i=TT)))
            cnt, nov, ovb, wide, one64, ybase = (e64[:, n, :] for n in range(6))
            link(dve.tensor_copy(cnt, ps[:, 6, 0:E]))
            link(ts(nov, cnt, P + 0.5, None, ALU.is_gt))
            for m in range(2, TT):
                link(stt(out=nov, in0=cnt, scalar=m * P + 0.5, in1=nov, op0=ALU.is_gt, op1=ALU.add))
            link(ts(wide, cnt, P // 2 + 0.5, None, ALU.is_gt))
            link(dve.memset(one64, 1.0))
            link(dve.tensor_tensor_scan(out=ovb, data0=one64, data1=nov, initial=0.0, op0=ALU.mult, op1=ALU.add))
            link(tt(ovb, ovb, nov, ALU.subtract))
            link(dve.tensor_tensor_scan(out=ybase, data0=one64, data1=cnt, initial=0.0, op0=ALU.mult, op1=ALU.add))
            link(tt(ybase, ybase, cnt, ALU.subtract))
            link(dve.tensor_copy(cnt_i[0:1, 0, 0:E], wide[0:1, :]), wait=False)
            link(dve.tensor_copy(cnt_i[0:1, 2, 1:E + 1], wide[0:1, :]), wait=False)
            link(dve.tensor_copy(cnt_i[0:1, 1, 0:E], nov[0:1, :]))
            link(stt(out=ovb, in0=ovb, scalar=float(E - 1), in1=iot[:, 0:E], op0=ALU.add, op1=ALU.subtract))
            link(ts(blk, rank, P - 0.5, None, ALU.is_gt))
            for m in range(2, TT):
                link(stt(out=blk, in0=rank, scalar=m * P - 0.5, in1=blk, op0=ALU.is_gt, op1=ALU.add))
            link(tt(tmpr, blk, ovb.unsqueeze(1).to_broadcast([P, TT, E]), ALU.add))
            link(stt(out=tmpr, in0=blk, scalar=0.5, in1=tmpr, op0=ALU.is_gt, op1=ALU.mult))
            link(tt(tmpr, tmpr, iot[:, 0:E].unsqueeze(1).to_broadcast([P, TT, E]), ALU.add))
            link(stt(out=row, in0=blk, scalar=-float(P), in1=rank, op0=ALU.mult, op1=ALU.add))
            link(stt(out=row, in0=tmpr, scalar=float(P), in1=row, op0=ALU.mult, op1=ALU.add))
            shared_act(1)
            for i in range(TT):
                link(tt(eq, iot[:, 0:E].unsqueeze(1).to_broadcast([P, TOPK, E]), bc(eif[:, i, :], E), ALU.is_equal))
                link(tt(eqm, eq, row[:, i, :].unsqueeze(1).to_broadcast([P, TOPK, E]), ALU.mult))
                link(dve.tensor_reduce(rowk[:, i, :], eqm, AX.X, ALU.add))
            link(ts(gs[:, :, 0], valid[:, :], -float(P * P), float(P * P), ALU.mult, ALU.add))
            link(tt(rowk, rowk, bc(valid[:, :], TOPK), ALU.mult))
            link(tt(rowk, rowk, bc(gs[:, :, 0], TOPK), ALU.add))
            place = s8(12).bitcast(I32)
            link(dve.tensor_copy(place, rowk))
            link(ts(row_i, place, P - 1, None, ALU.bitwise_and))
            link(dve.tensor_copy(g8, row_i))
            link(ts(row_i, place, 7, None, ALU.logical_shift_right))
            link(dve.tensor_copy(gi, row_i))
            for i in range(TT):
                for k in range(TOPK):
                    n = i * TOPK + k
                    if n >= 4:
                        dve.wait_ge(S["idx_mm"], n - 3)
                    ts(oneA[:, n % 4, :], iot[:, :], g8[:, i, k:k + 1], None, ALU.is_equal).then_inc(S["idx_ab"], 1)
                    ts(oneB[:, n % 4, :], iot[:, 0:JOBS], gi[:, i, k:k + 1], tokp1[:, i:i + 1], ALU.is_equal, ALU.mult).then_inc(S["idx_ab"], 1)
            dve.wait_ge(S["idx_mm"], TT * TOPK)
            tab, tb2 = eq.rearrange("p k e -> p (k e)")[:, 0:JOBS], eq.rearrange("p k e -> p (k e)")[:, 128:128 + JOBS]
            link(ts(tab, ps[:, 7, 0:JOBS], -1.0, None, ALU.add))
            link(dve.tensor_copy(idxT[:, :], tab))
            link(ts(tab, tab, -0.5, 1e6, ALU.is_lt, ALU.mult))
            link(dve.tensor_copy(beyond[:, :], tab))
            link(ts(tb2[:, 0:E], ybase, slotid[:, 0:1], None, ALU.add))
            link(dve.tensor_copy(firsty[:, :], tb2[:, 0:E]))
            link(tt(tb2[:, 0:E], tab[:, 0:E], tb2[:, 0:E], ALU.add))
            link(dve.tensor_copy(rowT[:, 1:], tb2[:, 0:E]), "table_dve")
            link(tt(tmpr, rank, ybase.unsqueeze(1).to_broadcast([P, TT, E]), ALU.add))
            dve.wait_ge(S["sh_done"], TT)
            dve.memset(ps[:, 2:4, :], 0.0).then_inc(S["sh_act"], 1)
            LA = 10
            ov, tile_no = dve.alloc_register("ov_dve"), dve.alloc_register("tile_no")
            dve.reg_mov(ov, 0)
            dve.reg_mov(tile_no, 0)

            def token_tile(i, u):
                n = [(0, 3, 7, 9)[u]]
                eight = wsum[:, 1, :]

                def chain(ins, wait=True):
                    n[0] += 1
                    ins.then_inc(S["late_chain"], 1)
                    if wait:
                        dve.wait_ge(S["late_chain"], i * LA + n[0])

                def at(ap):
                    return ap[:, ds(i, 1), :].rearrange("p a n -> p (a n)")

                def of_all(ap):
                    return at(ap).unsqueeze(1).to_broadcast([P, TOPK, E])

                if u > 0:
                    dve.wait_ge(S["late_chain"], i * LA + n[0])
                if u == 0:
                    chain(tt(eq, iot[:, 0:E].unsqueeze(1).to_broadcast([P, TOPK, E]), bc(at(eif), E), ALU.is_equal))
                    chain(tt(eqm, eq, of_all(score), ALU.mult))
                    chain(dve.tensor_reduce(eight, eqm, AX.X, ALU.add), wait=False)
                elif u == 1:
                    chain(dve.tensor_reduce(wsum[:, 0, 0:1], eight, AX.X, ALU.add))
                    chain(dve.reciprocal(wsum[:, 0, 1:2], wsum[:, 0, 0:1]))
                    chain(tt(eight, eight, wsum[:, 0, 1:2].to_broadcast([P, TOPK]), ALU.mult))
                    chain(ts(at(gates), eight, ROUTED_SCALE, None, ALU.mult), wait=False)
                elif u == 2:
                    chain(tt(eqm, eq, of_all(tmpr), ALU.mult))
                    chain(dve.tensor_reduce(eight, eqm, AX.X, ALU.add), wait=False)
                else:
                    chain(dve.tensor_copy(at(yidx), eight), wait=False)

            def y_out_of(e, b):
                dve.wait_ge(items_used, e + 82)
                dve.tensor_copy(yb[:, b, :], ps[:, 4:6, :].rearrange("p b n -> p (b n)")).then_inc(S["ex_yd"], 1)

            with dve.Fori(0, E // 4) as g:
                for u in range(4):
                    e = g * 4 + u
                    with dve.If(g < TT):
                        token_tile(dve.snap(tile_no, min_val=0, max_val=TT - 1), u)
                        if u == 3:
                            dve.reg_add(tile_no, tile_no, 1)
                    dve.wait_ge(S["ex_sil"], e + 1)
                    tt(eact[:, u % 2].rearrange("p f s -> p (f s)"), esil[:, u % 2].rearrange("p f s -> p (f s)"),
                       ps[:, 2 + u % 2, 256:512], ALU.mult).then_inc(S["ex_act"], 1)
                    if u == 0:
                        with dve.If(g > 0):
                            dve.wait_ge(y_out[1], g * 16)
                            y_out_of(e - 1, 1)
                    else:
                        if u < 3:
                            with dve.If(g > 0):
                                dve.wait_ge(y_out[u + 1], g * 16)
                                y_out_of(e - 1, u - 1)
                            with dve.If(g < 1):
                                y_out_of(e - 1, u - 1)
                        else:
                            dve.wait_ge(y_out[0], g * 16 + 16)
                            y_out_of(e - 1, 0)
                    more = dve.value_load(cnt_i[0:1, 1, ds(e, 1)], min_val=0, max_val=4)
                    with dve.If(more > 0):
                        with dve.Fori(0, more) as b:
                            o = dve.snap(ov, min_val=0, max_val=EXTRA - 1)
                            dve.wait_ge(S["ov_sil"], o + 1)
                            tt(flat(eacto), flat(esilo), ps[:, 3 - u % 2, 256:512], ALU.mult).then_inc(S["ov_act"], 1)
                            yo = ps[:, 6:8, :].rearrange("p b n -> p (b n)")
                            with dve.If(o > 0):
                                dve.wait_ge(S["ov_y"], o + 1)
                                dve.wait_ge(S["ov_scat"], dve.snap(ov, min_val=1, max_val=EXTRA - 1) * 16)
                                dve.tensor_copy(ybo, yo).then_inc(S["ov_yd"], 1)
                            with dve.If(o < 1):
                                dve.wait_ge(S["ov_y"], o + 1)
                                dve.tensor_copy(ybo, yo).then_inc(S["ov_yd"], 1)
                            dve.reg_add(ov, ov, 1)
            dve.wait_ge(y_out[1], 16 * (E // 4))
            y_out_of(E - 1, 1)
            for i in range(TT):
                n = P if i < TT - 1 else LAST
                acc = accb[0:n, i % 2, :]
                if i >= 2:
                    dve.wait_ge(fin_dma[i % 2], 16 * (i // 2))
                for k in range(TOPK):
                    b = (i % 2) * 8 + k
                    dve.wait_ge(yk_in[b], 16 * (i // 2 + 1))
                    ins = stt(out=acc, in0=yk[0:n, b, :], scalar=gates[0:n, i, k:k + 1],
                              in1=shared[0:n, i, :] if k == 0 else acc, op0=ALU.mult, op1=ALU.add)
                    if k < TOPK - 1:
                        link(ins)
                    else:
                        ins.then_inc(S["yacc"], 1)
                if i == 0:
                    dve.wait_ge(S["G2_act"], 2)
                dve.wait_ge(S["fin_rt"], i + 1)
                link(dve.reciprocal(red[0:n, 2:3], red[0:n, 2:3]))
                link(stt(out=acc, in0=acc, scalar=red[0:n, 2:3], in1=(G2 if i < TT - 1 else G2s)[0:n, :], op0=ALU.mult, op1=ALU.mult))
                tt(accb[0:n, 2 + i % 2, :], acc, x1tok[0:n, i, :], ALU.add).then_inc(S["fin_out"], 1)

        @block.tensor
        def _(pe):
            def mark(ins, name):
                ins.then_inc(S[name], 1)

            mm, tr = pe.matmul, pe.transpose
            pe.wait_ge(consts, 10)
            pe.wait_ge(vrow_in, 16 * 13)
            tr(ps[:, 6, 0:128], vrow, ident[:, :])
            for a in range(2):
                tr(ps[:, 6, 128 + 124 * a:128 + 124 * (a + 1)], wcrow[:, a, :], ident[0:124, 0:124])
            tr(ps[:, 6, 376:504], sarow, ident[:, :])
            mark(tr(ps[:, 6, 504:512], p2row, ident[0:C, 0:C]), "vecs_pe")
            pe.wait_ge(S["csilu_act"], 1)
            for c in range(C):
                ins = tr(ps[:, 7, c * NSEQ:(c + 1) * NSEQ], c_tok[:, c * P:(c + 1) * P], ident[0:NSEQ, 0:NSEQ])
            mark(ins, "cT_pe")
            pe.wait_ge(x_in, 32)
            for c in range(C):
                if c >= 4:
                    pe.wait_ge(S["xT_act"], c - 4 + 1)
                for i in range(TT - 1):
                    ins = tr(ps[:, c % 4, i * P:(i + 1) * P], x_tok[:, i, c * P:(c + 1) * P], ident[:, :])
                mark(ins, "xT_pe")
            for c in range(C):
                ins = tr(ps[:, 5, c * NS:(c + 1) * NS], x_stok[:, c * P:(c + 1) * P], ident[0:NS, 0:NS])
            mark(ins, "xs_pe")
            def stat(bank, src, c):
                for h, (a, b) in enumerate(half):
                    ins = mm(ps[:, bank + h, 0:HT], avg[:, :], src[:, a:b], start=(c == 0), stop=(c == C - 1))
                return ins

            for c in range(C):
                pe.wait_ge(S["xsq_act"], c + 1)
                ins = stat(6, hT[:, c, :], c)
            mark(ins, "xstat_pe")

            def conditioning(w, bank):
                for k in range(C):
                    ins = mm(ps[0:NSEQ, bank, :], scT[:, k, :], w[:, k, :], start=(k == 0), stop=(k == C - 1))
                ins.then_inc(S["ada_row"], 1)

            pe.wait_ge(S["cT_act"], 1)
            pe.wait_ge(S["xT_act"], C)
            for q in range(4):
                pe.wait_ge(w_ada1[q], 16)
                conditioning(ada_w[q], q)
            for q in range(4):
                pe.wait_ge(S["arow_done"], q + 1)
                for n in range(4 * q, 4 * q + 4):
                    ins = tr(ps[:, 4, n * NSEQ:(n + 1) * NSEQ], arow[:, n * P:(n + 1) * P], ident[0:NSEQ, 0:NSEQ])
            mark(ins, "ada_T")
            pe.wait_ge(st_in, 16)
            pe.wait_ge(S["s1_dve"], 1)
            pe.wait_ge(S["xrt_act"], 2)
            W2 = NS * (KC - 1)
            for q in range(4):
                for c in range(2 * q, 2 * q + 2):
                    for a in range(2):
                        at = (c % 2) * W2 + a * 120
                        ins = tr(ps[:, 4 + q, at:at + 120], sbrow[:, a, c * P:(c + 1) * P], ident[0:120, 0:120])
                mark(ins, "stB_pe")

            def product(bank, w, src):
                for h, (a, b) in enumerate(half):
                    for k in range(C):
                        ins = mm(ps[:, bank + h, 0:HT], w[:, k, :], src[:, k, a:b], start=(k == 0), stop=(k == C - 1))
                return ins

            def split_product(n, b, bank, hi, lo):
                pe.wait_ge(S["w_lo"], n + 6)
                for h, (p, q) in enumerate(half):
                    for k in range(C):
                        mm(ps[:, bank + h, 0:HT], wsplit[:, b, 0, k, :], hi[:, k, p:q], start=(k == 0), stop=False)
                        mm(ps[:, bank + h, 0:HT], wsplit[:, b, 0, k, :], lo[:, k, p:q], start=False, stop=False)
                        ins = mm(ps[:, bank + h, 0:HT], wsplit[:, b, 1, k, :], hi[:, k, p:q], start=False, stop=(k == C - 1))
                ins.then_inc(items_used, 1)

            pe.wait_ge(S["h_lo_dve"], C)
            with pe.Fori(0, C // 2) as it:
                for jj in range(2):
                    j = it * 2 + jj
                    for i, bank in enumerate((0, 2, 4, 0, 2)):
                        f = 5 * jj + i
                        if i == 0:
                            pe.wait_ge(S["acs_done"], j + 1)
                        elif i == 1:
                            pe.wait_ge(S["abs_done"], j + 1)
                        elif i == 2:
                            pe.wait_ge(S["ain_done"], j + 1)
                            pe.wait_ge(S["stB_act"], 4)
                        elif i == 3:
                            pe.wait_ge(S["sg_done"], j + 1)
                        else:
                            pe.wait_ge(w_ada2, it * 32 + (16 * jj + 16))
                            pe.wait_ge(S["arow_done"], j + 4)
                            conditioning(ada_w[2], 6)
                            pe.wait_ge(S["glu_done"], j + 2)
                        split_product(it * 10 + f, f % 2, bank, h_hi, h_lo)
                    pe.wait_ge(S["arow_done"], j + 5)
                    pe.wait_ge(S["ada2_done"], j + 1)
                    for n in range(4):
                        ins = mm(ps[:, 7, n * NSEQ:(n + 1) * NSEQ], arow[:, n * P:(n + 1) * P], ident[0:NSEQ, 0:NSEQ], start=True, stop=True)
                    ins.then_inc(S["ada_T"], 1)
            pe.wait_ge(S["va_done"], C + 1)
            pe.wait_ge(S["p2_dve"], 1)
            for c in range(C):
                ins = tr(ps[0:48, 6 + c // 4, (c % 4) * P:(c % 4 + 1) * P], tail[:, c, :], ident[:, :])
            mark(ins, "tails_pe")
            for c in range(C):
                ins = tr(ps[0:NSEQ, 4 + c // 4, (c % 4) * P:(c % 4 + 1) * P], ada[:, 5, c, :], ident[:, :])
            mark(ins, "g2rows_pe")
            pe.wait_ge(S["growc_act"], 1)
            for c in range(C):
                ins = stat(4, cv[:, c, :], c)
            mark(ins, "mean_pe")

            def merge(it, jj, br, hi, lo):
                q = it * 4 + (jj + 8 * br)
                n = it * 8 + (40 + 16 * br + 2 * jj)
                if not (isinstance(it, int) and it + jj + br == 0):
                    pe.wait_ge(S["g_done"], q)
                split_product(n, 0, 0, h_hi, h_lo)
                if br == 0 and it + jj == 0:
                    pe.wait_ge(S["va_lo_pool"], C)
                pe.wait_ge(S["m_done"], q + 1)
                split_product(n + 1, 1, 2, hi, lo)

            for it in range(2):
                for jj in range(4):
                    if it == 0 and jj == 0:
                        pe.wait_ge(S["cen_dve"], 2)
                    merge(it, jj, 0, vm_hi, va_lo)
                if it == 0:
                    for c in range(C):
                        pe.wait_ge(S["sqd"], c + 1)
                        stat(6, scr[:, c % 4, :], c).then_inc(S["stat_mm"], 1)
            pe.wait_ge(S["cv_lo_dve"], C)
            with pe.Fori(0, 2) as it:
                for jj in range(4):
                    merge(it, jj, 1, s_hi, cv_lo)
            pe.wait_ge(S["m_lo_dve"], C)
            pe.wait_ge(S["m_done"], 17)
            for j in range(C + 1):
                if j < C:
                    if j >= 2:
                        pe.wait_ge(S["t_cp"], j)
                    split_product(72 + j, j % 2, 2 * (j % 2), vm_hi, m_lo)
                if j > 0:
                    pe.wait_ge(S["sqd"], 8 + j)
                    stat(6, scr[:, (j - 1) % 4, :], j - 1).then_inc(S["stat_mm"], 1)
            for j in range(C):
                pe.wait_ge(S["sqd"], 17 + j)
                stat(4, scr[:, j % 4, :], j).then_inc(S["stat_mm"], 1)
            for i in range(TT):
                n = P if i < TT - 1 else LAST
                if i >= 1:
                    pe.wait_ge(S["x1t_done"], i)
                for c in range(C):
                    ins = tr(ps[0:n, c // 4, (c % 4) * P:(c % 4 + 1) * P], xT[:, c, i * P:i * P + n], ident[:, :])
                ins.then_inc(S["x1t_T"], 1)
            pe.wait_ge(S["h2_act"], 8)
            pe.wait_ge(S["h2_s_dve"], 1)
            pe.wait_ge(late_in, 32)
            for i in range(TT):
                n = P if i < TT - 1 else LAST
                for k in range(C):
                    ins = mm(ps[0:n, 4, i * E:(i + 1) * E], hT[:, k, i * P:i * P + n], wr[:, k, :], start=(k == 0), stop=(k == C - 1))
            mark(ins, "logits_pe")
            for i in range(TT):
                n = P if i < TT - 1 else LAST
                if i >= 1:
                    pe.wait_ge(S["hx_done"], i)
                for c in range(C):
                    ins = tr(ps[0:n, 2 + c // 4, (c % 4) * P:(c % 4 + 1) * P], hT[:, c, i * P:i * P + n], ident[:, :])
                ins.then_inc(S["hx_T"], 1)
            def shared_up(f):
                for m in range(2):
                    w = ring[:, 0, 2048 * m:2048 * (m + 1)].rearrange("p (k n) -> p k n", k=C)[:, :, f * P:(f + 1) * P]
                    ins = product(2 * m, w, hT)
                ins.then_inc(S["sh_mm"], 1)

            pe.wait_ge(w_sh, 48)
            pe.wait_ge(S["hx_done"], TT)
            pe.wait_ge(S["x1t_done"], TT)
            shared_up(0)
            pe.wait_ge(S["mask_dve"], 1)
            for i in range(TT):
                for q in range(i):
                    mm(ps[:, 5, i * E:(i + 1) * E], ones16[:, :], mask16[:, q, :], start=(q == 0), stop=False)
                mm(ps[:, 5, i * E:(i + 1) * E], upper[:, :], mask16[:, i, :], start=(i == 0), stop=True)
            for i in range(TT):
                ins = mm(ps[:, 6, 0:E], ones16[:, :], mask16[:, i, :], start=(i == 0), stop=(i == TT - 1))
            mark(ins, "rank_pe")
            pe.wait_ge(S["sh_act"], 1)
            shared_up(1)
            pe.wait_ge(S["sh_act"], 2)
            w2s = ring[:, 0, 4096:6144].rearrange("p (k n) -> p k n", k=FT)
            for i in range(TT):
                n = P if i < TT - 1 else LAST
                if i >= 2:
                    pe.wait_ge(S["sh_done"], i - 1)
                for h in range(2):
                    for k in range(FT):
                        ins = mm(ps[0:n, 2 * (i % 2) + h, :], scr[:, 2 + k, i * P:i * P + n], w2s[:, k, h * 512:(h + 1) * 512],
                                 start=(k == 0), stop=(k == FT - 1))
                ins.then_inc(S["sh_o"] if i < TT - 1 else items_used, 1)
            for n in range(TT * TOPK):
                pe.wait_ge(S["idx_ab"], 2 * n + 2)
                mm(ps[:, 7, 0:JOBS], oneA[:, n % 4, :], oneB[:, n % 4, :], start=(n == 0), stop=(n == TT * TOPK - 1)).then_inc(S["idx_mm"], 1)

            def rows_T(src, bank=0):
                v = src.rearrange("s (m c) -> s c m", c=C)
                for c in range(C):
                    ins = tr(ps[:, bank + c // 4, (c % 4) * P:(c % 4 + 1) * P], v[:, c, :], ident[:, :])
                return ins

            def up_products(slot, bank, src, n):
                for m in range(2):
                    w = ring[:, slot, 2048 * m:2048 * (m + 1)].rearrange("p (k n) -> p k n", k=C)
                    for f in range(FT):
                        q = 2 * m + f
                        for k in range(C):
                            ins = mm(ps[:, bank, q * P:q * P + n], w[:, k, f * P:(f + 1) * P], src[:, k, 0:n],
                                     start=(k == 0), stop=(k == C - 1))
                return ins

            def down_products(slot, src, bank=4):
                w = ring[:, slot, 4096:6144].rearrange("p (k n) -> p k n", k=FT)
                for h in range(2):
                    for k in range(FT):
                        ins = mm(ps[:, bank + h, :], src[:, k, :], w[:, k, h * 512:(h + 1) * 512], start=(k == 0), stop=(k == FT - 1))
                return ins

            pe.wait_ge(S["sh_act"], 3)
            pe.wait_ge(S["sh_done"], TT)
            pe.wait_ge(S["table_dve"], 1)
            pe.wait_ge(xg_in[0], 16)
            rows_T(xg[:, 0, :]).then_inc(S["exT"], 1)
            ov = pe.alloc_register("ov_pe")
            pe.reg_mov(ov, 0)
            with pe.Fori(0, E // 4) as g:
                for u in range(4):
                    e = g * 4 + u
                    slot = (u + 1) % 4
                    pe.wait_ge(w_ex[slot], g * 48 + 48)
                    pe.wait_ge(S["exT_done"], e + 1)
                    wide = pe.value_load(cnt_i[0:1, 0, ds(e, 1)], min_val=0, max_val=1)
                    with pe.If(wide > 0):
                        up_products(slot, 2 + u % 2, xgT, P).then_inc(S["ex13"], 1)
                    with pe.If(wide < 1):
                        up_products(slot, 2 + u % 2, xgT, P // 2).then_inc(S["ex13"], 1)

                    def next_rows():
                        pe.wait_ge(xg_in[(u + 1) % 2], g * 32 + 16 * ((u + 1) // 2 + 1))
                        rows_T(xg[:, (u + 1) % 2, :]).then_inc(S["exT"], 1)

                    def last_down():
                        pe.wait_ge(S["ex_act"], e)
                        pe.wait_ge(S["ex_yd"], e)
                        down_products((slot + 3) % 4, eact[:, (u + 3) % 2]).then_inc(items_used, 1)

                    if u < 3:
                        next_rows()
                    else:
                        with pe.If(g < E // 4 - 1):
                            next_rows()
                    if u > 0:
                        last_down()
                    else:
                        with pe.If(g > 0):
                            last_down()
                    more = pe.value_load(cnt_i[0:1, 1, ds(e, 1)], min_val=0, max_val=4)
                    with pe.If(more > 0):
                        with pe.Fori(0, more) as b:
                            o = pe.snap(ov, min_val=0, max_val=EXTRA - 1)
                            pe.wait_ge(S["ovx"], o * 16 + 16)
                            pe.wait_ge(S["ov_yd"], o + 1)
                            rows_T(xgo, 6).then_inc(S["ovT"], 1)
                            pe.wait_ge(S["ovT_done"], o + 1)
                            up_products(slot, 3 - u % 2, xgTo, P).then_inc(S["ov13"], 1)
                            pe.wait_ge(S["ov_act"], o + 1)
                            down_products(slot, eacto, 6).then_inc(S["ov_y"], 1)
                            pe.reg_add(ov, ov, 1)
            pe.wait_ge(S["ex_act"], E)
            pe.wait_ge(S["ex_yd"], E)
            down_products(0, eact[:, 1]).then_inc(items_used, 1)
            for h in range(2):
                mm(ps[:, h, :], firstrow[:, :], grow[:, h * 512:(h + 1) * 512], start=True, stop=True)
            for h in range(2):
                ins = mm(ps[0:NS, 2 + h, :], ident[0:NSEQ, 1:NSEQ], grow[:, h * 512:(h + 1) * 512], start=True, stop=True)
            mark(ins, "g2_pe")


_INS = ['x_prompt', 'x_sample', 'state_sconv', 'state_cconv', 'c_prompt', 'c_sample', 'w_ada', 'b_ada',
        'g_pre1', 'g_post1', 'g_pre2', 'g_post2', 'w_in', 'w_sconv', 'w_out_a', 'w_cconv', 'b_cconv', 'ln_g', 'ln_b',
        'w_out_b', 'b_out_b', 'w_o', 'w_router', 'e_bias', 'w1', 'w3', 'w2', 'ws1', 'ws3', 'ws2']


def kernel(**inputs):
    import numpy as _np
    import concourse.bacc as _bacc
    from concourse import mybir as _mybir
    from concourse.bass_utils import run_bass_kernel_spmd as _run

    nc = _bacc.Bacc("TRN2", target_bir_lowering=False, num_devices=1)
    arrays, args = {}, []
    for name in _INS:
        a = _np.ascontiguousarray(inputs[name])
        arrays[f"in_{name}_dram"] = a
        args.append(nc.dram_tensor(f"in_{name}_dram", a.shape, _mybir.dt.from_np(a.dtype), kind="ExternalInput").ap())
    x_p, x_s, st_a, st_b = (inputs[n].shape for n in ("x_prompt", "x_sample", "state_sconv", "state_cconv"))
    shapes = [x_p, x_s, (st_a[0], x_p[0], st_a[2], st_a[3]), st_a, (st_b[0], x_p[0], st_b[2], st_b[3]), st_b]
    for i, shape in enumerate(shapes):
        args.append(nc.dram_tensor(f"out_{i}_dram", shape, _mybir.dt.float32, kind="ExternalOutput").ap())
    build_program(nc, *args)
    r = _run(nc, [arrays], core_ids=[0])
    return tuple(r.results[0][f"out_{i}_dram"] for i in range(len(shapes)))
```

```python
from contextlib import ExitStack

import concourse.bass as bass
from concourse import mybir

F32 = mybir.dt.float32
F32R = mybir.dt.float32r
F16 = mybir.dt.float16
I32 = mybir.dt.int32
U32 = mybir.dt.uint32
ALU = mybir.AluOpType
ACT = mybir.ActivationFunctionType
AX = mybir.AxisListType
ds = bass.ds

P = 128
RMS_EPS = 1e-6
LN_EPS = 1e-5
ROUTED_SCALE = 2.5
NEG = -1e30


def build_program(
    nc, x_prompt, x_sample, state_sconv, state_cconv, c_prompt, c_sample,
    w_ada, b_ada, g_pre1, g_post1, g_pre2, g_post2, w_in, w_sconv, w_out_a,
    w_cconv, b_cconv, ln_g, ln_b, w_out_b, b_out_b, w_o, w_router, e_bias,
    w1, w3, w2, ws1, ws3, ws2,
    y_prompt, y_sample, new_sconv_p, new_sconv_s, new_cconv_p, new_cconv_s,
):
    D = x_prompt.shape[2]
    NP = x_prompt.shape[1]
    NS = x_sample.shape[0]
    T = NP + NS
    HT = T // 2
    C = D // P
    KS, KC = w_sconv.shape[1], w_cconv.shape[1]
    E, FE = w1.shape[1], w1.shape[3]
    TT = (T + P - 1) // P
    LAST = T - (TT - 1) * P
    TOPK, NG, TOPG = 8, 8, 4
    EG = E // NG
    NSEQ = NS + 1
    EXTRA = (T * TOPK) // (P + 1)
    JOBS = E + EXTRA + 1
    FT = FE // P
    assert T % 2 == 0 and FT == 2 and C == 8 and LAST == NS and E == 64 and NP % P == 0

    h2_rows = nc.dram_tensor("h2_rows", (T, D), F32, kind="Internal").ap()
    y_rows = nc.dram_tensor("y_rows", (T * TOPK, D), F32, kind="Internal").ap()

    ctx = ExitStack()
    with ctx:
        def sb(name, shape, dt=F32):
            return ctx.enter_context(nc.sbuf_tensor(name, shape, dt))

        def sem(name):
            return ctx.enter_context(nc.semaphore(name))

        SLOT = 6144
        RING = 4
        R = C * T
        UNIT = C * P
        RAW0, SPLIT0, ROWS0 = 3 * R, 3 * R + 5 * UNIT, 3 * R + 9 * UNIT

        def parts(*sizes):
            with ExitStack() as inner:
                return [inner.enter_context(nc.sbuf_tensor(f"{n}", [P, size], dt)) for n, size, dt in sizes]

        s_areas = parts(("h_hi", R, F32R), ("h_lo", R, F32R), ("s_hi", R, F32R), ("rawpad", 5 * UNIT, F32),
                        ("wsplit", 4 * UNIT, F32R))
        W2RAW, W2SPLIT = 4 * 4096, 4 * 4096 + 2 * 2048
        w2_split = parts(("w2pad", W2SPLIT, F32), ("w2_split", 4096, F32R))[1][:, :].rearrange(
            "p (a k n) -> p a k n", a=2, k=FT)
        ring = sb("ring", [P, RING, SLOT])
        x_areas = parts(("xpad", R, F32), ("vm_hi", R, F32R), ("cv_lo", R, F32R), ("va_lo", R, F32R), ("m_lo", R, F32R))
        act5 = sb("act5", [P, 5 * R])

        def tiles(t):
            return t[:, :].rearrange("p (c t) -> p c t", c=C)
        h_hi, h_lo, s_hi = (tiles(t) for t in s_areas[0:3])
        vm_hi, cv_lo, va_lo, m_lo = (tiles(t) for t in x_areas[1:5])
        wsplit = s_areas[4][:, :].rearrange("p (b a k n) -> p b a k n", b=2, a=2, k=C)
        rflat = ring[:, :, :].rearrange("p s n -> p (s n)")
        raw = rflat[:, RAW0:RAW0 + 5 * UNIT].rearrange("p (s k n) -> p s k n", s=5, k=C)
        tT = rflat[:, 2 * R:3 * R].rearrange("p (c t) -> p c t", c=C)
        ada_w = [rflat[:, a:a + 4 * UNIT].rearrange("p (k n) -> p k n", k=C) for a in (0, R, 2 * R, SPLIT0)]
        arow = rflat[0:1 + NS, ROWS0:ROWS0 + 2048]
        assert ROWS0 + 2048 <= RING * SLOT
        def region(n):
            return act5[:, n * R:(n + 1) * R].rearrange("p (c t) -> p c t", c=C)
        xT, hT, cv, va, mT = (region(n) for n in range(5))
        va_before = act5[:, 3 * R - T:4 * R - T].rearrange("p (c t) -> p c t", c=C)
        x_tok = cv.rearrange("p c t -> p (c t)")[:, 0:4 * D].rearrange("p (i d) -> p i d", i=4)
        va_flat = act5[:, 3 * R:4 * R]
        x_stok = va_flat[0:NS, 0:D]
        c_tok = va_flat[0:NSEQ, D:2 * D]
        vrow = va_flat[:, 2 * D:2 * D + P]
        wcrow = va_flat[0:124, 2 * D + P:2 * D + 3 * P].rearrange("p (a c) -> p a c", a=2)
        sarow = va_flat[:, 2 * D + 3 * P:2 * D + 4 * P]
        p2row = va_flat[0:C, 2 * D + 4 * P:2 * D + 5 * P]
        assert 2 * D + 5 * P <= R
        sbrow = act5[0:120, 4 * R:4 * R + 2 * D].rearrange("p (a d) -> p a d", a=2)
        o = 2 * R
        x1tok = act5[:, o:o + TT * D].rearrange("p (i d) -> p i d", i=TT)
        shared = act5[:, o + TT * D:o + 2 * TT * D].rearrange("p (i d) -> p i d", i=TT)
        o += 2 * TT * D
        xg = act5[:, o:o + 2 * D].rearrange("p (b d) -> p b d", b=2)
        assert o + 2 * D <= 5 * R
        hflat = act5[:, R:2 * R]
        xgT = hflat[:, 0:D].rearrange("p (c s) -> p c s", c=C)
        diag = hflat[:, 0:D].rearrange("p (b k m) -> p b k m", b=2, k=4)
        xgTo = hflat[:, D:2 * D].rearrange("p (c s) -> p c s", c=C)
        yb = hflat[:, 2 * D:4 * D].rearrange("p (b d) -> p b d", b=2)
        xflat = act5[:, 0:R]
        RE = TT * E
        def rt(n):
            return xflat[:, n * RE:(n + 1) * RE].rearrange("p (i e) -> p i e", i=TT)
        score, sel, selm, repl, tmpr = (rt(n) for n in range(5))
        rank, row, blk = sel, selm, repl
        o = 5 * RE
        eq, eqm = (xflat[:, o + n * TOPK * E:o + (n + 1) * TOPK * E].rearrange("p (k e) -> p k e", k=TOPK) for n in range(2))
        o += 2 * TOPK * E
        sm = xflat[:, o:o + 13 * TT * 8].rearrange("p (n k) -> p n k", n=13)
        o += 13 * TT * 8
        e64 = xflat[:, o:o + 6 * E].rearrange("p (n e) -> p n e", n=6)
        o += 6 * E
        assert o <= R
        yk = ring[:, :, :].rearrange("p s n -> p (s n)")[:, 0:16 * D].rearrange("p (b d) -> p b d", b=16)
        accb = ring[:, :, :].rearrange("p s n -> p (s n)")[:, 16 * D:20 * D].rearrange("p (b d) -> p b d", b=4)

        ident = sb("ident", [P, P])
        avg = sb("avg", [P, P])
        upper = sb("upper", [P, P], F16)
        ones16 = sb("ones16", [P, P], F16)
        firstrow = sb("firstrow", [NSEQ, P])
        eps = sb("eps", [P, 2])
        NV = 512
        act_split = parts(("act_split", 1024, F32R))[0][:, :].rearrange("p (b a f s) -> p b a f s", b=2, a=2, f=2)
        vecs = sb("vecs", [P, NV])
        scT = sb("scT", [P, C, NSEQ])
        ada = sb("ada", [P, 6, C, NSEQ])
        sb("act_split_end", [P, 1024 - NV - 7 * C * NSEQ])
        ada4 = ada[:, :, :, :].rearrange("p a c s -> p (a c s)")[:, 2 * C * NSEQ:].rearrange("p (j n) -> p j n", j=C)
        stB = act5[:, 4 * R + 2 * D:4 * R + 2 * D + C * NS * (KC - 1)].rearrange("p (c n) -> p c n", c=C)
        assert 2 * D + C * NS * (KC - 1) <= R
        wide_n = [KC - 1 + NP, NS * KC, KS - 1 + NP, NS * KS, NS * KC]
        conv = sb("conv", [P, sum(wide_n)])
        def cbuf(n):
            return conv[:, sum(wide_n[:n]):sum(wide_n[:n + 1])]
        glu, up = cbuf(0), cbuf(2)
        glus, us, tmps = (cbuf(n).rearrange("p (s k) -> p s k", s=NS) for n in (1, 3, 4))
        grow = conv[0:NSEQ, 0:D]
        wr = conv[:, D:D + C * E].rearrange("p (k e) -> p k e", k=C)
        sg = sb("sg", [P, T])
        scr = sb("scr", [P, 4, T])
        ain, acs, abs_, vv = (scr[:, n, :] for n in range(4))
        rs = sb("rs", [P, T])
        tail = sb("tail", [P, C, 48])
        sflat = scr[:, :, :].rearrange("p n t -> p (n t)")
        NB = 8
        o = NB * P // 2
        oneA = sflat[:, 0:o].bitcast(F16).rearrange("p (b n) -> p b n", b=NB)
        oneB = sflat[:, o:o + NB * JOBS // 2].bitcast(F16).rearrange("p (b n) -> p b n", b=NB)
        assert o + NB * JOBS // 2 <= 2 * T
        xgo, ybo = sflat[:, 0:D], sflat[:, D:2 * D]
        esil = sg[:, 0:512].rearrange("p (b f s) -> p b f s", b=2, f=2)
        eact = rs[:, 0:512].rearrange("p (b n) -> p b n", b=2)
        eacto = tail[:, :, :].rearrange("p c n -> p (c n)")[:, 0:256]
        w13 = rflat[:, 0:W2RAW].rearrange("p (s n) -> p s n", s=4)
        w2raw = rflat[:, W2RAW:W2SPLIT].rearrange("p (b k n) -> p b k n", b=2, k=FT)
        esilo = conv[:, D + 256:D + 512].rearrange("p (f s) -> p f s", f=2)
        tailrows = rflat[0:48, ROWS0:ROWS0 + D]
        s1 = sb("s1", [P, C, NSEQ])
        smp = sb("smp", [P, C, NS])
        G2 = rflat[:, 20 * D:21 * D]
        G2s = rflat[0:NS, 21 * D:22 * D]
        ebias = sb("ebias", [P, E])
        iot = sb("iot", [P, P])
        tokp1 = sb("tokp1", [P, TT])
        valid = sb("valid", [P, TT])
        slotid = sb("slotid", [P, 1])
        beyond = sb("beyond", [P, JOBS], I32)
        firsty = sb("firsty", [P, E], I32)
        blocks = sb("blocks", [P, TT], I32)
        ioti = cbuf(4).bitcast(I32)
        mask16 = sb("mask16", [P, TT, E], F16)
        def s8(n):
            return sm[:, n, :].rearrange("p (i k) -> p i k", k=8)
        gates = sb("gates", [P, TT, TOPK])
        yidx = sb("yidx", [P, TT, TOPK], I32)
        idxT = sb("idxT", [P, JOBS], I32)
        rowT = sb("rowT", [P, E + 1], I32)
        cnt_i = sb("cnt_i", [1, 3, E + 2], I32)
        gidx = sb("gidx", [P, 6], I32)
        sidx = sb("sidx", [P, 6], I32)
        red = sb("red", [P, 4])

        ps = ctx.enter_context(nc.psum_tensor("ps", [P, 8, 512], F32))

        V_ADA, V_PRE1, V_POST1, V_PRE2, V_SC, V_BC, V_LG, V_LB, V_OB = 0, 48, 56, 64, 72, 96, 104, 112, 120
        V_WC, V_SA, V_POST2 = 128, 376, 504

        consts = sem("consts")
        crow_in, vrow_in, x_in, st_in, late_in = (sem(n) for n in ("crow_in", "vrow_in", "x_in", "st_in", "late_in"))
        out_done = sem("out_done")
        w_big = [sem(f"w_big_{s}") for s in range(RING)]
        w2_in = [sem(f"w2_in_{b}") for b in range(2)]
        w_ada2 = sem("w_ada2")
        w_raw = [sem(f"w_raw_{s}") for s in range(5)]
        w_sh = sem("w_sh")
        items_used = sem("items_used")
        dve_step = sem("dve_step")
        pool_step = sem("pool_step")
        names = ("w2_hi w2_lo w_hi w_lo ada_row arow_done ada_T h_dve va_hi_act va_lo_pool h_lo_dve cv_lo_dve m_lo_dve sg_done ain_done acs_done abs_done glu_done ada2_done u_done v_done va_done "
                 "pa_chain pool_chain "
                 "vecs_pe vecs_act cT_pe cT_act xT_pe xT_act xs_pe xs_act xsq_act xstat_pe xrt_act stB_pe stB_act csilu_act "
                 "s1_dve xn_dve h_act h_s_dve tails_pe tailrows_act g2rows_pe growc_act p2_dve g2_pe G2_act "
                 "mean_pe cen_dve lrt_act ln_dve s_act trt_act x1_dve x1rt_act x1n_dve h2_act h2_s_dve logits_pe "
                 "score0_dve score_s_act mask_dve rank_pe table_dve late_chain "
                 "g_done m_done m_chain t_cp stat_mm sqd idx_ab idx_mm hx_T hx_done "
                 "x1t_T x1t_done sh_mm sh_act sh_o sh_done "
                 "exT exT_done ex13 ex_sil ex_full ex_act ex_yd gcopy scopy passed "
                 "ovT ovT_done ov13 ov_sil ov_full ov_act ov_y ov_yd ovcopy ovx ov_scat diag_act yacc fin_sq fin_rt fin_out").split()
        S = {n: sem(n) for n in names}
        rows_out = [sem(f"rows_out{b}") for b in range(2)]
        xg_in = [sem(f"xg_in{b}") for b in range(2)]
        y_out = [sem(f"y_out{u}") for u in range(4)]
        yk_in = [sem(f"yk_in{b}") for b in range(16)]

        LA = 10

        def flat(ap):
            return ap.rearrange("p c t -> p (c t)")

        half = [(0, HT), (HT, T)]

        block = ctx.enter_context(nc.Block())

        @block.sync
        def _(sp):
            def w_src(t, col, n):
                return t[0, :, col:col + n].rearrange("(k p) n -> p k n", p=P)

            sp.dma_start(x_tok, x_prompt[0].rearrange("(i p) d -> p i d", p=P)).then_inc(x_in, 16)
            sp.wait_ge(crow_in, 48)
            for q in range(4):
                sp.dma_start(ada_w[q], w_src(w_ada, q * 512, 512)).then_inc(w_big[q], 16)
            def passed():
                sp.sem_inc(S["passed"], 1)

            with sp.Fori(0, C // 2) as it:
                for jj in range(2):
                    j = it * 2 + jj
                    chunk = sp.snap(it * 1024 + (jj * 512 + 2 * D), min_val=2 * D, max_val=6 * D - 512)
                    for i, a in enumerate((4, 3, 0, 2, 1)):
                        sp.wait_ge(S["w_lo"], it * 10 + (5 * jj + i + 1))
                        passed()
                        sp.dma_start(raw[:, i], w_in[0, :, ds(j * P + a * D, P)].rearrange("(k p) n -> p k n", p=P)
                                     ).then_inc(w_raw[i], 16)
                    sp.wait_ge(S["ada_row"], it * 2 + (jj + 4))
                    passed()
                    sp.dma_start(ada_w[2], w_ada[0, :, ds(chunk, 512)].rearrange("(k p) n -> p k n", p=P)
                                 ).then_inc(w_ada2, 16)
            for n0, w, c0 in ((40, w_in[0], 5 * D), (48, w_out_a[0], 0)):
                with sp.Fori(0, 2) as it:
                    for jj in range(4):
                        sp.wait_ge(S["w_lo"], it * 4 + (n0 + jj + 2))
                        passed()
                        sp.dma_start(raw[:, jj], w[:, ds(it * 512 + (jj * P + c0), P)].rearrange("(k p) n -> p k n", p=P)
                                     ).then_inc(w_raw[jj], 16)
            with sp.Fori(0, 2) as it:
                for jj in range(4):
                    j = it * 4 + jj
                    for i in range(2):
                        slot = (2 * jj + i) % 4
                        sp.wait_ge(S["w_lo"], it * 8 + (56 + 2 * jj + i + 2))
                        passed()
                        src = w_in[0, :, ds(j * P + 6 * D, P)] if i == 0 else w_out_b[0, :, ds(j * P, P)]
                        sp.dma_start(raw[:, slot], src.rearrange("(k p) n -> p k n", p=P)).then_inc(w_raw[slot], 16)
            with sp.Fori(0, 2) as it:
                for jj in range(4):
                    j = it * 4 + jj
                    sp.wait_ge(S["w_lo"], it * 4 + (72 + jj + 2))
                    passed()
                    sp.dma_start(raw[:, jj], w_o[0, :, ds(j * P, P)].rearrange("(k p) n -> p k n", p=P)).then_inc(w_raw[jj], 16)
            sp.wait_ge(items_used, 72)
            sp.wait_ge(items_used, 41)
            sp.dma_start(w13[:, 0, 0:2048].rearrange("p (k n) -> p k n", k=C), w_src(ws1, 0, FE)).then_inc(w_sh, 16)
            sp.dma_start(w13[:, 0, 2048:4096].rearrange("p (k n) -> p k n", k=C), w_src(ws3, 0, FE)).then_inc(w_sh, 16)
            sp.wait_ge(out_done, 16 * 6)
            sp.wait_ge(items_used, 80)
            sp.wait_ge(S["x1_dve"], C)
            sp.dma_start(w2raw[:, 0], w_src(ws2, 0, D)).then_inc(w_sh, 16)
            with sp.Fori(0, E // 4) as g:
                for u in range(4):
                    slot = (u + 1) % 4
                    e = g * 4 + u
                    sp.wait_ge(items_used, g * 4 + (78 + u))
                    for m, w in enumerate((w1, w3)):
                        sp.dma_start(w13[:, slot, 2048 * m:2048 * (m + 1)],
                                     w[0, ds(e, 1), :, :].rearrange("a (p k) n -> p (a k n)", p=P)
                                     ).then_inc(w_big[slot], 16)
                    if u == 1:
                        sp.wait_ge(items_used, 81)
                    sp.wait_ge(S["w2_lo"], g * 4 + (u + 1))
                    passed()
                    sp.dma_start(w2raw[:, (u + 1) % 2],
                                 w2[0, ds(e, 1), :, :].rearrange("a (k p) n -> p (a k) n", p=P)
                                 ).then_inc(w2_in[(u + 1) % 2], 16)
            for i in range(TT):
                n = P if i < TT - 1 else LAST
                sp.wait_ge(S["fin_out"], i + 1)
                dst = y_prompt[0, i * P:(i + 1) * P, :] if i < TT - 1 else y_sample.rearrange("n a d -> (n a) d")
                sp.dma_start(dst, accb[0:n, 2 + i % 2, :]).then_inc(rows_out[i % 2], 16)
            sp.wait_ge(out_done, 16 * 6)
            sp.wait_ge(rows_out[0], 16 * 6)
            sp.wait_ge(rows_out[1], 16 * 4)

        @block.gpsimd
        def _(pool):
            n_step = [0]

            def link(ins):
                n_step[0] += 1
                ins.then_inc(pool_step, 1)
                pool.wait_ge(pool_step, n_step[0])

            for n in ("glu_done", "u_done", "va_done", "acs_done", "abs_done", "ain_done", "ada2_done", "v_done",
                      "m_done", "t_cp", "ex_yd", "ov_yd"):
                pool.sem_inc(S[n], 1)
            pool.sem_inc(S["w_lo"], 5)
            pool.sem_inc(S["w2_lo"], 2)
            link(pool.memset(ident[:, :], 0.0))
            pool.affine_select(out=ident[:, :], in_=ident[:, :], compare_op=ALU.not_equal, fill=1.0, base=0,
                               pattern=[[-1, P]], channel_multiplier=1).then_inc(consts, 1)
            pool.memset(avg[:, :], 1.0 / D).then_inc(consts, 1)
            pool.memset(eps[:, 0:1], RMS_EPS).then_inc(consts, 1)
            pool.memset(eps[:, 1:2], LN_EPS).then_inc(consts, 1)
            pool.memset(glu[:, 0:KC - 1], 0.0).then_inc(consts, 1)
            pool.memset(up[:, 0:KS - 1], 0.0).then_inc(consts, 1)
            link(pool.memset(firstrow[:, :], 1.0))
            pool.affine_select(out=firstrow[:, :], in_=firstrow[:, :], compare_op=ALU.is_ge, fill=0.0, base=0,
                               pattern=[[0, P]], channel_multiplier=-1).then_inc(consts, 1)
            pool.memset(ones16[:, :], 1.0).then_inc(consts, 1)
            link(pool.memset(upper[:, :], 1.0))
            pool.affine_select(out=upper[:, :], in_=upper[:, :], compare_op=ALU.is_ge, fill=0.0, base=-1,
                               pattern=[[1, P]], channel_multiplier=-1).then_inc(consts, 1)
            for dst, pattern, base, cm in ((iot[:, :], [[1, P]], 0, 0), (tokp1[:, :], [[P, TT]], 1, 1),
                                           (slotid[:, :], [[0, 1]], 0, 1)):
                n = dst.shape[1]
                link(pool.iota(ioti[:, 0:n], pattern=pattern, base=base, channel_multiplier=cm))
                link(pool.tensor_copy(dst, ioti[:, 0:n]))
            link(pool.iota(blocks[:, :], pattern=[[P, TT]], base=0, channel_multiplier=0))
            pool.tensor_scalar(valid[:, :], tokp1[:, :], T + 0.5, None, ALU.is_lt).then_inc(consts, 1)
            pool.wait_ge(S["vecs_act"], 1)

            def split_lo(n, raw_slot, b):
                pool.wait_ge(S["w_hi"], n + 1)
                pool.tensor_tensor(wsplit[:, b, 1], raw[:, raw_slot], wsplit[:, b, 0], ALU.subtract).then_inc(S["w_lo"], 1)

            def gated(j):
                pool.wait_ge(S["v_done"], j + 2)
                pool.wait_ge(S["abs_done"], j + 2)
                pool.tensor_tensor(va[:, ds(j, 1), :].rearrange("p a t -> p (a t)"), vv, abs_, ALU.mult).then_inc(S["va_done"], 1)

            split_lo(0, 0, 0)
            split_lo(1, 1, 1)
            with pool.Fori(0, C // 2) as it:
                for jj in range(2):
                    j = it * 2 + jj
                    for i in range(5):
                        f = 5 * jj + i
                        split_lo(it * 10 + (f + 2), (f + 2) % 5, f % 2)
                        if i == 2:
                            if jj == 1:
                                gated(j - 1)
                            else:
                                with pool.If(it > 0):
                                    pool.wait_ge(S["v_done"], j + 1)
                                    pool.wait_ge(S["abs_done"], j + 1)
                                    pool.tensor_tensor(va_before[:, ds(j, 1), :].rearrange("p a t -> p (a t)"), vv, abs_,
                                                       ALU.mult).then_inc(S["va_done"], 1)
                        if i == 3:
                            pool.wait_ge(S["acs_done"], j + 2)
                            pool.wait_ge(S["ain_done"], j + 2)
                            pool.wait_ge(S["v_done"], j + 1)
                            pool.tensor_tensor(up[:, KS - 1:], acs[:, 0:NP], ain[:, 0:NP], ALU.mult).then_inc(S["pool_chain"], 1)
                            pool.tensor_tensor(us[:, :, KS - 1], acs[:, NP:T], ain[:, NP:T], ALU.mult).then_inc(S["pool_chain"], 1)
                            pool.tensor_copy(us[:, :, 0:KS - 1],
                                             vecs[:, V_SA:V_SA + 128].rearrange("p (n k c) -> p n k c", n=NS, c=C)[:, :, :, ds(j, 1)]
                                             .rearrange("p n k c -> p n (k c)")).then_inc(S["pool_chain"], 1)
                            pool.wait_ge(S["pool_chain"], j * 4 + 3)
                            pool.tensor_copy(tail[:, ds(j, 1), 38:40].rearrange("p a n -> p (a n)"), up[:, NP:NP + 2]).then_inc(S["pool_chain"], 1)
                            pool.wait_ge(S["pool_chain"], j * 4 + 4)
                            pool.tensor_copy(tail[:, ds(j, 1), 40:48].rearrange("p a n -> p (a n)"), us[:, :, KS - 1]).then_inc(S["u_done"], 1)
            for n in range(42, 45):
                split_lo(n, n % 4, n % 2)
            gated(C - 1)
            for c in range(C):
                pool.wait_ge(S["va_hi_act"], c + 1)
                pool.tensor_tensor(va_lo[:, c, :], va[:, c, :], vm_hi[:, c, :], ALU.subtract).then_inc(S["va_lo_pool"], 1)
            for n in range(45, 80):
                split_lo(n, n % 4, n % 2)
            pool.wait_ge(rows_out[0], 16 * 3)
            pool.wait_ge(rows_out[1], 16 * 2)
            pool.wait_ge(S["table_dve"], 1)
            ov = pool.alloc_register("ov_pool")
            pool.reg_mov(ov, 0)
            last_row, last_y = pool.alloc_register("last_row"), pool.alloc_register("last_y")
            pool.reg_mov(last_row, T - 1)
            pool.reg_mov(last_y, T * TOPK - 1)

            def wait_here():
                pool.sem_inc(S["passed"], 1)

            def gather(e, u, count):
                pool.tensor_copy(gidx[:, u:u + 1], idxT[:, ds(e, 1)]).then_inc(S["gcopy"], 1)
                pool.wait_ge(S["gcopy"], count)
                wait_here()
                wide = pool.value_load(cnt_i[0:1, 0, ds(e, 1)], min_val=0, max_val=1)
                for m, n in ((1, P), (0, P // 2)):
                    with pool.If(wide > 0) if m else pool.If(wide < 1):
                        pool.indirect_dma_start(out=xg[0:n, u % 2, :], out_offset=None, in_=h2_rows,
                                                in_offset=bass.IndirectOffsetOnAxis(ap=gidx[0:n, u:u + 1], axis=0),
                                                bounds_check=last_row, oob_is_err=False).then_inc(xg_in[u % 2], 16)

            def scatter(after, u):
                pool.wait_ge(S["ex_yd"], after + 1)
                pool.tensor_copy(sidx[:, u:u + 1], rowT[:, ds(after, 1)]).then_inc(S["scopy"], 1)
                pool.wait_ge(S["scopy"], after)
                wait_here()
                wide = pool.value_load(cnt_i[0:1, 2, ds(after, 1)], min_val=0, max_val=1)
                for m, n in ((1, P), (0, P // 2)):
                    with pool.If(wide > 0) if m else pool.If(wide < 1):
                        pool.indirect_dma_start(out=y_rows,
                                                out_offset=bass.IndirectOffsetOnAxis(ap=sidx[0:n, u:u + 1], axis=0),
                                                in_=yb[0:n, u % 2, :], in_offset=None,
                                                bounds_check=last_y, oob_is_err=False).then_inc(y_out[u], 16)

            def gather_further(o, count):
                pool.tensor_copy(gidx[:, 4:5], idxT[:, ds(o + E, 1)]).then_inc(S["ovcopy"], 1)
                pool.wait_ge(S["ovcopy"], count)
                wait_here()
                pool.indirect_dma_start(out=xgo, out_offset=None, in_=h2_rows,
                                        in_offset=bass.IndirectOffsetOnAxis(ap=gidx[:, 4:5], axis=0),
                                        bounds_check=last_row, oob_is_err=False).then_inc(S["ovx"], 16)

            gather(0, 0, 1)
            gather(1, 1, 2)
            pool.wait_ge(items_used, 81)
            link(pool.memset(xgo, 0.0))
            gather_further(0, 1)
            with pool.Fori(0, E // 4) as g:
                for u in range(4):
                    e = g * 4 + u

                    def ahead():
                        pool.wait_ge(S["exT"], e + 1)
                        gather(e + 2, (u + 2) % 4, e + 3)

                    if u < 2:
                        ahead()
                    else:
                        with pool.If(g < E // 4 - 1):
                            ahead()
                    if u == 0:
                        with pool.If(g > 0):
                            scatter(e, 3)
                    else:
                        scatter(e, u - 1)
                    more = pool.value_load(cnt_i[0:1, 1, ds(e, 1)], min_val=0, max_val=4)
                    with pool.If(more > 0):
                        with pool.Fori(0, more) as b:
                            o = pool.snap(ov, min_val=0, max_val=EXTRA - 1)
                            pool.wait_ge(S["ovT"], o + 1)
                            gather_further(o + 1, o * 3 + 2)
                            pool.wait_ge(S["ov_yd"], o + 2)
                            pool.tensor_tensor(sidx[:, 4:5], firsty[:, ds(e, 1)], beyond[:, ds(o + E, 1)], ALU.add).then_inc(S["ovcopy"], 1)
                            pool.wait_ge(S["ovcopy"], o * 3 + 3)
                            pool.tensor_tensor(sidx[:, 5:6], sidx[:, 4:5], blocks[:, ds(b + 1, 1)], ALU.add).then_inc(S["ovcopy"], 1)
                            pool.wait_ge(S["ovcopy"], o * 3 + 4)
                            wait_here()
                            pool.indirect_dma_start(out=y_rows, out_offset=bass.IndirectOffsetOnAxis(ap=sidx[:, 5:6], axis=0),
                                                    in_=ybo, in_offset=None,
                                                    bounds_check=last_y, oob_is_err=False).then_inc(S["ov_scat"], 16)
                            pool.reg_add(ov, ov, 1)
            scatter(E, 3)
            for u in range(4):
                pool.wait_ge(y_out[u], 16 * (E // 4))
            pool.wait_ge(items_used, 81 + E)
            pool.wait_ge(S["late_chain"], LA * TT)
            for i in range(TT):
                n = P if i < TT - 1 else LAST
                if i >= 2:
                    pool.wait_ge(S["yacc"], i - 1)
                for k in range(TOPK):
                    b = (i % 2) * 8 + k
                    pool.indirect_dma_start(out=yk[0:n, b, :], out_offset=None, in_=y_rows,
                                            in_offset=bass.IndirectOffsetOnAxis(ap=yidx[0:n, i, k:k + 1], axis=0),
                                            bounds_check=last_y, oob_is_err=False).then_inc(yk_in[b], 16)

        @block.scalar
        def _(act):
            def mark(ins, name):
                ins.then_inc(S[name], 1)

            act.dma_start(c_tok[0:1, :], c_prompt).then_inc(crow_in, 16)
            act.dma_start(c_tok[1:NSEQ, :], c_sample).then_inc(crow_in, 16)
            act.dma_start(x_stok, x_sample.rearrange("n a d -> (n a) d")).then_inc(crow_in, 16)
            for base, n, t in ((V_ADA, 48, b_ada.rearrange("l (r c) -> (l r) c", c=P)),
                               (V_PRE1, C, g_pre1.rearrange("l (r c) -> (l r) c", c=P)),
                               (V_POST1, C, g_post1.rearrange("l (r c) -> (l r) c", c=P)),
                               (V_PRE2, C, g_pre2.rearrange("l (r c) -> (l r) c", c=P)),
                               (V_SC, C * KS, w_sconv.rearrange("l k (r c) -> (l k r) c", c=P)),
                               (V_BC, C, b_cconv.rearrange("l (r c) -> (l r) c", c=P)),
                               (V_LG, C, ln_g.rearrange("l (r c) -> (l r) c", c=P)),
                               (V_LB, C, ln_b.rearrange("l (r c) -> (l r) c", c=P)),
                               (V_OB, C, b_out_b.rearrange("l (r c) -> (l r) c", c=P))):
                act.dma_start(vrow[base:base + n, :], t).then_inc(vrow_in, 16)
            act.dma_start(p2row, g_post2.rearrange("l (r c) -> (l r) c", c=P)).then_inc(vrow_in, 16)
            wcr = w_cconv.rearrange("l k (r c) -> (l k r) c", c=P)
            for a in range(2):
                act.dma_start(wcrow[:, a, :], wcr[a * 124:(a + 1) * 124, :]).then_inc(vrow_in, 16)
            act.dma_start(sarow, state_sconv.rearrange("l n k (r c) -> (l n k r) c", c=P)).then_inc(vrow_in, 16)
            act.dma_start(sbrow, state_cconv.rearrange("l n k d -> (l n k) d").rearrange("(a r) d -> r a d", a=2)).then_inc(st_in, 16)
            act.dma_start(ebias[:, :], e_bias.to_broadcast([P, E])).then_inc(late_in, 16)
            for c in range(C):
                act.wait_ge(S["xT_pe"], c + 1)
                mark(act.activation(xT[:, c, 0:NP], ps[:, c % 4, 0:NP], ACT.Copy), "xT_act")
            act.wait_ge(S["xs_pe"], 1)
            mark(act.activation(xT[:, :, NP:T], ps[:, 5, 0:C * NS].rearrange("p (c s) -> p c s", c=C), ACT.Copy), "xs_act")
            act.wait_ge(crow_in, 48)
            mark(act.activation(c_tok, c_tok, ACT.Silu), "csilu_act")
            act.wait_ge(S["xs_act"], 1)
            for c in range(C):
                mark(act.activation(hT[:, c, :], xT[:, c, :], ACT.Square), "xsq_act")
            act.wait_ge(S["cT_pe"], 1)
            mark(act.activation(scT[:, :, :].rearrange("p c s -> p (c s)"), ps[:, 4, 0:C * NSEQ], ACT.Copy), "cT_act")
            act.wait_ge(S["xstat_pe"], 1)
            for h, (a, b) in enumerate(half):
                mark(act.activation(rs[:, a:b], ps[:, 6 + h, 0:HT], ACT.Sqrt, bias=eps[:, 0:1]), "xrt_act")
            for q in range(4):
                act.wait_ge(S["ada_row"], q + 1)
                mark(act.activation(arow[:, q * 512:(q + 1) * 512], ps[0:NSEQ, q, :], ACT.Copy), "arow_done")
            act.wait_ge(S["vecs_pe"], 1)
            mark(act.activation(vecs[:, 0:NV], ps[:, 5, 0:NV], ACT.Copy), "vecs_act")

            def split_hi(raw_slot, b, loads):
                act.wait_ge(w_raw[raw_slot], loads)
                act.activation(wsplit[:, b, 0], raw[:, raw_slot], ACT.Copy).then_inc(S["w_hi"], 1)

            split_hi(0, 0, 16)
            split_hi(1, 1, 16)
            for c in range(C):
                act.wait_ge(S["h_dve"], c + 1)
                mark(act.activation(h_hi[:, c, 0:NP], hT[:, c, 0:NP], ACT.Copy), "h_act")
            W2 = NS * (KC - 1)
            for q in range(4):
                act.wait_ge(S["stB_pe"], q + 1)
                mark(act.activation(stB[:, 2 * q:2 * q + 2, :].rearrange("p c n -> p (c n)"), ps[:, 4 + q, 0:2 * W2],
                                    ACT.Copy), "stB_act")
            act.dma_start(new_cconv_s[0, :, 0:KC - 2, :], state_cconv[0, :, 1:KC - 1, :]).then_inc(out_done, 16)
            act.dma_start(new_sconv_s[0, :, 0:KS - 2, :], state_sconv[0, :, 1:KS - 1, :]).then_inc(out_done, 16)
            with act.Fori(0, C // 2) as it:
                for jj in range(2):
                    j = it * 2 + jj
                    for i in range(5):
                        f = 5 * jj + i
                        act.wait_ge(items_used, it * 10 + (f + 1))
                        split_hi((f + 2) % 5, f % 2, it * 32 + (16 * ((f + 2) // 5) + 16))
                        if i == 0:
                            act.wait_ge(S["glu_done"], j + 1)
                            for h, (a, b) in enumerate(half):
                                ins = act.activation(sg[:, a:b], ps[:, h, 0:HT], ACT.Sigmoid)
                            ins.then_inc(S["sg_done"], 1)
                        elif i == 2:
                            act.wait_ge(S["u_done"], j + 1)
                            for h, (a, b) in enumerate(half):
                                ins = act.activation(ain[:, a:b], ps[:, 4 + h, 0:HT], ACT.Copy)
                            ins.then_inc(S["ain_done"], 1)
                        elif i == 3:
                            for h, (a, b) in enumerate(half):
                                ins = act.activation(acs[:, a:b], ps[:, h, 0:HT], ACT.Copy)
                            ins.then_inc(S["acs_done"], 1)
                            act.wait_ge(S["ada_row"], j + 5)
                            act.wait_ge(S["ada_T"], j + 1)
                            act.activation(arow[:, 0:512], ps[0:NSEQ, 6, :], ACT.Copy).then_inc(S["arow_done"], 1)
                        elif i == 4:
                            act.wait_ge(S["va_done"], j + 1)
                            for h, (a, b) in enumerate(half):
                                ins = act.activation(abs_[:, a:b], ps[:, 2 + h, 0:HT], ACT.Copy)
                            ins.then_inc(S["abs_done"], 1)
            def next_unit(n, raw_slot, b, loads):
                act.wait_ge(items_used, n + 1)
                split_hi(raw_slot, b, loads)

            def gate_a(j):
                next_unit(40 + j, (j + 2) % 4, j % 2, 16 * (8 + (j + 2) // 4 + 1))
                for h, (a, b) in enumerate(half):
                    ins = act.activation(mT[:, j, a:b], ps[:, 2 * (j % 2) + h, 0:HT], ACT.Sigmoid)
                ins.then_inc(S["g_done"], 1)

            act.wait_ge(S["glu_done"], C + 1)
            for j in range(3):
                gate_a(j)
            act.wait_ge(S["va_done"], C + 1)
            for c in range(C):
                mark(act.activation(vm_hi[:, c, :], va[:, c, :], ACT.Copy), "va_hi_act")
            act.wait_ge(S["tails_pe"], 1)
            mark(act.activation(tailrows[:, :], ps[0:48, 6:8, :].rearrange("p b n -> p (b n)"), ACT.Copy), "tailrows_act")
            act.wait_ge(S["g2rows_pe"], 1)
            mark(act.activation(grow, ps[0:NSEQ, 4:6, :].rearrange("p b n -> p (b n)"), ACT.Copy), "growc_act")
            act.dma_start(wr, w_router[0].rearrange("(k p) e -> p k e", p=P)).then_inc(late_in, 16)
            act.wait_ge(S["tailrows_act"], 1)
            act.dma_start(new_cconv_p[0, 0], tailrows[0:KC - 1, :]).then_inc(out_done, 16)
            act.dma_start(new_cconv_s[0, :, KC - 2, :], tailrows[KC - 1:KC - 1 + NS, :]).then_inc(out_done, 16)
            act.dma_start(new_sconv_p[0, 0], tailrows[38:40, :]).then_inc(out_done, 16)
            act.dma_start(new_sconv_s[0, :, KS - 2, :], tailrows[40:48, :]).then_inc(out_done, 16)
            for j in range(3, 5):
                gate_a(j)
            for h in range(2):
                act.wait_ge(S["cen_dve"], h + 1)
            for c in range(C):
                if c >= 4:
                    act.wait_ge(S["stat_mm"], c - 3)
                act.activation(scr[:, c % 4, :], cv[:, c, :], ACT.Square).then_inc(S["sqd"], 1)
            act.wait_ge(S["stat_mm"], 8)
            for h, (a, b) in enumerate(half):
                mark(act.activation(rs[:, a:b], ps[:, 6 + h, 0:HT], ACT.Sqrt, bias=eps[:, 1:2]), "lrt_act")
            for j in range(5, C):
                gate_a(j)
            for j in range(C):
                next_unit(48 + j, (j + 2) % 4, j % 2, 16 * (10 + (j + 2) // 4 + 1))
                act.wait_ge(S["ln_dve"], j + 1)
                for dst in (s_hi, cv):
                    ins = act.activation(dst[:, j, :], cv[:, j, :], ACT.Silu, bias=vecs[:, V_LB + j:V_LB + j + 1],
                                         scale=vecs[:, V_LG + j:V_LG + j + 1])
                mark(ins, "s_act")
            with act.Fori(0, 2) as it:
                for jj in range(4):
                    n = it * 8 + (56 + 2 * jj)
                    next_unit(n, (2 * jj + 2) % 4, 0, it * 32 + (16 * 12 + 16 * ((2 * jj + 2) // 4) + 16))
                    act.wait_ge(S["m_done"], it * 4 + (8 + jj + 1))
                    for h, (a, b) in enumerate(half):
                        ins = act.activation(sg[:, a:b], ps[:, h, 0:HT], ACT.Sigmoid)
                    ins.then_inc(S["g_done"], 1)
                    next_unit(n + 1, (2 * jj + 3) % 4, 1, it * 32 + (16 * 12 + 16 * ((2 * jj + 3) // 4) + 16))
            for j in range(C):
                q = 2 * (j % 2)
                act.wait_ge(items_used, 73 + j)
                if j < C - 2:
                    split_hi((j + 2) % 4, j % 2, 16 * (16 + (j + 2) // 4 + 1))
                for h, (a, b) in enumerate(half):
                    ins = act.activation(tT[:, j, a:b], ps[:, q + h, 0:HT], ACT.Copy)
                ins.then_inc(S["t_cp"], 1)
                act.wait_ge(S["stat_mm"], 8 + j - 3)
                act.wait_ge(S["t_cp"], j + 2)
                act.activation(scr[:, j % 4, :], tT[:, j, :], ACT.Square).then_inc(S["sqd"], 1)
            act.wait_ge(S["stat_mm"], 16)
            for h, (a, b) in enumerate(half):
                mark(act.activation(rs[:, a:b], ps[:, 6 + h, 0:HT], ACT.Sqrt, bias=eps[:, 0:1]), "trt_act")
            for j in range(C):
                act.wait_ge(S["x1_dve"], j + 1)
                act.wait_ge(S["stat_mm"], 16 + j - 3)
                act.activation(scr[:, j % 4, :], xT[:, j, :], ACT.Square).then_inc(S["sqd"], 1)
            act.wait_ge(S["stat_mm"], 24)
            for h, (a, b) in enumerate(half):
                mark(act.activation(rs[:, a:b], ps[:, 4 + h, 0:HT], ACT.Sqrt, bias=eps[:, 0:1]), "x1rt_act")
            def x1_rows(i):
                n, b = (P if i < TT - 1 else LAST), (0, 2, 6, 0, 2)[i]
                act.wait_ge(S["x1t_T"], i + 1)
                act.activation(x1tok[0:n, i, :], ps[0:n, b:b + 2, :].rearrange("p b n -> p (b n)"), ACT.Copy).then_inc(S["x1t_done"], 1)

            for i in range(3):
                x1_rows(i)
            for c in range(C):
                act.wait_ge(S["x1n_dve"], c + 1)
                mark(act.activation(hT[:, c, 0:NP], hT[:, c, 0:NP], ACT.Identity, bias=ada[:, 3, c, 0:1],
                                    scale=s1[:, c, 0:1]), "h2_act")
            for i in range(3, TT):
                x1_rows(i)
            act.wait_ge(S["logits_pe"], 1)
            act.wait_ge(S["score0_dve"], 1)
            mark(act.activation(score[:, 0:TT - 1, :], ps[:, 4, 0:(TT - 1) * E].rearrange("p (i e) -> p i e", e=E), ACT.Sigmoid), "score_s_act")
            mark(act.activation(score[0:LAST, TT - 1, :], ps[0:LAST, 4, (TT - 1) * E:TT * E], ACT.Sigmoid), "score_s_act")
            for i in range(TT):
                n = P if i < TT - 1 else LAST
                act.wait_ge(S["hx_T"], i + 1)
                if i >= 2:
                    act.wait_ge(rows_out[i % 2], 16 * (i // 2))
                act.activation(xg[0:n, i % 2, :], ps[0:n, 2:4, :].rearrange("p b n -> p (b n)"), ACT.Copy).then_inc(S["hx_done"], 1)
                act.wait_ge(S["hx_done"], i + 1)
                act.dma_start(h2_rows[i * P:i * P + n, :], xg[0:n, i % 2, :]).then_inc(rows_out[i % 2], 16)
            for f in range(FT):
                act.wait_ge(S["sh_mm"], f + 1)
                if f == 1:
                    act.wait_ge(S["sh_act"], 1)
                for h, (a, b) in enumerate(half):
                    ins = act.activation(sg[:, a:b], ps[:, h, 0:HT], ACT.Silu)
                ins.then_inc(S["g_done"], 1)
            for i in range(TT):
                n = P if i < TT - 1 else LAST
                if i < TT - 1:
                    act.wait_ge(S["sh_o"], i + 1)
                else:
                    act.wait_ge(items_used, 81)
                act.activation(shared[0:n, i, :], ps[0:n, 2 * (i % 2):2 * (i % 2) + 2, :].rearrange("p b n -> p (b n)"),
                               ACT.Copy).then_inc(S["sh_done"], 1)
            act.wait_ge(S["exT"], 1)
            act.activation(flat(xgT), ps[:, 0:2, :].rearrange("p b n -> p (b n)"), ACT.Copy).then_inc(S["exT_done"], 1)
            ov = act.alloc_register("ov_act")
            act.reg_mov(ov, 0)
            with act.Fori(0, E // 4) as g:
                for u in range(4):
                    e = g * 4 + u
                    act.wait_ge(S["ex13"], e + 1)
                    act.activation(esil[:, u % 2].rearrange("p f s -> p (f s)"), ps[:, 2 + u % 2, 0:256], ACT.Silu).then_inc(S["ex_sil"], 1)

                    def next_rows():
                        act.wait_ge(S["exT"], e + 2)
                        act.activation(flat(xgT), ps[:, 0:2, :].rearrange("p b n -> p (b n)"), ACT.Copy).then_inc(S["exT_done"], 1)

                    if u < 3:
                        next_rows()
                    else:
                        with act.If(g < E // 4 - 1):
                            next_rows()
                    act.wait_ge(items_used, g * 4 + (81 + u))
                    act.wait_ge(w2_in[(u + 1) % 2], g * 32 + (16 * (u // 2) + 16))
                    act.activation(w2_split[:, 0], w2raw[:, (u + 1) % 2], ACT.Copy).then_inc(S["w2_hi"], 1)
                    more = act.value_load(cnt_i[0:1, 1, ds(e, 1)], min_val=0, max_val=4)
                    with act.If(more > 0):
                        with act.Fori(0, more) as b:
                            o = act.snap(ov, min_val=0, max_val=EXTRA - 1)
                            act.wait_ge(S["ovT"], o + 1)
                            act.activation(flat(xgTo), ps[:, 6:8, :].rearrange("p b n -> p (b n)"), ACT.Copy).then_inc(S["ovT_done"], 1)
                            act.wait_ge(S["ov13"], o + 1)
                            act.activation(flat(esilo), ps[:, 3 - u % 2, 0:256], ACT.Silu).then_inc(S["ov_sil"], 1)
                            act.reg_add(ov, ov, 1)
            act.wait_ge(S["late_chain"], LA * TT)
            act.wait_ge(S["g2_pe"], 1)
            mark(act.activation(G2, ps[:, 0:2, :].rearrange("p b n -> p (b n)"), ACT.Copy), "G2_act")
            mark(act.activation(G2s, ps[0:NS, 2:4, :].rearrange("p b n -> p (b n)"), ACT.Copy), "G2_act")
            def diagonals(i):
                if i >= 2:
                    act.wait_ge(S["stat_mm"], 3 * C + i - 1)
                for k in range(4):
                    ins = act.activation(diag[:, i % 2, k, :], ident[:, :], ACT.Copy, scale=gates[:, i, k:k + 1])
                mark(ins, "diag_act")

            diagonals(0)
            diagonals(1)
            for i in range(TT):
                n = P if i < TT - 1 else LAST
                if 2 <= i + 1 < TT:
                    diagonals(i + 1)
                act.wait_ge(S["yacc"], i + 1)
                act.activation(accb[0:n, 2 + i % 2, :], accb[0:n, i % 2, :], ACT.Square,
                               accum_out=red[0:n, 1:2]).then_inc(S["fin_sq"], 1)
                act.wait_ge(S["fin_sq"], i + 1)
                act.activation(red[0:n, 2:3], red[0:n, 1:2], ACT.Sqrt, bias=eps[0:n, 0:1], scale=1.0 / D).then_inc(S["fin_rt"], 1)

        @block.vector
        def _(dve):
            counts = {}

            def link(ins, name=None, wait=True):
                key = name or "dve_step"
                counts[key] = counts.get(key, 0) + 1
                ins.then_inc(S[name] if name else dve_step, 1)
                if wait:
                    dve.wait_ge(S[name] if name else dve_step, counts[key])

            tt, ts, stt = dve.tensor_tensor, dve.tensor_scalar, dve.scalar_tensor_tensor

            def bc(ap, n):
                return ap.unsqueeze(len(ap.shape)).to_broadcast(list(ap.shape) + [n])

            dve.wait_ge(S["xrt_act"], 2)
            link(dve.reciprocal(rs[:, :], rs[:, :]))
            for c in range(C):
                link(tt(hT[:, c, :], xT[:, c, :], rs[:, :], ALU.mult), "xn_dve", wait=False)
            dve.wait_ge(S["xn_dve"], C)
            dve.wait_ge(S["vecs_act"], 1)
            dve.wait_ge(S["ada_T"], 1)
            link(tt(ada[:, 0:2, :, :].rearrange("p a c s -> p (a c) s"),
                    ps[:, 4, 0:2 * C * NSEQ].rearrange("p (a s) -> p a s", s=NSEQ), bc(vecs[:, V_ADA:V_ADA + 2 * C], NSEQ), ALU.add))
            link(stt(out=s1[:, :, :], in0=ada[:, 1], scalar=1.0, in1=bc(vecs[:, V_PRE1:V_PRE1 + C], NSEQ),
                     op0=ALU.add, op1=ALU.mult), "s1_dve")
            link(tt(smp[:, :, :], hT[:, :, NP:T], s1[:, :, 1:NSEQ], ALU.mult))
            tt(h_hi[:, :, NP:T], smp[:, :, :], ada[:, 0, :, 1:NSEQ], ALU.add).then_inc(S["h_s_dve"], 1)
            tt(hT[:, :, NP:T], smp[:, :, :], ada[:, 0, :, 1:NSEQ], ALU.add).then_inc(S["h_s_dve"], 1)
            for c in range(C + 2):
                if c < C:
                    ts(hT[:, c, 0:NP], hT[:, c, 0:NP], s1[:, c, 0:1], ada[:, 0, c, 0:1], ALU.mult, ALU.add).then_inc(S["h_dve"], 1)
                if c == 2:
                    dve.wait_ge(S["h_s_dve"], 2)
                if c >= 2:
                    dve.wait_ge(S["h_act"], c - 1)
                    tt(h_lo[:, c - 2, :], hT[:, c - 2, :], h_hi[:, c - 2, :], ALU.subtract).then_inc(S["h_lo_dve"], 1)
            dve.wait_ge(S["stB_act"], 4)
            dve.wait_ge(consts, 10)
            KA = 43
            with dve.Fori(0, C // 2) as it:
                for jj in range(2):
                    j = it * 2 + jj
                    n = [0]

                    def chain(ins, wait=True):
                        n[0] += 1
                        ins.then_inc(S["pa_chain"], 1)
                        if wait:
                            dve.wait_ge(S["pa_chain"], j * KA + n[0])

                    def at(ap3):
                        return ap3.rearrange("p a n -> p (a n)")

                    dve.wait_ge(items_used, it * 10 + (5 * jj + 2))
                    dve.wait_ge(S["sg_done"], j + 1)
                    chain(tt(glu[:, KC - 1:KC - 1 + HT], ps[:, 2, 0:HT], sg[:, 0:HT], ALU.mult), wait=False)
                    chain(tt(glu[:, KC - 1 + HT:KC - 1 + NP], ps[:, 3, 0:NP - HT], sg[:, HT:NP], ALU.mult), wait=False)
                    chain(dve.tensor_copy(glus[:, :, 0:KC - 1],
                                          at(stB[:, ds(j, 1), :]).rearrange("p (n k) -> p n k", n=NS)), wait=False)
                    chain(tt(glus[:, :, KC - 1], ps[:, 3, NP - HT:HT], sg[:, NP:T], ALU.mult))
                    chain(dve.tensor_copy(at(tail[:, ds(j, 1), 0:KC - 1]), glu[:, NP:NP + KC - 1]), wait=False)
                    dve.tensor_copy(at(tail[:, ds(j, 1), KC - 1:KC - 1 + NS]), glus[:, :, KC - 1]).then_inc(S["glu_done"], 1)
                    dve.wait_ge(S["glu_done"], j + 2)
                    acc = at(cv[:, ds(j, 1), 0:NP])
                    chain(ts(acc, glu[:, 0:NP], vecs[:, ds(j + V_WC, 1)], vecs[:, ds(j + V_BC, 1)], ALU.mult, ALU.add))
                    for k in range(1, KC):
                        chain(stt(out=acc, in0=glu[:, k:k + NP], scalar=vecs[:, ds(j + (V_WC + 8 * k), 1)], in1=acc,
                                  op0=ALU.mult, op1=ALU.add))
                    wk = vecs[:, V_WC:V_WC + 8 * KC].rearrange("p (k c) -> p c k", c=C)[:, ds(j, 1), :]
                    chain(tt(tmps[:, :, :], glus[:, :, :], wk.to_broadcast([P, NS, KC]), ALU.mult))
                    chain(dve.tensor_reduce(smp[:, 0, :], tmps[:, :, :], AX.X, ALU.add))
                    chain(ts(at(cv[:, ds(j, 1), NP:T]), smp[:, 0, :], vecs[:, ds(j + V_BC, 1)], None, ALU.add), wait=False)
                    dve.wait_ge(S["u_done"], j + 2)
                    dve.wait_ge(S["va_done"], j + 1)
                    for k in range(KS):
                        w = vecs[:, ds(j + (V_SC + 8 * k), 1)]
                        if k == 0:
                            chain(ts(vv[:, 0:NP], up[:, 0:NP], w, None, ALU.mult))
                        else:
                            chain(stt(out=vv[:, 0:NP], in0=up[:, k:k + NP], scalar=w, in1=vv[:, 0:NP], op0=ALU.mult, op1=ALU.add))
                    ws = vecs[:, V_SC:V_SC + 8 * KS].rearrange("p (k c) -> p c k", c=C)[:, ds(j, 1), :]
                    chain(tt(tmps[:, :, 0:KS], us[:, :, :], ws.to_broadcast([P, NS, KS]), ALU.mult))
                    dve.tensor_reduce(vv[:, NP:T], tmps[:, :, 0:KS], AX.X, ALU.add).then_inc(S["v_done"], 1)
                    dve.wait_ge(S["ada_T"], j + 2)
                    tt(ada4[:, ds(j, 1), :].rearrange("p a (r s) -> p (a r) s", s=NSEQ),
                       ps[:, 7, 0:4 * NSEQ].rearrange("p (r s) -> p r s", s=NSEQ),
                       bc(vecs[:, V_ADA + 2 * C:V_ADA + 6 * C].rearrange("p (j r) -> p j r", r=4)[:, ds(j, 1), :]
                          .rearrange("p j r -> p (j r)"), NSEQ), ALU.add).then_inc(S["ada2_done"], 1)
                    assert n[0] == KA, n[0]
            dve.wait_ge(S["ada2_done"], C + 1)
            tt(ada[:, 5], ada[:, 5], bc(vecs[:, V_POST2:V_POST2 + C], NSEQ), ALU.mult).then_inc(S["p2_dve"], 1)
            dve.wait_ge(S["mean_pe"], 1)
            for h, (a, b) in enumerate(half):
                link(tt(cv[:, :, a:b], cv[:, :, a:b], ps[:, 4 + h, 0:HT].unsqueeze(1).to_broadcast([P, C, HT]), ALU.subtract), "cen_dve")

            def cv_rest(c):
                dve.wait_ge(S["s_act"], c + 1)
                tt(cv_lo[:, c, :], cv[:, c, :], s_hi[:, c, :], ALU.subtract).then_inc(S["cv_lo_dve"], 1)

            dve.wait_ge(S["lrt_act"], 2)
            link(dve.reciprocal(rs[:, :], rs[:, :]))
            for j in range(C):
                link(tt(cv[:, j, :], cv[:, j, :], rs[:, :], ALU.mult), "ln_dve", wait=False)
                dve.wait_ge(items_used, 49 + j)
                dve.wait_ge(S["g_done"], j + 1)
                for h, (a, b) in enumerate(half):
                    ins = tt(mT[:, j, a:b], mT[:, j, a:b], ps[:, 2 * (j % 2) + h, 0:HT], ALU.mult)
                ins.then_inc(S["m_done"], 1)
                if j > 0:
                    cv_rest(j - 1)
            cv_rest(C - 1)
            with dve.Fori(0, 2) as it:
                for jj in range(4):
                    j = it * 4 + jj
                    dve.wait_ge(items_used, it * 8 + (58 + 2 * jj))
                    dve.wait_ge(S["g_done"], j + 9)
                    for h, (a, b) in enumerate(half):
                        stt(out=sg[:, a:b], in0=ps[:, 2 + h, 0:HT], scalar=vecs[:, ds(j + V_OB, 1)], in1=sg[:, a:b],
                            op0=ALU.add, op1=ALU.mult).then_inc(S["m_chain"], 1)
                    dve.wait_ge(S["m_chain"], j * 2 + 2)
                    mj = mT[:, ds(j, 1), :].rearrange("p a t -> p (a t)")
                    m_hi = vm_hi[:, ds(j, 1), :].rearrange("p a t -> p (a t)")
                    tt(m_hi, mj, sg[:, :], ALU.add)
                    tt(mj, mj, sg[:, :], ALU.add).then_inc(S["m_done"], 1)
                    dve.wait_ge(S["m_done"], j + 10)
                    tt(m_lo[:, ds(j, 1), :].rearrange("p a t -> p (a t)"), mj, m_hi, ALU.subtract).then_inc(S["m_lo_dve"], 1)
            link(tt(ada[:, 2], ada[:, 2], bc(vecs[:, V_POST1:V_POST1 + C], NSEQ), ALU.mult))
            link(stt(out=s1[:, :, :], in0=ada[:, 4], scalar=1.0, in1=bc(vecs[:, V_PRE2:V_PRE2 + C], NSEQ),
                     op0=ALU.add, op1=ALU.mult))
            dve.wait_ge(S["trt_act"], 2)
            link(dve.reciprocal(rs[:, :], rs[:, :]))
            for c in range(C):
                link(tt(tT[:, c, :], tT[:, c, :], rs[:, :], ALU.mult))
                link(tt(smp[:, c, :], tT[:, c, NP:T], ada[:, 2, c, 1:NSEQ], ALU.mult), wait=False)
                link(stt(out=xT[:, c, 0:NP], in0=tT[:, c, 0:NP], scalar=ada[:, 2, c, 0:1], in1=xT[:, c, 0:NP],
                         op0=ALU.mult, op1=ALU.add))
                link(tt(xT[:, c, NP:T], xT[:, c, NP:T], smp[:, c, :], ALU.add), "x1_dve", wait=False)
            dve.wait_ge(S["x1rt_act"], 2)
            link(dve.reciprocal(rs[:, :], rs[:, :]))
            for c in range(C):
                link(tt(hT[:, c, :], xT[:, c, :], rs[:, :], ALU.mult), "x1n_dve", wait=False)
            dve.wait_ge(S["x1n_dve"], C)
            link(tt(smp[:, :, :], hT[:, :, NP:T], s1[:, :, 1:NSEQ], ALU.mult))
            link(tt(hT[:, :, NP:T], smp[:, :, :], ada[:, 3, :, 1:NSEQ], ALU.add), "h2_s_dve")
            dve.wait_ge(S["x1t_T"], TT)
            link(dve.memset(score[:, TT - 1, :], 0.5), "score0_dve")
            dve.wait_ge(S["score_s_act"], 2)
            dve.wait_ge(late_in, 32)
            link(tt(sel, score, ebias[:, :].unsqueeze(1).to_broadcast([P, TT, E]), ALU.add))
            gs, g8, gi, gm, gneg, t8, wk8, wsum, eif, rowk = (s8(n) for n in range(10))
            gi_u = s8(10).bitcast(U32)
            row_i = s8(11).bitcast(I32)
            top = eq
            for i in range(TT):
                for q in range(NG):
                    link(dve.max(out=top[:, q, 8 * i:8 * i + 8], in_=sel[:, i, q * EG:(q + 1) * EG]),
                         wait=(i == TT - 1 and q == NG - 1))
            tops = top[:, :, 0:8 * TT].rearrange("p q (i r) -> p i q r", r=8)
            link(tt(gs, tops[:, :, :, 0], tops[:, :, :, 1], ALU.add))
            for i in range(TT):
                link(dve.max(out=g8[:, i, :], in_=gs[:, i, :]), wait=(i == TT - 1))
            for i in range(TT):
                link(dve.max_index(out=gi_u[:, i, :], in_max=g8[:, i, :], in_values=gs[:, i, :]), wait=(i == TT - 1))
            link(dve.tensor_copy(gi, gi_u))
            em = [(eq if i % 2 else eqm)[:, 0:TOPG, 8 * i:8 * i + NG] for i in range(TT)]
            for i in range(TT):
                link(tt(em[i], iot[:, 0:NG].unsqueeze(1).to_broadcast([P, TOPG, NG]), bc(gi[:, i, 0:TOPG], NG), ALU.is_equal),
                     wait=(i == TT - 1))
            for i in range(TT):
                link(dve.tensor_reduce(gm[:, i, :], em[i].rearrange("p j g -> p g j"), AX.X, ALU.add), wait=(i == TT - 1))
            link(ts(gneg, gm, -NEG, NEG, ALU.mult, ALU.add))
            for i in range(TT):
                sv, mv = (t[:, i, :].rearrange("p (g q) -> p g q", g=NG) for t in (sel, selm))
                link(tt(mv, sv, bc(gm[:, i, :], EG), ALU.mult), wait=(i == TT - 1))
            for i in range(TT):
                mv = selm[:, i, :].rearrange("p (g q) -> p g q", g=NG)
                link(tt(mv, mv, bc(gneg[:, i, :], EG), ALU.add), wait=(i == TT - 1))
            for i in range(TT):
                link(dve.max(out=t8[:, i, :], in_=selm[:, i, :]), wait=(i == TT - 1))
            for i in range(TT):
                link(dve.max_index(out=gi_u[:, i, :], in_max=t8[:, i, :], in_values=selm[:, i, :]), wait=False)
                link(dve.match_replace(out=repl[:, i, :], in_to_replace=t8[:, i, :], in_values=selm[:, i, :], imm_value=2 * NEG),
                     wait=(i == TT - 1))
            link(dve.tensor_copy(eif, gi_u), wait=False)
            link(ts(repl, repl, 1.5 * NEG, None, ALU.is_le))
            link(tt(mask16[:, :, :], repl, bc(valid[:, :], E), ALU.mult), "mask_dve")
            def shared_act(f):
                dve.wait_ge(S["g_done"], 17 + f)
                for h, (a, b) in enumerate(half):
                    ins = tt(scr[:, 2 + f, a:b], sg[:, a:b], ps[:, 2 + h, 0:HT], ALU.mult)
                ins.then_inc(S["sh_act"], 1)

            dve.wait_ge(S["rank_pe"], 1)
            link(dve.tensor_copy(rank, ps[:, 5, 0:RE].rearrange("p (i e) -> p i e", i=TT)))
            cnt, nov, ovb, wide, one64, ybase = (e64[:, n, :] for n in range(6))
            link(dve.tensor_copy(cnt, ps[:, 6, 0:E]))
            link(ts(nov, cnt, P + 0.5, None, ALU.is_gt))
            for m in range(2, TT):
                link(stt(out=nov, in0=cnt, scalar=m * P + 0.5, in1=nov, op0=ALU.is_gt, op1=ALU.add))
            link(ts(wide, cnt, P // 2 + 0.5, None, ALU.is_gt))
            link(dve.memset(one64, 1.0))
            link(dve.tensor_tensor_scan(out=ovb, data0=one64, data1=nov, initial=0.0, op0=ALU.mult, op1=ALU.add))
            link(tt(ovb, ovb, nov, ALU.subtract))
            link(dve.tensor_tensor_scan(out=ybase, data0=one64, data1=cnt, initial=0.0, op0=ALU.mult, op1=ALU.add))
            link(tt(ybase, ybase, cnt, ALU.subtract))
            link(dve.tensor_copy(cnt_i[0:1, 0, 0:E], wide[0:1, :]), wait=False)
            link(dve.tensor_copy(cnt_i[0:1, 2, 1:E + 1], wide[0:1, :]), wait=False)
            link(dve.tensor_copy(cnt_i[0:1, 1, 0:E], nov[0:1, :]))
            link(stt(out=ovb, in0=ovb, scalar=float(E - 1), in1=iot[:, 0:E], op0=ALU.add, op1=ALU.subtract))
            link(ts(blk, rank, P - 0.5, None, ALU.is_gt))
            for m in range(2, TT):
                link(stt(out=blk, in0=rank, scalar=m * P - 0.5, in1=blk, op0=ALU.is_gt, op1=ALU.add))
            link(tt(tmpr, blk, ovb.unsqueeze(1).to_broadcast([P, TT, E]), ALU.add))
            link(stt(out=tmpr, in0=blk, scalar=0.5, in1=tmpr, op0=ALU.is_gt, op1=ALU.mult))
            link(tt(tmpr, tmpr, iot[:, 0:E].unsqueeze(1).to_broadcast([P, TT, E]), ALU.add))
            link(stt(out=row, in0=blk, scalar=-float(P), in1=rank, op0=ALU.mult, op1=ALU.add))
            link(stt(out=row, in0=tmpr, scalar=float(P), in1=row, op0=ALU.mult, op1=ALU.add))
            shared_act(0)
            for i in range(TT):
                link(tt(eq, iot[:, 0:E].unsqueeze(1).to_broadcast([P, TOPK, E]), bc(eif[:, i, :], E), ALU.is_equal))
                link(tt(eqm, eq, row[:, i, :].unsqueeze(1).to_broadcast([P, TOPK, E]), ALU.mult))
                link(dve.tensor_reduce(rowk[:, i, :], eqm, AX.X, ALU.add))
            link(ts(gs[:, :, 0], valid[:, :], -float(P * P), float(P * P), ALU.mult, ALU.add))
            link(tt(rowk, rowk, bc(valid[:, :], TOPK), ALU.mult))
            link(tt(rowk, rowk, bc(gs[:, :, 0], TOPK), ALU.add))
            place = s8(12).bitcast(I32)
            link(dve.tensor_copy(place, rowk))
            link(ts(row_i, place, P - 1, None, ALU.bitwise_and))
            link(dve.tensor_copy(g8, row_i))
            link(ts(row_i, place, 7, None, ALU.logical_shift_right))
            link(dve.tensor_copy(gi, row_i))
            for i in range(TT):
                for k in range(TOPK):
                    n = i * TOPK + k
                    if n >= NB:
                        dve.wait_ge(S["idx_mm"], n - NB + 1)
                    if n == NB:
                        shared_act(1)
                    ts(oneA[:, n % NB, :], iot[:, :], g8[:, i, k:k + 1], None, ALU.is_equal).then_inc(S["idx_ab"], 1)
                    ts(oneB[:, n % NB, :], iot[:, 0:JOBS], gi[:, i, k:k + 1], tokp1[:, i:i + 1], ALU.is_equal, ALU.mult).then_inc(S["idx_ab"], 1)
            dve.wait_ge(S["idx_mm"], TT * TOPK)
            tab, tb2 = eq.rearrange("p k e -> p (k e)")[:, 0:JOBS], eq.rearrange("p k e -> p (k e)")[:, 128:128 + JOBS]
            link(ts(tab, ps[:, 7, 0:JOBS], -1.0, None, ALU.add))
            link(dve.tensor_copy(idxT[:, :], tab))
            link(ts(tab, tab, -0.5, 1e6, ALU.is_lt, ALU.mult))
            link(dve.tensor_copy(beyond[:, :], tab))
            link(ts(tb2[:, 0:E], ybase, slotid[:, 0:1], None, ALU.add))
            link(dve.tensor_copy(firsty[:, :], tb2[:, 0:E]))
            link(tt(tb2[:, 0:E], tab[:, 0:E], tb2[:, 0:E], ALU.add))
            link(dve.tensor_copy(rowT[:, 1:], tb2[:, 0:E]), "table_dve")
            link(tt(tmpr, rank, ybase.unsqueeze(1).to_broadcast([P, TT, E]), ALU.add))
            dve.wait_ge(S["sh_done"], TT)
            dve.memset(ps[:, 2:4, :], 0.0).then_inc(S["sh_act"], 1)
            ov, tile_no = dve.alloc_register("ov_dve"), dve.alloc_register("tile_no")
            dve.reg_mov(ov, 0)
            dve.reg_mov(tile_no, 0)

            def token_tile(i, u):
                n = [(0, 3, 7, 9)[u]]
                eight = wsum[:, 1, :]

                def chain(ins, wait=True):
                    n[0] += 1
                    ins.then_inc(S["late_chain"], 1)
                    if wait:
                        dve.wait_ge(S["late_chain"], i * LA + n[0])

                def at(ap):
                    return ap[:, ds(i, 1), :].rearrange("p a n -> p (a n)")

                def of_all(ap):
                    return at(ap).unsqueeze(1).to_broadcast([P, TOPK, E])

                if u > 0:
                    dve.wait_ge(S["late_chain"], i * LA + n[0])
                if u == 0:
                    chain(tt(eq, iot[:, 0:E].unsqueeze(1).to_broadcast([P, TOPK, E]), bc(at(eif), E), ALU.is_equal))
                    chain(tt(eqm, eq, of_all(score), ALU.mult))
                    chain(dve.tensor_reduce(eight, eqm, AX.X, ALU.add), wait=False)
                elif u == 1:
                    chain(dve.tensor_reduce(wsum[:, 0, 0:1], eight, AX.X, ALU.add))
                    chain(dve.reciprocal(wsum[:, 0, 1:2], wsum[:, 0, 0:1]))
                    chain(tt(eight, eight, wsum[:, 0, 1:2].to_broadcast([P, TOPK]), ALU.mult))
                    chain(ts(at(gates), eight, ROUTED_SCALE, None, ALU.mult), wait=False)
                elif u == 2:
                    chain(tt(eqm, eq, of_all(tmpr), ALU.mult))
                    chain(dve.tensor_reduce(eight, eqm, AX.X, ALU.add), wait=False)
                else:
                    chain(dve.tensor_copy(at(yidx), eight), wait=False)

            def split_act(b, sil, bank, full_there, full, done):
                hi, lo, whole = flat(act_split[:, b, 0]), flat(act_split[:, b, 1]), eacto if full == "ov_full" else eact[:, b]
                tt(hi, flat(sil), ps[:, bank, 256:512], ALU.mult)
                tt(whole, flat(sil), ps[:, bank, 256:512], ALU.mult).then_inc(S[full], 1)
                full_there()
                tt(lo, whole, hi, ALU.subtract).then_inc(S[done], 1)

            def y_out_of(e, b):
                dve.wait_ge(items_used, e + 82)
                dve.tensor_copy(yb[:, b, :], ps[:, 4:6, :].rearrange("p b n -> p (b n)")).then_inc(S["ex_yd"], 1)

            with dve.Fori(0, E // 4) as g:
                for u in range(4):
                    e = g * 4 + u
                    with dve.If(g < TT):
                        token_tile(dve.snap(tile_no, min_val=0, max_val=TT - 1), u)
                        if u == 3:
                            dve.reg_add(tile_no, tile_no, 1)
                    dve.wait_ge(S["ex_sil"], e + 1)
                    split_act(u % 2, esil[:, u % 2], 2 + u % 2, lambda: dve.wait_ge(S["ex_full"], e + 1), "ex_full", "ex_act")
                    if u == 0:
                        with dve.If(g > 0):
                            dve.wait_ge(y_out[1], g * 16)
                            y_out_of(e - 1, 1)
                    else:
                        if u < 3:
                            with dve.If(g > 0):
                                dve.wait_ge(y_out[u + 1], g * 16)
                                y_out_of(e - 1, u - 1)
                            with dve.If(g < 1):
                                y_out_of(e - 1, u - 1)
                        else:
                            dve.wait_ge(y_out[0], g * 16 + 16)
                            y_out_of(e - 1, 0)
                    dve.wait_ge(S["w2_hi"], e + 1)
                    tt(w2_split[:, 1], w2raw[:, (u + 1) % 2], w2_split[:, 0], ALU.subtract).then_inc(S["w2_lo"], 1)
                    more = dve.value_load(cnt_i[0:1, 1, ds(e, 1)], min_val=0, max_val=4)
                    with dve.If(more > 0):
                        with dve.Fori(0, more) as b:
                            o = dve.snap(ov, min_val=0, max_val=EXTRA - 1)
                            dve.wait_ge(S["ov_sil"], o + 1)
                            split_act((u + 1) % 2, esilo, 3 - u % 2, lambda: dve.wait_ge(S["ov_full"], o + 1), "ov_full", "ov_act")
                            yo = ps[:, 6:8, :].rearrange("p b n -> p (b n)")
                            with dve.If(o > 0):
                                dve.wait_ge(S["ov_y"], o + 1)
                                dve.wait_ge(S["ov_scat"], dve.snap(ov, min_val=1, max_val=EXTRA - 1) * 16)
                                dve.tensor_copy(ybo, yo).then_inc(S["ov_yd"], 1)
                            with dve.If(o < 1):
                                dve.wait_ge(S["ov_y"], o + 1)
                                dve.tensor_copy(ybo, yo).then_inc(S["ov_yd"], 1)
                            dve.reg_add(ov, ov, 1)
            dve.wait_ge(y_out[1], 16 * (E // 4))
            y_out_of(E - 1, 1)
            for i in range(TT):
                n = P if i < TT - 1 else LAST
                acc = accb[0:n, i % 2, :]
                if i >= 2:
                    dve.wait_ge(rows_out[i % 2], 16 * (i // 2 + 3 - i % 2))
                for k in range(4, TOPK):
                    b = (i % 2) * 8 + k
                    dve.wait_ge(yk_in[b], 16 * (i // 2 + 1))
                    link(stt(out=acc, in0=yk[0:n, b, :], scalar=gates[0:n, i, k:k + 1],
                             in1=shared[0:n, i, :] if k == 4 else acc, op0=ALU.mult, op1=ALU.add))
                dve.wait_ge(S["stat_mm"], 3 * C + i + 1)
                f = 4 + 2 * (i % 2)
                tt(acc, acc, ps[0:n, f:f + 2, :].rearrange("p b n -> p (b n)"), ALU.add).then_inc(S["yacc"], 1)
                if i == 0:
                    dve.wait_ge(S["G2_act"], 2)
                dve.wait_ge(S["fin_rt"], i + 1)
                link(dve.reciprocal(red[0:n, 2:3], red[0:n, 2:3]))
                link(stt(out=acc, in0=acc, scalar=red[0:n, 2:3], in1=(G2 if i < TT - 1 else G2s)[0:n, :], op0=ALU.mult, op1=ALU.mult))
                tt(accb[0:n, 2 + i % 2, :], acc, x1tok[0:n, i, :], ALU.add).then_inc(S["fin_out"], 1)

        @block.tensor
        def _(pe):
            def mark(ins, name):
                ins.then_inc(S[name], 1)

            mm, tr = pe.matmul, pe.transpose
            pe.wait_ge(consts, 10)
            pe.wait_ge(x_in, 16)
            for c in range(C):
                if c >= 4:
                    pe.wait_ge(S["xT_act"], c - 4 + 1)
                for i in range(TT - 1):
                    ins = tr(ps[:, c % 4, i * P:(i + 1) * P], x_tok[:, i, c * P:(c + 1) * P], ident[:, :])
                mark(ins, "xT_pe")
            pe.wait_ge(crow_in, 48)
            for c in range(C):
                ins = tr(ps[:, 5, c * NS:(c + 1) * NS], x_stok[:, c * P:(c + 1) * P], ident[0:NS, 0:NS])
            mark(ins, "xs_pe")
            pe.wait_ge(S["csilu_act"], 1)
            for c in range(C):
                ins = tr(ps[:, 4, c * NSEQ:(c + 1) * NSEQ], c_tok[:, c * P:(c + 1) * P], ident[0:NSEQ, 0:NSEQ])
            mark(ins, "cT_pe")

            def stat(bank, src, c):
                for h, (a, b) in enumerate(half):
                    ins = mm(ps[:, bank + h, 0:HT], avg[:, :], src[:, a:b], start=(c == 0), stop=(c == C - 1))
                return ins

            for c in range(C):
                pe.wait_ge(S["xsq_act"], c + 1)
                ins = stat(6, hT[:, c, :], c)
            mark(ins, "xstat_pe")

            def conditioning(w, bank):
                for k in range(C):
                    ins = mm(ps[0:NSEQ, bank, :], scT[:, k, :], w[:, k, :], start=(k == 0), stop=(k == C - 1))
                ins.then_inc(S["ada_row"], 1)

            pe.wait_ge(S["cT_act"], 1)
            pe.wait_ge(S["xT_act"], C)
            for q in range(4):
                pe.wait_ge(w_big[q], 16)
                conditioning(ada_w[q], q)
            pe.wait_ge(vrow_in, 16 * 13)
            pe.wait_ge(S["xs_act"], 1)
            tr(ps[:, 5, 0:128], vrow, ident[:, :])
            for a in range(2):
                tr(ps[:, 5, 128 + 124 * a:128 + 124 * (a + 1)], wcrow[:, a, :], ident[0:124, 0:124])
            tr(ps[:, 5, 376:504], sarow, ident[:, :])
            mark(tr(ps[:, 5, 504:512], p2row, ident[0:C, 0:C]), "vecs_pe")
            for q in range(4):
                pe.wait_ge(S["arow_done"], q + 1)
                for n in range(4 * q, 4 * q + 4):
                    ins = tr(ps[:, 4, n * NSEQ:(n + 1) * NSEQ], arow[:, n * P:(n + 1) * P], ident[0:NSEQ, 0:NSEQ])
            mark(ins, "ada_T")
            pe.wait_ge(st_in, 16)
            pe.wait_ge(S["s1_dve"], 1)
            pe.wait_ge(S["xrt_act"], 2)
            W2 = NS * (KC - 1)
            for q in range(4):
                for c in range(2 * q, 2 * q + 2):
                    for a in range(2):
                        at = (c % 2) * W2 + a * 120
                        ins = tr(ps[:, 4 + q, at:at + 120], sbrow[:, a, c * P:(c + 1) * P], ident[0:120, 0:120])
                mark(ins, "stB_pe")

            def product(bank, w, src):
                for h, (a, b) in enumerate(half):
                    for k in range(C):
                        ins = mm(ps[:, bank + h, 0:HT], w[:, k, :], src[:, k, a:b], start=(k == 0), stop=(k == C - 1))
                return ins

            def split_product(n, b, bank, hi, lo, as_they_come=False):
                pe.wait_ge(S["w_lo"], n + 6)
                for h, (p, q) in enumerate(half):
                    for k in range(C):
                        if as_they_come and h == 0:
                            pe.wait_ge(S["h_lo_dve"], k + 1)
                        mm(ps[:, bank + h, 0:HT], wsplit[:, b, 0, k, :], hi[:, k, p:q], start=(k == 0), stop=False)
                        mm(ps[:, bank + h, 0:HT], wsplit[:, b, 0, k, :], lo[:, k, p:q], start=False, stop=False)
                        ins = mm(ps[:, bank + h, 0:HT], wsplit[:, b, 1, k, :], hi[:, k, p:q], start=False, stop=(k == C - 1))
                ins.then_inc(items_used, 1)

            with pe.Fori(0, C // 2) as it:
                for jj in range(2):
                    j = it * 2 + jj
                    for i, bank in enumerate((0, 2, 4, 0, 2)):
                        f = 5 * jj + i
                        if i == 0:
                            pe.wait_ge(S["acs_done"], j + 1)
                        elif i == 1:
                            pe.wait_ge(S["abs_done"], j + 1)
                        elif i == 2:
                            pe.wait_ge(S["ain_done"], j + 1)
                            pe.wait_ge(S["stB_act"], 4)
                        elif i == 3:
                            pe.wait_ge(S["sg_done"], j + 1)
                        else:
                            pe.wait_ge(w_ada2, it * 32 + (16 * jj + 16))
                            pe.wait_ge(S["arow_done"], j + 4)
                            conditioning(ada_w[2], 6)
                            pe.wait_ge(S["glu_done"], j + 2)
                        split_product(it * 10 + f, f % 2, bank, h_hi, h_lo, f == 0)
                    pe.wait_ge(S["arow_done"], j + 5)
                    pe.wait_ge(S["ada2_done"], j + 1)
                    for n in range(4):
                        ins = mm(ps[:, 7, n * NSEQ:(n + 1) * NSEQ], arow[:, n * P:(n + 1) * P], ident[0:NSEQ, 0:NSEQ], start=True, stop=True)
                    ins.then_inc(S["ada_T"], 1)
            def gates_a(js):
                for j in js:
                    if j >= 2:
                        pe.wait_ge(S["g_done"], j - 1)
                    split_product(40 + j, j % 2, 2 * (j % 2), h_hi, h_lo)

            pe.wait_ge(S["acs_done"], C + 1)
            pe.wait_ge(S["abs_done"], C + 1)
            gates_a(range(3))
            pe.wait_ge(S["va_done"], C + 1)
            pe.wait_ge(S["p2_dve"], 1)
            for c in range(C):
                ins = tr(ps[0:48, 6 + c // 4, (c % 4) * P:(c % 4 + 1) * P], tail[:, c, :], ident[:, :])
            mark(ins, "tails_pe")
            for c in range(C):
                ins = tr(ps[0:NSEQ, 4 + c // 4, (c % 4) * P:(c % 4 + 1) * P], ada[:, 5, c, :], ident[:, :])
            mark(ins, "g2rows_pe")
            pe.wait_ge(S["growc_act"], 1)
            for c in range(C):
                ins = stat(4, cv[:, c, :], c)
            mark(ins, "mean_pe")
            gates_a(range(3, 5))
            for c in range(C):
                pe.wait_ge(S["sqd"], c + 1)
                stat(6, scr[:, c % 4, :], c).then_inc(S["stat_mm"], 1)
            gates_a(range(5, C))
            pe.wait_ge(S["va_lo_pool"], C)
            for j in range(C):
                if j < 2:
                    pe.wait_ge(S["g_done"], 7 + j)
                else:
                    pe.wait_ge(S["m_done"], j)
                split_product(48 + j, j % 2, 2 * (j % 2), vm_hi, va_lo)
            pe.wait_ge(S["m_done"], 9)
            pe.wait_ge(S["cv_lo_dve"], C)
            with pe.Fori(0, 2) as it:
                for jj in range(4):
                    n = it * 8 + (56 + 2 * jj)
                    pe.wait_ge(S["g_done"], it * 4 + (8 + jj))
                    split_product(n, 0, 0, h_hi, h_lo)
                    pe.wait_ge(S["m_done"], it * 4 + (9 + jj))
                    split_product(n + 1, 1, 2, s_hi, cv_lo)
            pe.wait_ge(S["m_lo_dve"], C)
            pe.wait_ge(S["m_done"], 17)
            for j in range(C + 1):
                if j < C:
                    if j >= 2:
                        pe.wait_ge(S["t_cp"], j)
                    split_product(72 + j, j % 2, 2 * (j % 2), vm_hi, m_lo)
                if j > 0:
                    pe.wait_ge(S["sqd"], 8 + j)
                    stat(6, scr[:, (j - 1) % 4, :], j - 1).then_inc(S["stat_mm"], 1)
            for j in range(C):
                pe.wait_ge(S["sqd"], 17 + j)
                stat(4, scr[:, j % 4, :], j).then_inc(S["stat_mm"], 1)
            for i in range(TT):
                n = P if i < TT - 1 else LAST
                b = (0, 2, 6, 0, 2)[i]
                if i >= 3:
                    pe.wait_ge(S["x1t_done"], i - 2)
                elif i == 2:
                    pe.wait_ge(S["trt_act"], 2)
                for c in range(C):
                    ins = tr(ps[0:n, b + c // 4, (c % 4) * P:(c % 4 + 1) * P], xT[:, c, i * P:i * P + n], ident[:, :])
                ins.then_inc(S["x1t_T"], 1)
            pe.wait_ge(S["h2_act"], 8)
            pe.wait_ge(S["h2_s_dve"], 1)
            pe.wait_ge(late_in, 32)
            for i in range(TT):
                n = P if i < TT - 1 else LAST
                for k in range(C):
                    ins = mm(ps[0:n, 4, i * E:(i + 1) * E], hT[:, k, i * P:i * P + n], wr[:, k, :], start=(k == 0), stop=(k == C - 1))
            mark(ins, "logits_pe")
            for i in range(TT):
                n = P if i < TT - 1 else LAST
                if i >= 1:
                    pe.wait_ge(S["hx_done"], i)
                else:
                    pe.wait_ge(S["x1t_done"], TT)
                for c in range(C):
                    ins = tr(ps[0:n, 2 + c // 4, (c % 4) * P:(c % 4 + 1) * P], hT[:, c, i * P:i * P + n], ident[:, :])
                ins.then_inc(S["hx_T"], 1)
            def shared_up(f, m):
                w = w13[:, 0, 2048 * m:2048 * (m + 1)].rearrange("p (k n) -> p k n", k=C)[:, :, f * P:(f + 1) * P]
                ins = product(2 * m, w, hT)
                if m == 1:
                    ins.then_inc(S["sh_mm"], 1)

            pe.wait_ge(S["mask_dve"], 1)
            for i in range(TT):
                for q in range(i):
                    mm(ps[:, 5, i * E:(i + 1) * E], ones16[:, :], mask16[:, q, :], start=(q == 0), stop=False)
                mm(ps[:, 5, i * E:(i + 1) * E], upper[:, :], mask16[:, i, :], start=(i == 0), stop=True)
            for i in range(TT):
                ins = mm(ps[:, 6, 0:E], ones16[:, :], mask16[:, i, :], start=(i == 0), stop=(i == TT - 1))
            mark(ins, "rank_pe")
            pe.wait_ge(w_sh, 48)
            pe.wait_ge(S["hx_done"], TT)
            for f in range(FT):
                if f == 1:
                    pe.wait_ge(S["sh_act"], 1)
                for m in range(2):
                    shared_up(f, m)
            w2s = w2raw[:, 0]
            for n in range(TT * TOPK):
                pe.wait_ge(S["idx_ab"], 2 * n + 2)
                mm(ps[:, 7, 0:JOBS], oneA[:, n % NB, :], oneB[:, n % NB, :], start=(n == 0), stop=(n == TT * TOPK - 1)).then_inc(S["idx_mm"], 1)
                if n % TOPK == TOPK - 1:
                    i = n // TOPK
                    rows = P if i < TT - 1 else LAST
                    if i == 0:
                        pe.wait_ge(S["sh_act"], 2)
                    if i >= 2:
                        pe.wait_ge(S["sh_done"], i - 1)
                    for h in range(2):
                        for k in range(FT):
                            ins = mm(ps[0:rows, 2 * (i % 2) + h, :], scr[:, 2 + k, i * P:i * P + rows],
                                     w2s[:, k, h * 512:(h + 1) * 512], start=(k == 0), stop=(k == FT - 1))
                    ins.then_inc(S["sh_o"] if i < TT - 1 else items_used, 1)

            def rows_T(src, bank=0):
                v = src.rearrange("s (m c) -> s c m", c=C)
                for c in range(C):
                    ins = tr(ps[:, bank + c // 4, (c % 4) * P:(c % 4 + 1) * P], v[:, c, :], ident[:, :])
                return ins

            def up_products(slot, bank, src, n):
                for m in range(2):
                    w = w13[:, slot, 2048 * m:2048 * (m + 1)].rearrange("p (k n) -> p k n", k=C)
                    for f in range(FT):
                        q = 2 * m + f
                        for k in range(C):
                            ins = mm(ps[:, bank, q * P:q * P + n], w[:, k, f * P:(f + 1) * P], src[:, k, 0:n],
                                     start=(k == 0), stop=(k == C - 1))
                return ins

            def down_products(b, bank=4):
                hi, lo = act_split[:, b, 0], act_split[:, b, 1]
                for h in range(2):
                    cols = slice(h * 512, (h + 1) * 512)
                    for k in range(FT):
                        mm(ps[:, bank + h, :], hi[:, k, :], w2_split[:, 0, k, cols], start=(k == 0), stop=False)
                        mm(ps[:, bank + h, :], hi[:, k, :], w2_split[:, 1, k, cols], start=False, stop=False)
                        ins = mm(ps[:, bank + h, :], lo[:, k, :], w2_split[:, 0, k, cols], start=False, stop=(k == FT - 1))
                return ins

            pe.wait_ge(S["sh_act"], 3)
            pe.wait_ge(S["sh_done"], TT)
            pe.wait_ge(S["table_dve"], 1)
            pe.wait_ge(xg_in[0], 16)
            rows_T(xg[:, 0, :]).then_inc(S["exT"], 1)
            ov = pe.alloc_register("ov_pe")
            pe.reg_mov(ov, 0)
            with pe.Fori(0, E // 4) as g:
                for u in range(4):
                    e = g * 4 + u
                    slot = (u + 1) % 4
                    pe.wait_ge(w_big[slot], g * 32 + 48)
                    pe.wait_ge(S["exT_done"], e + 1)
                    wide = pe.value_load(cnt_i[0:1, 0, ds(e, 1)], min_val=0, max_val=1)
                    with pe.If(wide > 0):
                        up_products(slot, 2 + u % 2, xgT, P).then_inc(S["ex13"], 1)
                    with pe.If(wide < 1):
                        up_products(slot, 2 + u % 2, xgT, P // 2).then_inc(S["ex13"], 1)

                    def next_rows():
                        pe.wait_ge(xg_in[(u + 1) % 2], g * 32 + 16 * ((u + 1) // 2 + 1))
                        rows_T(xg[:, (u + 1) % 2, :]).then_inc(S["exT"], 1)

                    def last_down():
                        pe.wait_ge(S["ex_act"], e)
                        pe.wait_ge(S["ex_yd"], e)
                        pe.wait_ge(S["w2_lo"], e + 2)
                        down_products((u + 1) % 2).then_inc(items_used, 1)

                    if u < 3:
                        next_rows()
                    else:
                        with pe.If(g < E // 4 - 1):
                            next_rows()
                    if u > 0:
                        last_down()
                    else:
                        with pe.If(g > 0):
                            last_down()
                    more = pe.value_load(cnt_i[0:1, 1, ds(e, 1)], min_val=0, max_val=4)
                    with pe.If(more > 0):
                        with pe.Fori(0, more) as b:
                            o = pe.snap(ov, min_val=0, max_val=EXTRA - 1)
                            pe.wait_ge(S["ovx"], o * 16 + 16)
                            pe.wait_ge(S["ov_yd"], o + 1)
                            rows_T(xgo, 6).then_inc(S["ovT"], 1)
                            pe.wait_ge(S["ovT_done"], o + 1)
                            up_products(slot, 3 - u % 2, xgTo, P).then_inc(S["ov13"], 1)
                            pe.wait_ge(S["ov_act"], o + 1)
                            pe.wait_ge(S["w2_lo"], e + 3)
                            down_products((u + 1) % 2, 6).then_inc(S["ov_y"], 1)
                            pe.reg_add(ov, ov, 1)
            pe.wait_ge(S["ex_act"], E)
            pe.wait_ge(S["ex_yd"], E)
            pe.wait_ge(S["w2_lo"], E + 2)
            down_products(1).then_inc(items_used, 1)
            for h in range(2):
                mm(ps[:, h, :], firstrow[:, :], grow[:, h * 512:(h + 1) * 512], start=True, stop=True)
            for h in range(2):
                ins = mm(ps[0:NS, 2 + h, :], ident[0:NSEQ, 1:NSEQ], grow[:, h * 512:(h + 1) * 512], start=True, stop=True)
            mark(ins, "g2_pe")
            for i in range(TT):
                n = P if i < TT - 1 else LAST
                pe.wait_ge(S["diag_act"], i + 1)
                if i >= 2:
                    pe.wait_ge(S["yacc"], i - 1)
                for k in range(4):
                    b = (i % 2) * 8 + k
                    pe.wait_ge(yk_in[b], 16 * (i // 2 + 1))
                    for h in range(2):
                        ins = mm(ps[0:n, 4 + 2 * (i % 2) + h, :], diag[0:n, i % 2, k, 0:n], yk[0:n, b, h * 512:(h + 1) * 512],
                                 start=(k == 0), stop=(k == 3))
                mark(ins, "stat_mm")


_INS = ['x_prompt', 'x_sample', 'state_sconv', 'state_cconv', 'c_prompt', 'c_sample', 'w_ada', 'b_ada',
        'g_pre1', 'g_post1', 'g_pre2', 'g_post2', 'w_in', 'w_sconv', 'w_out_a', 'w_cconv', 'b_cconv', 'ln_g', 'ln_b',
        'w_out_b', 'b_out_b', 'w_o', 'w_router', 'e_bias', 'w1', 'w3', 'w2', 'ws1', 'ws3', 'ws2']


def kernel(**inputs):
    import numpy as _np
    import concourse.bacc as _bacc
    from concourse import mybir as _mybir
    from concourse.bass_utils import run_bass_kernel_spmd as _run

    nc = _bacc.Bacc("TRN2", target_bir_lowering=False, num_devices=1)
    arrays, args = {}, []
    for name in _INS:
        a = _np.ascontiguousarray(inputs[name])
        arrays[f"in_{name}_dram"] = a
        args.append(nc.dram_tensor(f"in_{name}_dram", a.shape, _mybir.dt.from_np(a.dtype), kind="ExternalInput").ap())
    x_p, x_s, st_a, st_b = (inputs[n].shape for n in ("x_prompt", "x_sample", "state_sconv", "state_cconv"))
    shapes = [x_p, x_s, (st_a[0], x_p[0], st_a[2], st_a[3]), st_a, (st_b[0], x_p[0], st_b[2], st_b[3]), st_b]
    for i, shape in enumerate(shapes):
        args.append(nc.dram_tensor(f"out_{i}_dram", shape, _mybir.dt.float32, kind="ExternalOutput").ap())
    build_program(nc, *args)
    r = _run(nc, [arrays], core_ids=[0])
    return tuple(r.results[0][f"out_{i}_dram"] for i in range(len(shapes)))
```
